# Optimizing a Trainium2 kernel written in Bass

```python
import jax, jax.numpy as jnp
from jax import lax
import numpy as np

D_MODEL = 1024
BATCH = 1
SEQ = 512
DEPTH = 2
DEC_BATCH = 1
DEC_SEQ = 32
PAST_LEN = 256

CHUNK = 64
N_MIXERS = 2
N_A_LAYERS = (DEPTH + 1) // 2
N_B_LAYERS = DEPTH // 2
A_HEADS = 16
A_KV_HEADS = 4
A_GROUP = A_HEADS // A_KV_HEADS
A_HEAD_DIM = 64
WINDOW = 128
WIN_CHUNKS = WINDOW // CHUNK
B_HEADS = 8
B_HEAD_DIM = 64
B_Q_BLOCK = 128
N_GROUPS = 4
EXPERTS_PER_GROUP = 8
TOP_K_IN_GROUP = 2
D_EXPERT = 256
NORM_EPS = 1e-6
SUBLN_EPS = 1e-5

kernel_name = "hybrid_swa_sink_diffattn_hmoe_stream_step"

def rms_norm(x, g, eps=NORM_EPS):
    xf = x.astype(jnp.float32)
    y = xf * lax.rsqrt(jnp.mean(xf * xf, axis=-1, keepdims=True) + eps)
    return (y * g.astype(jnp.float32)).astype(x.dtype)

def alibi_slopes(n):
    return jnp.asarray(2.0 ** (-8.0 * np.arange(1, n + 1) / n), dtype=jnp.float32)

def _a_project(h, w_qkv, b_qkv):
    b_, t = h.shape[:2]
    qkv = h @ w_qkv + b_qkv
    nq = A_HEADS * A_HEAD_DIM
    nk = A_KV_HEADS * A_HEAD_DIM
    q = qkv[..., :nq].reshape(b_, t, A_KV_HEADS, A_GROUP, A_HEAD_DIM)
    k = qkv[..., nq:nq + nk].reshape(b_, t, A_KV_HEADS, A_HEAD_DIM)
    v = qkv[..., nq + nk:].reshape(b_, t, A_KV_HEADS, A_HEAD_DIM)
    return q, k, v

def sink_attend(q, k, v, bias, valid, sinks):
    s = jnp.einsum('...qhgd,...shd->...hgqs', q, k).astype(jnp.float32) * (A_HEAD_DIM ** -0.5) + bias
    if valid is not None:
        s = jnp.where(valid, s, -jnp.inf)
    sk = sinks.astype(jnp.float32)[:, :, None, None]
    m = jnp.maximum(jnp.max(s, axis=-1, keepdims=True), sk)
    e = jnp.exp(s - m)
    p = e / (jnp.sum(e, axis=-1, keepdims=True) + jnp.exp(sk - m))
    return jnp.einsum('...hgqs,...shd->...qhgd', p.astype(v.dtype), v)

def _a_bias(qpos, kpos):
    dist = jnp.abs(qpos[:, None] - kpos[None, :]).astype(jnp.float32)
    slopes = alibi_slopes(A_HEADS).reshape(A_KV_HEADS, A_GROUP)
    return -slopes[:, :, None, None] * dist

def mixer_a_prompt(h, w_qkv, b_qkv, sinks, w_o):
    b_, t, _ = h.shape
    nc = t // CHUNK
    band = CHUNK * (WIN_CHUNKS + 1)
    q, k, v = _a_project(h, w_qkv, b_qkv)
    qc = q.reshape(b_, nc, CHUNK, A_KV_HEADS, A_GROUP, A_HEAD_DIM)
    pad = ((0, 0), (WIN_CHUNKS, 0), (0, 0), (0, 0), (0, 0))
    kp = jnp.pad(k.reshape(b_, nc, CHUNK, A_KV_HEADS, A_HEAD_DIM), pad)
    vp = jnp.pad(v.reshape(b_, nc, CHUNK, A_KV_HEADS, A_HEAD_DIM), pad)
    kb = jnp.concatenate([kp[:, j:j + nc] for j in range(WIN_CHUNKS + 1)], axis=2)
    vb = jnp.concatenate([vp[:, j:j + nc] for j in range(WIN_CHUNKS + 1)], axis=2)
    qi = jnp.arange(CHUNK)
    kj = jnp.arange(band) - WIN_CHUNKS * CHUNK
    bias = _a_bias(qi, kj)
    kpos = jnp.arange(nc)[:, None] * CHUNK + kj[None, :]
    valid = (kpos >= 0)[None, :, None, None, None, :]
    o = sink_attend(qc, kb, vb, bias, valid, sinks.reshape(A_KV_HEADS, A_GROUP))
    y = o.reshape(b_, t, A_HEADS * A_HEAD_DIM) @ w_o
    keep = min(WINDOW, t)
    return y, k[:, t - keep:], v[:, t - keep:]

def mixer_a_sample(h, ck, cv, w_qkv, b_qkv, sinks, w_o):
    b_, t, _ = h.shape
    l = ck.shape[1]
    q, k, v = _a_project(h, w_qkv, b_qkv)
    kk = jnp.concatenate([ck.astype(k.dtype), k], axis=1)
    vv = jnp.concatenate([cv.astype(v.dtype), v], axis=1)
    kpos = jnp.concatenate([jnp.arange(l) - l, jnp.arange(t)])
    bias = _a_bias(jnp.arange(t), kpos)
    o = sink_attend(q, kk, vv, bias, None, sinks.reshape(A_KV_HEADS, A_GROUP))
    y = o.reshape(b_, t, A_HEADS * A_HEAD_DIM) @ w_o
    return y, kk[:, t:], vv[:, t:]

def _b_project(h, w_qkv):
    b_, t = h.shape[:2]
    qkv = h @ w_qkv
    w = B_HEADS * 2 * B_HEAD_DIM
    q = qkv[..., :w].reshape(b_, t, B_HEADS, 2, B_HEAD_DIM)
    k = qkv[..., w:2 * w].reshape(b_, t, B_HEADS, 2, B_HEAD_DIM)
    v = qkv[..., 2 * w:].reshape(b_, t, B_HEADS, 2 * B_HEAD_DIM)
    return q, k, v

def _b_lambda(lam_p, lam_init):
    lp = lam_p.astype(jnp.float32)
    return jnp.exp(jnp.sum(lp[0] * lp[1])) - jnp.exp(jnp.sum(lp[2] * lp[3])) + lam_init

def diff_attend(q, k, v, bias, valid, lam):
    s = jnp.einsum('bqhcd,bshcd->bhcqs', q, k).astype(jnp.float32) * (B_HEAD_DIM ** -0.5) + bias[:, None]
    if valid is not None:
        s = jnp.where(valid, s, -jnp.inf)
    p = jax.nn.softmax(s, axis=-1)
    a = p[:, :, 0] - lam * p[:, :, 1]
    return jnp.einsum('bhqs,bshe->bqhe', a.astype(v.dtype), v)

def _b_out(o, subln, lam_init, w_o):
    b_, t = o.shape[:2]
    o = rms_norm(o, subln, SUBLN_EPS) * (1.0 - lam_init)
    return o.reshape(b_, t, B_HEADS * 2 * B_HEAD_DIM) @ w_o

def mixer_b_prompt(h, w_qkv, lam_p, subln, w_o, lam_init):
    b_, t, _ = h.shape
    q, k, v = _b_project(h, w_qkv)
    lam = _b_lambda(lam_p, lam_init)
    slopes = alibi_slopes(B_HEADS)
    nb = t // B_Q_BLOCK
    qb = jnp.moveaxis(q.reshape(b_, nb, B_Q_BLOCK, B_HEADS, 2, B_HEAD_DIM), 1, 0)
    kpos = jnp.arange(t)

    def block(args):
        qblk, bi = args
        qpos = bi * B_Q_BLOCK + jnp.arange(B_Q_BLOCK)
        dist = jnp.abs(qpos[:, None] - kpos[None, :]).astype(jnp.float32)
        bias = -slopes[:, None, None] * dist
        valid = (kpos[None, :] // CHUNK) <= (qpos[:, None] // CHUNK)
        return diff_attend(qblk, k, v, bias, valid, lam)

    o = lax.map(block, (qb, jnp.arange(nb)))
    o = jnp.moveaxis(o, 0, 1).reshape(b_, t, B_HEADS, 2 * B_HEAD_DIM)
    y = _b_out(o, subln, lam_init, w_o)
    return y, k.reshape(b_, t, B_HEADS, 2 * B_HEAD_DIM), v

def mixer_b_sample(h, ck, cv, w_qkv, lam_p, subln, w_o, lam_init):
    b_, t, _ = h.shape
    p = ck.shape[1]
    q, k, v = _b_project(h, w_qkv)
    lam = _b_lambda(lam_p, lam_init)
    kk = jnp.concatenate([ck.astype(k.dtype).reshape(b_, p, B_HEADS, 2, B_HEAD_DIM), k], axis=1)
    vv = jnp.concatenate([cv.astype(v.dtype), v], axis=1)
    kpos = jnp.arange(p + t)
    qpos = p + jnp.arange(t)
    dist = jnp.abs(qpos[:, None] - kpos[None, :]).astype(jnp.float32)
    bias = -alibi_slopes(B_HEADS)[:, None, None] * dist
    o = diff_attend(q, kk, vv, bias, None, lam)
    y = _b_out(o, subln, lam_init, w_o)
    return y, k.reshape(b_, t, B_HEADS, 2 * B_HEAD_DIM), v

def hier_moe(h, w_rg, b_rg, w_re, b_re, w_gate, w_up, w_down):
    b_, t, d = h.shape
    x = h.reshape(-1, d)
    pg = jax.nn.softmax((x @ w_rg).astype(jnp.float32) + b_rg.astype(jnp.float32), axis=-1)
    g_idx = jnp.argmax(pg, axis=-1)
    g_prob = jnp.max(pg, axis=-1)
    g_hot = jax.nn.one_hot(g_idx, N_GROUPS, dtype=jnp.float32)
    el = ((x @ w_re).astype(jnp.float32) + b_re.astype(jnp.float32)).reshape(-1, N_GROUPS, EXPERTS_PER_GROUP)
    el_sel = jnp.einsum('nge,ng->ne', el, g_hot)
    pe = jax.nn.softmax(el_sel, axis=-1)
    top_v, top_i = lax.top_k(pe, TOP_K_IN_GROUP)
    top_v = top_v / jnp.sum(top_v, axis=-1, keepdims=True)
    gate_e = jnp.sum(jax.nn.one_hot(top_i, EXPERTS_PER_GROUP, dtype=jnp.float32) * top_v[..., None], axis=1)
    gate = g_hot[:, :, None] * (g_prob[:, None] * gate_e)[:, None, :]
    y = jnp.zeros_like(x)
    for g in range(N_GROUPS):
        a = jnp.einsum('nd,edf->nef', x, w_gate[g])
        u = jnp.einsum('nd,edf->nef', x, w_up[g])
        hh = jax.nn.silu(a) * u * gate[:, g, :, None].astype(x.dtype)
        y = y + jnp.einsum('nef,efd->nd', hh, w_down[g])
    return y.reshape(b_, t, d)

def setup_inputs(seed: int = 0) -> dict:
    key = jax.random.key(seed)
    ks = iter(jax.random.split(key, 32))
    f32 = jnp.float32

    def nrm(shape, scale):
        return jax.random.normal(next(ks), shape, f32) * scale

    a_w = (A_HEADS + 2 * A_KV_HEADS) * A_HEAD_DIM
    b_w = B_HEADS * 2 * B_HEAD_DIM
    a_len = min(WINDOW, PAST_LEN)
    G, E, F, D = N_GROUPS, EXPERTS_PER_GROUP, D_EXPERT, D_MODEL
    return {
        "x_prompt": nrm((BATCH, SEQ, D), 1.0),
        "x_sample": nrm((DEC_BATCH, DEC_SEQ, D), 1.0),
        "cache_a_k": nrm((N_A_LAYERS, DEC_BATCH, a_len, A_KV_HEADS, A_HEAD_DIM), 1.0),
        "cache_a_v": nrm((N_A_LAYERS, DEC_BATCH, a_len, A_KV_HEADS, A_HEAD_DIM), 1.0),
        "cache_b_k": nrm((N_B_LAYERS, DEC_BATCH, PAST_LEN, B_HEADS, 2 * B_HEAD_DIM), 1.0),
        "cache_b_v": nrm((N_B_LAYERS, DEC_BATCH, PAST_LEN, B_HEADS, 2 * B_HEAD_DIM), 1.0),
        "norm_mix": 1.0 + nrm((DEPTH, D), 0.01),
        "norm_ffn": 1.0 + nrm((DEPTH, D), 0.01),
        "norm_final": 1.0 + nrm((D,), 0.01),
        "w_a_qkv": nrm((N_A_LAYERS, D, a_w), D ** -0.5),
        "b_a_qkv": nrm((N_A_LAYERS, a_w), 0.02),
        "a_sinks": nrm((N_A_LAYERS, A_HEADS), 0.5),
        "w_a_o": nrm((N_A_LAYERS, A_HEADS * A_HEAD_DIM, D), (A_HEADS * A_HEAD_DIM) ** -0.5),
        "w_b_qkv": nrm((N_B_LAYERS, D, 3 * b_w), D ** -0.5),
        "b_lambda": nrm((N_B_LAYERS, 4, B_HEAD_DIM), 0.1),
        "b_subln": 1.0 + nrm((N_B_LAYERS, 2 * B_HEAD_DIM), 0.01),
        "w_b_o": nrm((N_B_LAYERS, b_w, D), b_w ** -0.5),
        "w_route_group": nrm((DEPTH, D, G), D ** -0.5),
        "b_route_group": nrm((DEPTH, G), 0.01),
        "w_route_expert": nrm((DEPTH, D, G * E), D ** -0.5),
        "b_route_expert": nrm((DEPTH, G * E), 0.01),
        "w_gate": nrm((DEPTH, G, E, D, F), D ** -0.5),
        "w_up": nrm((DEPTH, G, E, D, F), D ** -0.5),
        "w_down": nrm((DEPTH, G, E, F, D), F ** -0.5),
    }

def reference(x_prompt, x_sample, cache_a_k, cache_a_v, cache_b_k, cache_b_v,
              norm_mix, norm_ffn, norm_final,
              w_a_qkv, b_a_qkv, a_sinks, w_a_o,
              w_b_qkv, b_lambda, b_subln, w_b_o,
              w_route_group, b_route_group, w_route_expert, b_route_expert,
              w_gate, w_up, w_down):
    hp, hs = x_prompt, x_sample
    akp, avp, aks, avs = [], [], [], []
    bkp, bvp, bks, bvs = [], [], [], []
    for i in range(DEPTH):
        hp_n = rms_norm(hp, norm_mix[i])
        hs_n = rms_norm(hs, norm_mix[i])
        j = i // N_MIXERS
        if i % N_MIXERS == 0:
            yp, kp_, vp_ = mixer_a_prompt(hp_n, w_a_qkv[j], b_a_qkv[j], a_sinks[j], w_a_o[j])
            ys, ks_, vs_ = mixer_a_sample(hs_n, cache_a_k[j], cache_a_v[j], w_a_qkv[j], b_a_qkv[j], a_sinks[j], w_a_o[j])
            akp.append(kp_); avp.append(vp_); aks.append(ks_); avs.append(vs_)
        else:
            lam_init = 0.8 - 0.6 * float(np.exp(-0.3 * i))
            yp, kp_, vp_ = mixer_b_prompt(hp_n, w_b_qkv[j], b_lambda[j], b_subln[j], w_b_o[j], lam_init)
            ys, ks_, vs_ = mixer_b_sample(hs_n, cache_b_k[j], cache_b_v[j], w_b_qkv[j], b_lambda[j], b_subln[j], w_b_o[j], lam_init)
            bkp.append(kp_); bvp.append(vp_); bks.append(ks_); bvs.append(vs_)
        hp = hp + yp
        hs = hs + ys
        hp = hp + hier_moe(rms_norm(hp, norm_ffn[i]), w_route_group[i], b_route_group[i], w_route_expert[i], b_route_expert[i], w_gate[i], w_up[i], w_down[i])
        hs = hs + hier_moe(rms_norm(hs, norm_ffn[i]), w_route_group[i], b_route_group[i], w_route_expert[i], b_route_expert[i], w_gate[i], w_up[i], w_down[i])
    y_prompt = rms_norm(hp, norm_final)
    y_sample = rms_norm(hs, norm_final)
    a_k_prompt = jnp.stack(akp)
    a_v_prompt = jnp.stack(avp)
    a_k_sample = jnp.stack(aks)
    a_v_sample = jnp.stack(avs)
    b_k_prompt = jnp.stack(bkp)
    b_v_prompt = jnp.stack(bvp)
    b_k_sample = jnp.stack(bks)
    b_v_sample = jnp.stack(bvs)
    return (y_prompt, y_sample, a_k_prompt, a_v_prompt, a_k_sample, a_v_sample, b_k_prompt, b_v_prompt, b_k_sample, b_v_sample)


_drawn_inputs = setup_inputs


def setup_inputs(seed=0):
    import zlib

    import numpy as np

    out = dict(_drawn_inputs(seed))
    spreads = {}
    factors = {'norm_final': 5.968, 'b_subln': 3.491, 'b_route_group': 3.032}
    for name, (base, spread) in spreads.items():
        noise = np.random.default_rng([zlib.crc32(name.encode()), seed]).standard_normal(out[name].shape)
        drawn = base * np.exp(spread * noise) if base else spread * noise
        out[name] = __import__('jax').numpy.asarray(drawn.astype(out[name].dtype))
    for name, factor in factors.items():
        out[name] = (out[name] * factor).astype(out[name].dtype)
    return out
```

```python
from contextlib import ExitStack

import numpy as np

import concourse.bass as bass
from concourse import mybir

F32 = mybir.dt.float32
I32 = mybir.dt.int32
U32 = mybir.dt.uint32
ALU = mybir.AluOpType
ACT = mybir.ActivationFunctionType
AX = mybir.AxisListType.X

D = 1024
SEQ, DEC, PAST = 512, 32, 256
CHUNK, WINDOW = 64, 128
N = SEQ + DEC
P = 128
KD = D // P
NT = 5
ROWS = [P, P, P, P, DEC]
COL = [P * t for t in range(NT)]
HALF_N = N // 2

A_HEADS, A_KV, HD = 16, 4, 64
A_GROUP = A_HEADS // A_KV
AQ, AKV = A_HEADS * HD, A_KV * HD
B_HEADS, BHD = 8, 128
SCALE = HD ** -0.5
LAM_INIT = 0.8 - 0.6 * float(np.exp(-0.3))
EPS, SUB_EPS = 1e-6, 1e-5
MASKED = 1e32
BIG = 1e30

G, EPG, F = 4, 8, 256
NE = G * EPG
CAP = 64
MAX_EXTRA = 17
KEY0 = 2048
OUT_HALF = D // 2

RING, SLOT = 6, 2048
A_STREAM0, A_SLOTS = 0, (AQ + 2 * AKV) // F + D // F
B_SLOTS = 3 * D // F + D // F
MOE_STREAM0 = [A_SLOTS, A_SLOTS + 3 * NE + B_SLOTS]
B_STREAM0 = A_SLOTS + 3 * NE

C_ID, C_REV, C_K1, C_K2, C_HALF, C_THR, C_IOTA, C_END = 0, 128, 160, 165, 170, 171, 179, 211


def a_slopes():
    return [float(np.float32(2.0 ** (-8.0 * (h + 1) / A_HEADS))) for h in range(A_HEADS)]


def b_slopes():
    return [float(np.float32(2.0 ** (-8.0 * (h + 1) / B_HEADS))) for h in range(B_HEADS)]


def shape_constants():
    c = np.zeros((P, C_END), np.float32)
    c[:, C_ID:C_ID + P] = np.eye(P)
    c[:, C_REV:C_REV + NE] = NE - np.arange(NE)
    tok = np.arange(NT)[None, :] * P + np.arange(P)[:, None]
    c[:, C_K1:C_K1 + NT] = KEY0 - 2 * tok
    c[:, C_K2:C_K2 + NT] = KEY0 - 2 * tok - 1
    c[:, C_HALF] = np.arange(P) // CAP
    c[:, C_THR:C_THR + 8] = CAP * np.arange(1, 9)
    c[:, C_IOTA:C_IOTA + NE] = np.arange(NE)
    q = np.arange(P)[:, None]
    ka = np.arange(2 * P)[None, :]
    da = np.abs(q - (ka - P)).astype(np.float32)
    seen = (ka // CHUNK >= q // CHUNK) & (ka // CHUNK <= q // CHUNK + WINDOW // CHUNK)
    da = np.where(seen, da, np.float32(MASKED))
    kb = np.arange(4 * P)[None, :]
    db = np.abs(q + 3 * P - kb).astype(np.float32)
    seen = (kb - 3 * P) // CHUNK <= q // CHUNK
    db = np.where(seen, db, np.float32(MASKED))
    return c, da.astype(np.float32), db.astype(np.float32)


class Link:

    def __init__(self, sem):
        self.sem, self.n = sem, 0

    def __call__(self, eng, instruction):
        self.n += 1
        instruction.then_inc(self.sem, 1)
        eng.wait_ge(self.sem, self.n)


def build(nc, I, O):
    ctx = ExitStack()
    with ctx:
        program(nc, ctx, I, O)


def program(nc, ctx, I, O):
    def sb(name, shape, dt=F32):
        return ctx.enter_context(nc.sbuf_tensor(name, shape, dt))

    def sem(name):
        return ctx.enter_context(nc.semaphore(name))

    hn_dram = nc.dram_tensor("hn_scratch", [N, D], F32).ap()
    y2_dram = nc.dram_tensor("y2_scratch", [4 * N, OUT_HALF], F32).ap()

    ring = sb("ring", [P, RING, SLOT])
    hid = sb("hid", [P, NT, D])
    xT = sb("xT", [P, KD, N])
    oT = xT
    cst = sb("cst", [P, C_END])
    ident = cst[:, C_ID:C_ID + P]
    small = sb("small", [P, 160])
    wr_sb = sb("wr", [P, 2, KD, 36])
    AREA = 29696
    area = sb("area", [P, AREA])

    def part(at, *shape):
        n = int(np.prod(shape))
        v = area[:, at:at + n]
        if len(shape) == 2:
            v = v.rearrange("p (a b) -> p a b", b=shape[1])
        if len(shape) == 3:
            v = v.rearrange("p (a b c) -> p a b c", b=shape[1], c=shape[2])
        return v

    qT = part(0, KD, N)
    R_K = KD * N
    kTa = part(R_K, A_KV, SEQ + WINDOW + DEC)
    kTb = part(R_K, B_HEADS, SEQ + PAST + DEC)
    R_V = R_K + B_HEADS * (SEQ + PAST + DEC)
    va = part(R_V, 6, AKV)
    vb = part(R_V, 7, D)
    R_TAB = R_V + 7 * D
    tabA = part(R_TAB, A_HEADS, 2 * P)
    tabB = part(R_TAB, B_HEADS, 4 * P)
    R_W = R_TAB + 4096
    dist_a = part(R_W, 2 * P)
    dist_b = part(R_W + 5120, 4 * P)
    kst = part(R_W + 512, 6, A_KV * 2 * HD)
    kca = part(R_W + 512 + 3072, AKV)
    kbt = part(R_W, NT, D)
    kcb = part(R_V, 2, D)
    E_A = [part(R_W + 1024 * i, 4, 2 * P) for i in range(3)]
    PT_A = [part(R_W + 3072 + 1024 * i, 4, 2, P) for i in range(2)]
    E_B = [part(R_W + 2048 * i, 4, 4 * P) for i in range(3)]
    PT_B = part(R_W + 6144, 2, 4, P)
    ON = [part(R_W + 7168 + 256 * i, 2, P) for i in range(2)]
    gbc = part(R_W, D)
    ynorm = [part(R_W + D * (1 + i), D) for i in range(2)]
    junk = part(R_W + 3 * D, D)
    xg = [part(1024 * i, D) for i in range(2)]
    xts = [part(2048 + 512 * i, KD, CAP) for i in range(2)]
    sil = [part(3072 + 256 * i, F) for i in range(2)]
    hmul = [part(3584 + 256 * i, F) for i in range(2)]
    hts = [part(4096 + 128 * i, 2, CAP) for i in range(2)]
    yout = [part(4352 + 512 * i, OUT_HALF) for i in range(2)]
    y2b = [part(5376 + 2048 * i, 2, D) for i in range(2)]
    ovw = part(9472, 3, SLOT)
    M0 = 15616
    rT = part(M0, N)
    lg = part(M0 + 544, NT, 36)
    keytab = part(M0 + 736, N)
    topk = part(M0 + 1280, P)
    key = part(M0 + 1408, NT, NE)
    rt = [part(M0 + 1568 + 160 * i, NT, NE) for i in range(5)]
    rs = part(M0 + 2368, 24, 8)
    gw = part(M0 + 2560, 2, 8)
    keytmp = part(M0 + 2576, N)
    ovs = part(M0 + 3120, 128)
    assert M0 + 3248 <= R_W
    idx_i = sb("idx_i", [P, 3, NE], I32)
    cur_i = sb("cur_i", [P, 8], I32)
    ov_i = sb("ov_i", [P, 8], I32)
    ov_u = sb("ov_u", [1, 8], U32)
    ss, rstd, pbase = small[:, 0:8], small[:, 8:16], small[:, 16:24]
    neghalf = small[:, 24:28]
    bq = small[:, 28:36]
    sink8 = small[:, 36:52]
    brT = small[:, 52:54]
    lam4 = small[:, 54:58]
    neglam = small[:, 58:59]
    st = [small[:, 60 + 32 * i:92 + 32 * i] for i in range(3)]
    bkv = sb("bkv", [P, 2 * AKV])
    subg = bkv[:, 0:BHD]
    lamb = bkv[:, 128:384].rearrange("p (a b) -> p a b", b=HD)

    ps = ctx.enter_context(nc.psum_tensor("ps", [P, 8, 512], F32))

    w_ready = [sem(f"w_ready{i}") for i in range(RING)]
    const_in = sem("const_in")
    passed = sem("passed")
    x_in = [sem(f"x_in{i}") for i in range(2)]
    bias_in = sem("bias_in")
    cache_a_in, cache_b_in, lam_in, dist_b_in = sem("cache_a_in"), sem("cache_b_in"), sem("lam_in"), sem("dist_b_in")
    router_in = sem("router_in")
    router_packed = sem("router_packed")
    g_in = sem("g_in")
    sumsq, rstd_ready, y_ready, y_flip, xt_act, xt_dve = (
        sem("sumsq"), sem("rstd_ready"), sem("y_ready"), sem("y_flip"), sem("xt_act"), sem("xt_dve"))
    y_out = [sem(f"y_out{i}") for i in range(2)]
    hid_attn = sem("hid_attn")
    hid_moe = [sem(f"hid_moe{l}") for l in range(2)]
    k_out, v_out = sem("k_out"), sem("v_out")
    pool_own, dve_own, act_own = sem("pool_own"), sem("dve_own"), sem("act_own")
    q_mm, q_act, q_dve = sem("q_mm"), sem("q_act"), sem("q_dve")
    kv_mm, kv_sb, k_flip, k_sb = sem("kv_mm"), sem("kv_sb"), sem("k_flip"), sem("k_sb")
    cachek_sb = sem("cachek_sb")
    tab_ready = sem("tab_ready")
    at = {}
    for layer in "ab":
        for name in ("scores", "biased", "exp", "recip", "probs", "flip", "pt", "pv", "o", "scaled",
                     "sq", "rms", "on", "onflip"):
            if layer == "b" or name not in ("scaled", "sq", "rms", "on", "onflip"):
                at[layer, name] = sem(f"{layer}_{name}")
    ptd = {c: sem(f"{c}_pt_dve") for c in "ab"}
    o_mm = sem("o_mm")
    r_mm, r_sb, r_flip, r_exp, r_key, r_kflip, r_top, r_idx = (
        sem("r_mm"), sem("r_sb"), sem("r_flip"), sem("r_exp"), sem("r_key"), sem("r_kflip"), sem("r_top"), sem("r_idx"))
    r_d = sem("r_d")
    r_tflip = sem("r_tflip")
    lam_sum = sem("lam_sum")
    ones = cst[:, C_REV + NE - 1:C_REV + NE]
    zeroed, ix_cur = sem("zeroed"), sem("ix_cur")
    ix_s = sem("ix_s")
    gath = [sem(f"gath{i}") for i in range(2)]
    scat = [sem(f"scat{i}") for i in range(2)]
    x_flip, x_sb, gu_mm, silu, h_sb, h_flip, ht_sb, d_mm, ye_sb = (
        sem("x_flip"), sem("x_sb"), sem("gu_mm"), sem("silu"), sem("h_sb"), sem("h_flip"), sem("ht_sb"),
        sem("d_mm"), sem("ye_sb"))
    ov = [{k: sem(f"ov{k}{l}") for k in ("count", "own", "pick", "mask", "list", "idx", "w", "gath", "xf", "xs", "gu",
                                         "silu", "h", "hf", "ht", "d", "y", "scat", "irow")} for l in range(2)]
    y2_in = [sem(f"y2_in{i}") for i in range(2)]

    def wait_apart(eng, s, value):
        eng.wait_ge(s, value)
        eng.sem_inc(passed, 1)

    def slot(n):
        return n % RING

    def landed(n):
        return 16 * (n // RING + 1)

    def slot_left(n):
        layer, i = (0, n) if n < A_SLOTS else (1, n - B_STREAM0)
        if i < 4:
            return q_mm, 8 * layer + 2 * i + 2
        n_kv = (2, 8)[layer]
        if i < 4 + n_kv:
            return kv_mm, 2 * NT * layer + NT * (i - 3)
        return o_mm, 4 * NT * layer + 4 * (NT - 1) + i - 3 - n_kv

    def a_unit(u):
        t, j = divmod(u, A_KV)
        if t == 0:
            return t, j, 0, P, P, [(0, P)]
        if t < 4:
            return t, j, (t - 1) * P, 2 * P, 0, [(t - 1, P), (t, P)]
        return t, j, SEQ, WINDOW + DEC, 0, [(4, P), (5, DEC)]

    def b_unit(u):
        t, hp = divmod(u, B_HEADS // 2)
        if t < 4:
            return t, hp, 0, P * (t + 1), (3 - t) * P, [(i, P) for i in range(t + 1)]
        return t, hp, SEQ, PAST + DEC, P, [(4, P), (5, P), (6, DEC)]

    UNITS = NT * 4

    def blk(kb, total):
        return min(P, total - kb * P)

    block = ctx.enter_context(nc.Block())

    @block.sync
    def _(sp):
        def load(n, src):
            sp.dma_start(ring[:, slot(n), :].rearrange("p (k f) -> p k f", f=src.shape[-1]), src) \
              .then_inc(w_ready[slot(n)], 16)

        def rows8(w, lo, hi):
            return w[:, lo:hi].rearrange("(p k) f -> p k f", k=KD)

        def rows128(w, lo, hi):
            return w[:, lo:hi].rearrange("(k p) f -> p k f", p=P)

        wa, wao = I["w_a_qkv"][0], I["w_a_o"][0]
        wb, wbo = I["w_b_qkv"][0], I["w_b_o"][0]
        a_src = [rows8(wa, F * i, F * i + F) for i in range(6)] + [rows128(wao, F * i, F * i + F) for i in range(4)]
        b_src = [rows8(wb, F * i, F * i + F) for i in range(12)] + [rows128(wbo, F * i, F * i + F) for i in range(4)]

        gate = [I["w_gate"][l].rearrange("g e (p k) f -> (g e) p k f", k=KD) for l in range(2)]
        up = [I["w_up"][l].rearrange("g e (p k) f -> (g e) p k f", k=KD) for l in range(2)]
        down = [I["w_down"][l].rearrange("g e (c p) d -> (g e) p c d", p=P) for l in range(2)]

        def expert_loads(layer, e, n):
            own = NE * layer
            for j, w in enumerate((gate, up, down)):
                if isinstance(e, int):
                    sp.wait_ge(*slot_left(n + j - RING))
                elif j < 2:
                    sp.wait_ge(gu_mm, own + e - 1)
                else:
                    sp.wait_ge(d_mm, own + e - 1)
                src = w[layer][e] if isinstance(e, int) else w[layer][bass.ds(e, 1)].rearrange("o p k f -> p (o k) f")
                s = slot(n + j)
                sp.dma_start(ring[:, s, :].rearrange("p (k f) -> p k f", f=src.shape[-1]), src) \
                  .then_inc(w_ready[s], 16)

        def moe_loads(layer):
            base = MOE_STREAM0[layer]
            for e in range(2):
                expert_loads(layer, e, base + 3 * e)
            with sp.Fori(1, NE // 2) as i:
                for u in range(2):
                    expert_loads(layer, 2 * i + u, base + 3 * u)
            s = ov[layer]
            sp.wait_ge(s["count"], 1)
            extra = sp.value_load(ov_i[0:1, layer:layer + 1], min_val=0, max_val=MAX_EXTRA)
            with sp.If(extra > 0):
                with sp.Fori(0, extra) as o:
                    wait_apart(sp, s["pick"], o + 1)
                    e = sp.value_load(ov_u[0:1, 0:1], min_val=0, max_val=NE - 1)
                    for j, w in enumerate((gate, up, down)):
                        src = w[layer][bass.ds(e, 1)].rearrange("o p k f -> p (o k) f")
                        sp.dma_start(ovw[:, j, :].rearrange("p (k f) -> p k f", f=src.shape[-1]), src) \
                          .then_inc(s["w"], 16)

        for n in range(A_SLOTS):
            if n >= RING:
                sp.wait_ge(*slot_left(n - RING))
            load(n, a_src[n])
        moe_loads(0)
        for i in range(B_SLOTS):
            n = B_STREAM0 + i
            if i < RING:
                sp.wait_ge(d_mm if i % 3 == 2 else gu_mm, NE - 1 + i // 3)
            else:
                sp.wait_ge(*slot_left(n - RING))
            load(n, b_src[i])
        moe_loads(1)

    @block.gpsimd
    def _(pool):
        own = Link(pool_own)

        def bcast(dst, src, s):
            pool.dma_start(dst, src).then_inc(s, 16)

        def norm_small(n, rows=None):
            for t in range(NT):
                r = ROWS[t]
                pool.wait_ge(sumsq, NT * n + t + 1)
                own(pool, nc.gpsimd.tensor_scalar(pbase[:r, t:t + 1], ss[:r, t:t + 1], 1.0 / D, EPS, ALU.mult, ALU.add))
                nc.gpsimd.tensor_tensor(rstd[:r, t:t + 1], pbase[:r, t:t + 1], neghalf[:r, 0:1], ALU.pow) \
                    .then_inc(rstd_ready, 1)
                if rows and t > 0:
                    rows(t - 1)
            if rows:
                rows(NT - 1)

        def rows_out(n):
            def rows(t):
                r = ROWS[t]
                pool.wait_ge(y_ready, NT * n + t + 1)
                if n == 4:
                    dst = O[0][0, COL[t]:COL[t] + P, :] if t < 4 else O[1][0]
                else:
                    dst = hn_dram[COL[t]:COL[t] + r, :]
                pool.dma_start(dst, ynorm[t % 2][:r, :]).then_inc(y_out[t % 2], 16)
            norm_small(n, rows)

        def g_load(w, after=None):
            if after is not None:
                pool.wait_ge(*after)
            pool.dma_start(gbc, w.rearrange("(o d) -> o d", o=1).broadcast_to([P, D])).then_inc(g_in, 16)

        pool.dma_start(cst[:, :], I["const"]).then_inc(const_in, 16)
        g_load(I["norm_mix"][0])
        own(pool, nc.gpsimd.memset(neghalf, -0.5))
        pool.dma_start(bq, I["b_a_qkv"][0, 0:AQ].rearrange("(m p) -> p m", p=P),
                       allow_slow_non_contiguous=True).then_inc(bias_in, 16)
        pool.dma_start(bkv[:, :], I["b_a_qkv"][0:1, AQ:AQ + 2 * AKV].broadcast_to([P, 2 * AKV])).then_inc(bias_in, 16)
        pool.dma_start(st[0][:, 0:16], I["a_sinks"][0:1, :].broadcast_to([P, A_HEADS])).then_inc(bias_in, 16)
        norm_small(0)
        pool.wait_ge(xt_act, NT)
        pool.wait_ge(xt_dve, NT)
        pool.wait_ge(y_flip, NT)
        pool.dma_start(dist_a, I["dist_a"]).then_inc(cache_a_in, 16)
        pool.dma_start(kca, I["cache_a_k"][0, 0].rearrange("s h d -> s (h d)")).then_inc(cache_a_in, 16)
        pool.dma_start(va[:, 4, :], I["cache_a_v"][0, 0].rearrange("s h d -> s (h d)")).then_inc(cache_a_in, 16)
        stage_g, stage_e = part(R_K + 2688, 2, KD, G), part(R_K + 2688 + 64, 2, KD, NE)
        for l in range(2):
            pool.dma_start(stage_g[:, l], I["w_route_group"][l].rearrange("(p k) g -> p k g", k=KD)).then_inc(router_in, 16)
            pool.dma_start(stage_e[:, l], I["w_route_expert"][l].rearrange("(p k) g -> p k g", k=KD)).then_inc(router_in, 16)
            pool.dma_start(brT[0:G, l:l + 1], I["b_route_group"][l].rearrange("(g o) -> g o", o=1),
                           allow_slow_non_contiguous=True).then_inc(router_in, 16)
            pool.dma_start(brT[G:G + NE, l:l + 1], I["b_route_expert"][l].rearrange("(g o) -> g o", o=1),
                           allow_slow_non_contiguous=True).then_inc(router_in, 16)
        pool.wait_ge(cache_a_in, 48)
        for h, slope in enumerate(a_slopes()):
            ins = nc.gpsimd.tensor_scalar(tabA[:, h, :], dist_a, -slope / SCALE, 1.0, ALU.mult, ALU.mult)
        ins.then_inc(tab_ready, 1)
        pool.wait_ge(router_in, 128)
        for l in range(2):
            nc.gpsimd.tensor_copy(wr_sb[:, l, :, 0:G], stage_g[:, l])
            ins = nc.gpsimd.tensor_copy(wr_sb[:, l, :, G:G + NE], stage_e[:, l])
        ins.then_inc(router_packed, 1)
        kview = [kst[:, i, :].rearrange("p (h c d) -> p h c d", c=2, d=HD)[:, :, 0, :] for i in range(6)]
        pool.wait_ge(kv_sb, NT)
        pool.wait_ge(cachek_sb, 1)
        pool.dma_start(O[2][0, 0], kview[3]).then_inc(k_out, 16)
        pool.dma_start(O[4][0, 0, 0:WINDOW - DEC], I["cache_a_k"][0, 0, DEC:WINDOW]).then_inc(k_out, 16)
        pool.dma_start(O[4][0, 0, WINDOW - DEC:WINDOW], kview[4][0:DEC]).then_inc(k_out, 16)
        pool.dma_start(O[5][0, 0, 0:WINDOW - DEC], I["cache_a_v"][0, 0, DEC:WINDOW]).then_inc(k_out, 16)
        pool.wait_ge(kv_sb, 2 * NT)
        pool.dma_start(O[3][0, 0].rearrange("s h d -> s (h d)"), va[:, 3, :]).then_inc(k_out, 16)
        pool.dma_start(O[5][0, 0, WINDOW - DEC:WINDOW].rearrange("s h d -> s (h d)"), va[0:DEC, 5, :]).then_inc(k_out, 16)
        for u in range(UNITS):
            t, j, kc, nk, tc, vt = a_unit(u)
            r = ROWS[t]
            pool.wait_ge(at["a", "recip"], u + 1)
            for g in range(4):
                ins = nc.gpsimd.tensor_scalar(E_A[u % 3][:r, g, 0:nk], E_A[u % 3][:r, g, 0:nk],
                                              st[u % 3][:r, 24 + g:25 + g], 1.0, ALU.mult, ALU.mult)
            ins.then_inc(at["a", "probs"], 1)

        def moe(layer):
            n = 1 + 2 * layer
            c0 = "ab"[layer]
            g_load(I["norm_ffn"][layer], (at[c0, "o"], UNITS))
            rows_out(n)
            for b in range(2):
                ins = nc.gpsimd.memset(xg[b], 0.0)
            own(pool, ins)
            for b in range(2):
                pool.wait_ge(y_out[b], 16 * (3, 2)[b] * (layer + 1))
            pool.wait_ge(r_idx, layer + 1)

            def pick(e, b):
                nc.gpsimd.tensor_copy(cur_i[:, 4 * b + 1:4 * b + 2], idx_i[:, 1, bass.ds(e, 1)]).then_inc(ix_cur, 1)

            def gather(e, b):
                wait_apart(pool, ix_cur, NE * layer + e + 1)
                nc.gpsimd.indirect_dma_start(xg[b][0:CAP, :], None, hn_dram,
                                             bass.IndirectOffsetOnAxis(ap=cur_i[0:CAP, 4 * b + 1:4 * b + 2], axis=0),
                                             bounds_check=N - 1, oob_is_err=False).then_inc(gath[b], 16)

            def copy_scatter_index(e, b):
                nc.gpsimd.tensor_copy(cur_i[:, 4 * b + 2:4 * b + 3], idx_i[:, 0, bass.ds(e, 1)]).then_inc(ix_s, 1)

            def scatter(e, b):
                pool.wait_ge(ye_sb, NE * layer + e + 1)
                wait_apart(pool, ix_s, NE * layer + e + 1)
                nc.gpsimd.indirect_dma_start(y2_dram,
                                             bass.IndirectOffsetOnAxis(ap=cur_i[:, 4 * b + 2:4 * b + 3], axis=0),
                                             yout[b], None, bounds_check=4 * N - 1, oob_is_err=False) \
                    .then_inc(scat[b], 16)

            for e in range(2):
                pick(e, e)
                gather(e, e)
            for e in range(2):
                copy_scatter_index(e, e)
                pool.wait_ge(x_flip, NE * layer + e + 1)
                pick(e + 2, e)
                gather(e + 2, e)
                scatter(e, e)
            with pool.Fori(1, NE // 2 - 1) as i:
                for b in range(2):
                    e = 2 * i + b
                    pool.wait_ge(scat[b], (NE // 2 * layer + i) * 16)
                    copy_scatter_index(e, b)
                    pool.wait_ge(x_flip, NE * layer + e + 1)
                    pick(e + 2, b)
                    gather(e + 2, b)
                    scatter(e, b)
            for b in range(2):
                e = NE - 2 + b
                pool.wait_ge(scat[b], (NE // 2 * layer + NE // 2 - 1) * 16)
                copy_scatter_index(e, b)
                scatter(e, b)
            s = ov[layer]
            for b in range(2):
                pool.wait_ge(scat[b], NE // 2 * (layer + 1) * 16)
            pool.wait_ge(s["count"], 1)
            extra = pool.value_load(ov_i[0:1, layer:layer + 1], min_val=0, max_val=MAX_EXTRA)
            with pool.If(extra > 0):
                with pool.Fori(0, extra) as o:
                    wait_apart(pool, s["idx"], o + 1)
                    nc.gpsimd.indirect_dma_start(xg[0][0:CAP, :], None, hn_dram,
                                                 bass.IndirectOffsetOnAxis(ap=ov_i[0:CAP, 4:5], axis=0),
                                                 bounds_check=N - 1, oob_is_err=False).then_inc(s["gath"], 16)
                    wait_apart(pool, s["y"], o + 1)
                    nc.gpsimd.indirect_dma_start(y2_dram,
                                                 bass.IndirectOffsetOnAxis(ap=ov_i[:, 5:6], axis=0),
                                                 yout[0], None, bounds_check=4 * N - 1, oob_is_err=False) \
                        .then_inc(s["scat"], 16)

        moe(0)
        g_load(I["norm_mix"][1], (hid_moe[0], NT))
        pool.dma_start(subg, I["b_subln"][0:1, :].broadcast_to([P, BHD])).then_inc(lam_in, 16)
        pool.dma_start(lamb, I["b_lambda"][0:1].rearrange("o a b -> o (a b)").broadcast_to([P, 4 * HD])
                       .rearrange("p (a b) -> p a b", b=HD)).then_inc(lam_in, 16)
        for i in range(2):
            pool.dma_start(kcb[:, i, :], I["cache_b_k"][0, 0, P * i:P * i + P].rearrange("s h d -> s (h d)")) \
                .then_inc(cache_b_in, 16)
            pool.dma_start(vb[:, 4 + i, :], I["cache_b_v"][0, 0, P * i:P * i + P].rearrange("s h d -> s (h d)")) \
                .then_inc(cache_b_in, 16)
        pool.dma_start(dist_b, I["dist_b"]).then_inc(dist_b_in, 16)
        norm_small(2)
        pool.wait_ge(dist_b_in, 16)
        for h, slope in enumerate(b_slopes()):
            ins = nc.gpsimd.tensor_scalar(tabB[:, h, :], dist_b, -slope / SCALE, 1.0, ALU.mult, ALU.mult)
        ins.then_inc(tab_ready, 1)
        pool.wait_ge(kv_sb, 2 * NT + 4 * NT)
        for t in range(NT):
            dst = O[6][0, 0, COL[t]:COL[t] + P] if t < 4 else O[8][0, 0]
            pool.dma_start(dst.rearrange("s h d -> s (h d)"), kbt[:ROWS[t], t, :]).then_inc(k_out, 16)
        pool.wait_ge(kv_sb, 2 * NT + 8 * NT)
        for t in range(NT):
            dst = O[7][0, 0, COL[t]:COL[t] + P] if t < 4 else O[9][0, 0]
            pool.dma_start(dst.rearrange("s h d -> s (h d)"), vb[:ROWS[t], t if t < 4 else 6, :]).then_inc(v_out, 16)

        def rms(u):
            t = b_unit(u)[0]
            r = ROWS[t]
            pool.wait_ge(at["b", "sq"], u + 1)
            sm = st[u % 3]
            own(pool, nc.gpsimd.tensor_scalar(sm[:r, 22:24], sm[:r, 20:22], 1.0 / BHD, SUB_EPS, ALU.mult, ALU.add))
            nc.gpsimd.tensor_tensor(sm[:r, 24:26], sm[:r, 22:24], neghalf[:r, 0:2], ALU.pow).then_inc(at["b", "rms"], 1)

        for s in range(UNITS + 4):
            if s < UNITS:
                t, hp, kc, nk, tc, vt = b_unit(s)
                r = ROWS[t]
                pool.wait_ge(at["b", "recip"], s + 1)
                for hh in range(2):
                    ins = nc.gpsimd.tensor_scalar(E_B[s % 3][:r, 2 * hh + 1, 0:nk], E_B[s % 3][:r, 2 * hh + 1, 0:nk],
                                                  st[s % 3][:r, 16 + hh:17 + hh], 1.0, ALU.mult, ALU.mult)
                ins.then_inc(at["b", "scaled"], 1)
            if 0 <= s - 2 < UNITS:
                rms(s - 2)
        moe(1)
        g_load(I["norm_final"], (hid_moe[1], NT))
        rows_out(4)
        pool.wait_ge(y_out[0], 16 * 9)
        pool.wait_ge(y_out[1], 16 * 6)
        pool.wait_ge(v_out, 16 * NT)
        pool.wait_ge(k_out, 16 * (6 + NT))

    @block.scalar
    def _(act):
        own = Link(act_own)

        def norm(n):
            for t in range(NT):
                r = ROWS[t]
                if n == 0:
                    act.wait_ge(x_in[t // 2 % 2], 16 if t < 4 else 32)
                elif n % 2:
                    act.wait_ge(hid_attn, 4 * NT * (n // 2) + 4 * t + 4)
                else:
                    act.wait_ge(hid_moe[n // 2 - 1], t + 1)
                if n in (1, 3) and t == 0:
                    act.wait_ge(at["ab"[n // 2], "o"], UNITS)
                if n or t:
                    act.wait_ge(sumsq, NT * n + t)
                nc.scalar.activation(junk[:r, :], hid[:r, t, :], ACT.Square, accum_out=ss[:r, t:t + 1]) \
                    .then_inc(sumsq, 1)
                if n < 4:
                    if t > 0:
                        xt_copy(n, t - 1)
            if n < 4:
                xt_copy(n, NT - 1)

        def xt_copy(n, t):
            r = ROWS[t]
            b = 2 * (t % 2)
            act.wait_ge(y_flip, NT * n + t + 1)
            nc.scalar.activation(xT[:, 0:4, COL[t]:COL[t] + r],
                                 ps[:, b, :].rearrange("p (k c) -> p k c", c=P)[:, :, 0:r], ACT.Copy).then_inc(xt_act, 1)

        act.dma_start(hid[:, 0:2, :], I["x_prompt"][0, 0:2 * P].rearrange("(t p) d -> p t d", p=P)).then_inc(x_in[0], 16)
        act.dma_start(hid[:, 2:4, :], I["x_prompt"][0, 2 * P:4 * P].rearrange("(t p) d -> p t d", p=P)).then_inc(x_in[1], 16)
        act.wait_ge(x_in[0], 16)
        act.dma_start(hid[0:DEC, 4, :], I["x_sample"][0]).then_inc(x_in[0], 16)
        norm(0)
        act.wait_ge(bias_in, 48)
        for m in range(8):
            act.wait_ge(q_mm, m + 1)
            nc.scalar.activation(qT[:, m, 0:HALF_N], ps[:, 2 * (m % 2), 0:HALF_N], ACT.Identity,
                                 bias=bq[:, m:m + 1]).then_inc(q_act, 1)
        for i in range(6):
            act.wait_ge(k_flip, i + 1)
            r = (P, P, P, P, DEC, P)[i]
            c = (0, P, 2 * P, 3 * P, SEQ + WINDOW, SEQ)[i]
            nc.scalar.activation(kTa[:, :, c:c + r], ps[:, 6 + i % 2, :].rearrange("p (h c) -> p h c", c=P)[:, :, 0:r],
                                 ACT.Copy).then_inc(k_sb, 1)

        def attention(layer, unit, E, step):
            nh = 4
            if step < UNITS:
                u = step
                t, j, kc, nk, tc, vt = unit(u)
                r = ROWS[t]
                sm = st[u % 3]
                act.wait_ge(at[layer, "biased"], u + 1)
                for g in range(nh):
                    ins = nc.scalar.activation(E[u % 3][:r, g, 0:nk], E[u % 3][:r, g, 0:nk], ACT.Exp,
                                               bias=sm[:r, 4 + g:5 + g], scale=SCALE, accum_out=sm[:r, 8 + g:9 + g])
                if layer == "a":
                    ins = nc.scalar.activation(sm[:r, 16:20], sm[:r, 12:16], ACT.Exp, scale=SCALE)
                ins.then_inc(at[layer, "exp"], 1)

        for step in range(UNITS + 2):
            attention("a", a_unit, E_A, step)
            u = step - 2
            if 0 <= u < UNITS:
                t, j, kc, nk, tc, vt = a_unit(u)
                r = ROWS[t]
                act.wait_ge(at["a", "flip"], u + 1)
                if u >= 2:
                    act.wait_ge(at["a", "pv"], u - 1)
                nc.scalar.activation(PT_A[u % 2][:, :, 0, 0:r],
                                     ps[:, 4, :].rearrange("p (g c) -> p g c", c=P)[:, :, 0:r],
                                     ACT.Copy).then_inc(at["a", "pt"], 1)

        def moe(layer):
            norm(1 + 2 * layer)
            act.wait_ge(r_exp, 2 * layer + 1)
            nc.scalar.activation(rt[0][:, :, 0:G], rt[0][:, :, 0:G], ACT.Exp).then_inc(r_d, 1)
            act.wait_ge(r_exp, 2 * layer + 2)
            nc.scalar.activation(rs[:, 5, 0:NT], rs[:, 4, 0:NT], ACT.Exp).then_inc(r_d, 1)

            def x_copy(e, b):
                act.wait_ge(x_flip, NE * layer + e + 1)
                if not isinstance(e, int) or e >= 2 or layer:
                    act.wait_ge(gu_mm, NE * layer + e - 1)
                nc.scalar.activation(xts[b].rearrange("p k c -> p (k c)"), ps[:, 2 + b, :], ACT.Copy).then_inc(x_sb, 1)

            def silu_step(e, b):
                act.wait_ge(gu_mm, NE * layer + e + 1)
                if not isinstance(e, int) or e >= 2 or layer:
                    act.wait_ge(h_sb, NE * layer + e - 1)
                nc.scalar.activation(sil[b][CAP:P, :], ps[0:CAP, b, 0:F], ACT.Silu).then_inc(silu, 1)

            x_copy(0, 0)
            for e in range(2):
                silu_step(e, e)
                x_copy(e + 1, 1 - e)
            with act.Fori(1, NE // 2 - 1) as i:
                for u in range(2):
                    silu_step(2 * i + u, u)
                    x_copy(2 * i + u + 1, 1 - u)
            silu_step(NE - 2, 0)
            x_copy(NE - 1, 1)
            silu_step(NE - 1, 1)
            s = ov[layer]
            act.wait_ge(s["count"], 1)
            extra = act.value_load(ov_i[0:1, layer:layer + 1], min_val=0, max_val=MAX_EXTRA)
            with act.If(extra > 0):
                with act.Fori(0, extra) as o:
                    act.wait_ge(s["xf"], o + 1)
                    nc.scalar.activation(xts[0].rearrange("p k c -> p (k c)"), ps[:, 2, :], ACT.Copy).then_inc(s["xs"], 1)
                    act.wait_ge(s["gu"], o + 1)
                    nc.scalar.activation(sil[0][CAP:P, :], ps[0:CAP, 0, 0:F], ACT.Silu).then_inc(s["silu"], 1)
                wait_apart(act, s["scat"], 16 * extra)
            for b in range(2):
                act.wait_ge(scat[b], NE // 2 * (layer + 1) * 16)
            for t in range(NT):
                if t >= 2:
                    act.wait_ge(hid_moe[layer], t - 1)
                r = ROWS[t]
                act.dma_start(y2b[t % 2][:r, :, :],
                              y2_dram[4 * COL[t]:4 * COL[t] + 4 * r, :].rearrange("(p c) d -> p (c d)", c=4)
                              .rearrange("p (a b) -> p a b", b=D)).then_inc(y2_in[t % 2], 16)

        moe(0)
        norm(2)
        act.wait_ge(lam_in, 32)
        act.wait_ge(lam_sum, 1)
        nc.scalar.activation(lam4[:, 2:4], lam4[:, 0:2], ACT.Exp).then_inc(r_d, 1)
        for m in range(8):
            act.wait_ge(q_mm, 8 + m + 1)
            nc.scalar.activation(qT[:, m, 0:HALF_N], ps[:, 2 * (m % 2), 0:HALF_N], ACT.Copy).then_inc(q_act, 1)
        for i in range(4):
            tile, quad = divmod(i, 2)
            act.wait_ge(k_flip, 6 + i + 1)
            nc.scalar.activation(kTb[:, 4 * quad:4 * quad + 4, SEQ + P * tile:SEQ + P * tile + P],
                                 ps[:, 6 + i % 2, :].rearrange("p (h c) -> p h c", c=P), ACT.Copy).then_inc(k_sb, 1)
        for i in range(4 * NT):
            sl, t = divmod(i, NT)
            r = ROWS[t]
            c = COL[t] if t < 4 else SEQ + PAST
            act.wait_ge(k_flip, 10 + i + 1)
            nc.scalar.activation(kTb[:, 2 * sl:2 * sl + 2, c:c + r],
                                 ps[:, 6 + i % 2, 0:2 * P].rearrange("p (h c) -> p h c", c=P)[:, :, 0:r],
                                 ACT.Copy).then_inc(k_sb, 1)
        for step in range(UNITS + 5):
            attention("b", b_unit, E_B, step)
            u = step - 2
            if 0 <= u < UNITS:
                t, hp, kc, nk, tc, vt = b_unit(u)
                r = ROWS[t]
                act.wait_ge(at["b", "flip"], u + 1)
                if u >= 1:
                    act.wait_ge(at["b", "pv"], u)
                for kb, (_, kr) in enumerate(vt):
                    if kb == 0 or kr < P:
                        nb = sum(1 for _, x in vt if x == P) if kb == 0 else 1
                        ins = nc.scalar.activation(
                            PT_B[0:kr, 0, kb:kb + nb, 0:r],
                            ps[0:kr, 4, :].rearrange("p (k c) -> p k c", c=P)[:, kb:kb + nb, 0:r], ACT.Copy)
                ins.then_inc(at["b", "pt"], 1)
            u = step - 3
            if 0 <= u < UNITS:
                r = ROWS[b_unit(u)[0]]
                act.wait_ge(at["b", "pv"], u + 1)
                if u >= 2:
                    act.wait_ge(at["b", "onflip"], u - 1)
                for hh in range(2):
                    ins = nc.scalar.activation(ON[u % 2][:r, hh, :], ps[:r, 6 + u % 2, hh * P:hh * P + P], ACT.Square,
                                               accum_out=st[u % 3][:r, 20 + hh:21 + hh])
                ins.then_inc(at["b", "sq"], 1)
            u = step - 4
            if 0 <= u < UNITS:
                t, hp = b_unit(u)[:2]
                r = ROWS[t]
                act.wait_ge(at["b", "onflip"], u + 1)
                nc.scalar.activation(oT[:, 2 * hp:2 * hp + 2, COL[t]:COL[t] + r],
                                     ps[:, 6 + u % 2, 2 * P:4 * P].rearrange("p (h c) -> p h c", c=P)[:, :, 0:r],
                                     ACT.Copy).then_inc(at["b", "o"], 1)
        moe(1)
        norm(4)

    @block.vector
    def _(dve):
        own = Link(dve_own)

        def norm(n):
            def rows(t):
                r = ROWS[t]
                dve.wait_ge(rstd_ready, NT * n + t + 1)
                if t == 0:
                    dve.wait_ge(g_in, 16 * (n + 1))
                if t >= 2 and n < 4:
                    dve.wait_ge(y_flip, NT * n + t - 1)
                if t >= 2 and n in (1, 3):
                    before = 3 * (n // 2), 2 * (n // 2)
                    dve.wait_ge(y_out[t % 2], 16 * (before[t % 2] + t // 2))
                if t >= 2 and n == 4:
                    dve.wait_ge(y_out[t % 2], 16 * ((6, 4)[t % 2] + t // 2))
                nc.vector.scalar_tensor_tensor(ynorm[t % 2][:r, :], hid[:r, t, :], rstd[:r, t:t + 1], gbc[:r, :],
                                               ALU.mult, ALU.mult).then_inc(y_ready, 1)

            def xt_copy(t):
                r = ROWS[t]
                b = 2 * (t % 2) + 1
                dve.wait_ge(y_flip, NT * n + t + 1)
                nc.vector.tensor_copy(xT[:, 4:8, COL[t]:COL[t] + r],
                                      ps[:, b, :].rearrange("p (k c) -> p k c", c=P)[:, :, 0:r]).then_inc(xt_dve, 1)

            for t in range(NT):
                rows(t)
                if t > 0 and n < 4:
                    xt_copy(t - 1)
            if n < 4:
                xt_copy(NT - 1)

        norm(0)
        dve.wait_ge(bias_in, 48)
        own(dve, nc.vector.tensor_scalar(sink8, st[0][:, 0:16], 1.0 / SCALE, None, ALU.mult))
        for m in range(8):
            dve.wait_ge(q_mm, m + 1)
            nc.vector.tensor_scalar(qT[:, m, HALF_N:N], ps[:, 2 * (m % 2) + 1, 0:HALF_N], bq[:, m:m + 1], None,
                                    ALU.add).then_inc(q_dve, 1)
        dve.wait_ge(cache_a_in, 48)

        def twice(x):
            return x.rearrange("p (h d) -> p h d", d=HD).unsqueeze(2).broadcast_to([x.shape[0], A_KV, 2, HD])

        def dup(i, r):
            return kst[:r, i, :].rearrange("p (h c d) -> p h c d", c=2, d=HD)

        nc.vector.tensor_copy(dup(5, P), twice(kca)).then_inc(cachek_sb, 1)
        for t in range(NT):
            r = ROWS[t]
            dve.wait_ge(kv_mm, t + 1)
            for c in range(2):
                ins = nc.vector.tensor_tensor(dup(t, r)[:, :, c, :],
                                              ps[:r, 4 + t % 2, 0:AKV].rearrange("p (h d) -> p h d", d=HD),
                                              bkv[:r, 0:AKV].rearrange("p (h d) -> p h d", d=HD), ALU.add)
            ins.then_inc(kv_sb, 1)
        for t in range(NT):
            r = ROWS[t]
            i = NT + t
            dve.wait_ge(kv_mm, i + 1)
            nc.vector.tensor_tensor(va[:r, t if t < 4 else 5, :], ps[:r, 4 + i % 2, 0:AKV], bkv[:r, AKV:2 * AKV],
                                    ALU.add).then_inc(kv_sb, 1)

        def bias_max(layer, unit, E, u, bank, tab, head):
            t, j, kc, nk, tc, vt = unit(u)
            r = ROWS[t]
            sm = st[u % 3]
            dve.wait_ge(at[layer, "scores"], u + 1)
            if u >= 3:
                dve.wait_ge(at[layer, "flip"], u - 2)
            for g in range(4):
                b, c = bank(u, g)
                ins = nc.vector.tensor_tensor_reduce(
                    out=E[u % 3][:r, g, 0:nk], in0=ps[:r, b, c:c + nk], in1=tab[:r, head(j, g), tc:tc + nk],
                    scale=1.0, scalar=-3e38, op0=ALU.add, op1=ALU.max, accum_out=sm[:r, g:g + 1])
            own(dve, ins)
            if layer == "a":
                own(dve, nc.vector.tensor_tensor(sm[:r, 0:4], sm[:r, 0:4], sink8[:r, 4 * j:4 * j + 4], ALU.max))
                nc.vector.tensor_tensor(sm[:r, 12:16], sink8[:r, 4 * j:4 * j + 4], sm[:r, 0:4], ALU.subtract)
            nc.vector.tensor_scalar(sm[:r, 4:8], sm[:r, 0:4], -SCALE, None, ALU.mult).then_inc(at[layer, "biased"], 1)

        def bank_a(u, g):
            return 2 * (u % 2) + g % 2, (g // 2) * 2 * P

        dve.wait_ge(tab_ready, 1)
        dve.wait_ge(k_out, 16 * 6)
        dve.wait_ge(k_flip, 6)
        dve.wait_ge(router_packed, 1)
        for step in range(UNITS + 3):
            if step < UNITS:
                bias_max("a", a_unit, E_A, step, bank_a, tabA, lambda j, g: 4 * j + g)
            u = step - 1
            if 0 <= u < UNITS:
                r = ROWS[a_unit(u)[0]]
                sm = st[u % 3]
                dve.wait_ge(at["a", "exp"], u + 1)
                own(dve, nc.vector.tensor_tensor(sm[:r, 20:24], sm[:r, 8:12], sm[:r, 16:20], ALU.add))
                nc.vector.reciprocal(sm[:r, 24:28], sm[:r, 20:24]).then_inc(at["a", "recip"], 1)
            u = step - 2
            if 0 <= u < UNITS:
                t, j, kc, nk, tc, vt = a_unit(u)
                if len(vt) > 1:
                    r, kr = ROWS[t], vt[1][1]
                    dve.wait_ge(at["a", "flip"], u + 1)
                    if u >= 2:
                        dve.wait_ge(at["a", "pv"], u - 1)
                    nc.vector.tensor_copy(
                        PT_A[u % 2][:kr, :, 1, 0:r],
                        ps[:kr, 5, :].rearrange("p (g c) -> p g c", c=P)[:, :, 0:r]) \
                        .then_inc(ptd["a"], 1)
            u = step - 3
            if 0 <= u < UNITS:
                t, j = a_unit(u)[:2]
                r = ROWS[t]
                dve.wait_ge(at["a", "pv"], u + 1)
                nc.vector.tensor_copy(oT[:, 2 * j:2 * j + 2, COL[t]:COL[t] + r],
                                      ps[:, 6 + u % 2, 0:2 * P].rearrange("p (m c) -> p m c", c=P)[:, :, 0:r]) \
                    .then_inc(at["a", "o"], 1)

        def residual(layer):
            for t in range(NT):
                r = ROWS[t]
                for s in range(4):
                    i = 4 * t + s
                    dve.wait_ge(o_mm, 4 * NT * layer + i + 1)
                    h = hid[:r, t, F * s:F * s + F]
                    ins = nc.vector.tensor_tensor(h, h, ps[:r, 4 + i % 4, 0:F], ALU.add)
                    ins.then_inc(hid_attn, 1)

        residual(0)

        def moe(layer):
            norm(1 + 2 * layer)
            s = ov[layer]
            own(dve, nc.vector.memset(lg, 0.0))
            dve.wait_ge(r_mm, layer + 1)
            dve.wait_ge(router_in, 128)
            for h in range(2):
                ins = nc.vector.tensor_scalar(rT[0:36, HALF_N * h:HALF_N * h + HALF_N], ps[0:36, 4 + h, 0:HALF_N],
                                              brT[0:36, layer:layer + 1], None, ALU.add)
            ins.then_inc(r_sb, 1)
            dve.wait_ge(r_flip, layer + 1)
            pr = ps[:, 6, 0:NT * 36].rearrange("p (t c) -> p t c", c=36)
            nc.vector.tensor_copy(lg[:, 0:4, :], pr[:, 0:4, :])
            own(dve, nc.vector.tensor_copy(lg[0:DEC, 4, :], pr[0:DEC, 4, :]))

            def per_tile(i):
                return rs[:, i, 0:NT]

            def over(x, w):
                return x.unsqueeze(2).broadcast_to([P, NT, w])

            gl, el = lg[:, :, 0:G], lg[:, :, G:G + NE]
            own(dve, nc.vector.tensor_reduce(per_tile(0), gl, AX, ALU.max))
            nc.vector.tensor_tensor(rt[0][:, :, 0:G], gl, over(per_tile(0), G), ALU.subtract).then_inc(r_exp, 1)
            ghot = rt[1][:, :, 0:G]
            own(dve, nc.vector.tensor_tensor(rt[2][:, :, 0:G], gl, over(per_tile(0), G), ALU.is_equal))
            own(dve, nc.vector.tensor_tensor(rt[2][:, :, 0:G], rt[2][:, :, 0:G],
                                             cst[:, C_REV:C_REV + G].unsqueeze(1).broadcast_to([P, NT, G]), ALU.mult))
            own(dve, nc.vector.tensor_reduce(per_tile(1), rt[2][:, :, 0:G], AX, ALU.max))
            own(dve, nc.vector.tensor_tensor(ghot, rt[2][:, :, 0:G], over(per_tile(1), G), ALU.is_equal))
            own(dve, nc.vector.tensor_scalar(ghot, ghot, BIG, -BIG, ALU.mult, ALU.add))
            em = rt[3]
            own(dve, nc.vector.tensor_tensor(
                em.rearrange("p t (g e) -> p t g e", e=EPG), el.rearrange("p t (g e) -> p t g e", e=EPG),
                ghot.unsqueeze(3).broadcast_to([P, NT, G, EPG]), ALU.add))

            def top(dst, best, free):
                own(dve, nc.vector.tensor_reduce(per_tile(best), em, AX, ALU.max))
                own(dve, nc.vector.tensor_tensor(rt[4], em, over(per_tile(best), NE), ALU.is_equal))
                own(dve, nc.vector.tensor_tensor(
                    rt[4], rt[4], cst[:, C_REV:C_REV + NE].unsqueeze(1).broadcast_to([P, NT, NE]), ALU.mult))
                own(dve, nc.vector.tensor_reduce(per_tile(free), rt[4], AX, ALU.max))
                own(dve, nc.vector.tensor_tensor(dst, rt[4], over(per_tile(free), NE), ALU.is_equal))

            h1, h2 = rt[1], rt[2]
            top(h1, 2, 6)
            own(dve, nc.vector.scalar_tensor_tensor(em, h1, -2 * BIG, em, ALU.mult, ALU.add))
            top(h2, 3, 7)
            nc.vector.tensor_tensor(per_tile(4), per_tile(3), per_tile(2), ALU.subtract).then_inc(r_exp, 1)
            own(dve, nc.vector.tensor_tensor(h1, h1, over(cst[:, C_K1:C_K1 + NT], NE), ALU.mult))
            own(dve, nc.vector.tensor_tensor(h2, h2, over(cst[:, C_K2:C_K2 + NT], NE), ALU.mult))
            own(dve, nc.vector.tensor_tensor(key, h1, h2, ALU.add))
            nc.vector.tensor_scalar(rt[4], key, 0.0, None, ALU.is_gt).then_inc(r_key, 1)
            dve.wait_ge(r_d, 2 * layer + 2 + layer)
            own(dve, nc.vector.tensor_reduce(per_tile(8), rt[0][:, :, 0:G], AX, ALU.add))
            own(dve, nc.vector.reciprocal(per_tile(9), per_tile(8)))
            own(dve, nc.vector.tensor_scalar(per_tile(10), per_tile(5), 1.0, None, ALU.add))
            own(dve, nc.vector.reciprocal(per_tile(11), per_tile(10)))
            own(dve, nc.vector.tensor_tensor(gw[:, 0, 0:NT], per_tile(9), per_tile(11), ALU.mult))
            own(dve, nc.vector.tensor_tensor(gw[:, 1, 0:NT], gw[:, 0, 0:NT], per_tile(5), ALU.mult))
            dve.wait_ge(r_kflip, layer + 1)
            nc.vector.tensor_copy(keytab[0:NE, 0:SEQ], ps[0:NE, 5, :])
            own(dve, nc.vector.tensor_copy(keytab[0:NE, SEQ:N], ps[0:NE, 4, 0:DEC]))
            cnt = ovs[0:1, 0:NE]
            own(dve, nc.vector.tensor_scalar(cnt, ps[0:1, 7, 0:NE], float(-CAP), None, ALU.add))
            own(dve, nc.vector.tensor_tensor(
                keytmp[0:1, 0:NE * 8].rearrange("p (e j) -> p e j", j=8),
                cnt.unsqueeze(2).broadcast_to([1, NE, 8]),
                cst[0:1, C_THR:C_THR + 8].unsqueeze(1).broadcast_to([1, NE, 8]), ALU.subtract))
            own(dve, nc.vector.tensor_scalar(keytmp[0:1, 0:NE * 8], keytmp[0:1, 0:NE * 8], float(-CAP), None, ALU.is_gt))
            own(dve, nc.vector.tensor_reduce(ovs[0:1, 32:33], keytmp[0:1, 0:NE * 8], AX, ALU.add))
            nc.vector.tensor_copy(ov_i[0:1, layer:layer + 1], ovs[0:1, 32:33]).then_inc(s["count"], 1)

            def top64(table):
                return [lambda r=r: nc.vector.max(topk[0:NE, 8 * r:8 * r + 8], table[0:NE, :]) for r in range(CAP // 8)], \
                       [lambda r=r: nc.vector.match_replace(table[0:NE, :], topk[0:NE, 8 * r:8 * r + 8],
                                                            table[0:NE, :], -1.0) for r in range(CAP // 8)]

            take, strike = top64(keytab)
            for r in range(CAP // 8):
                own(dve, take[r]())
                own(dve, strike[r]())
            nc.vector.tensor_copy(topk[0:NE, CAP:P], topk[0:NE, 0:CAP]).then_inc(r_top, 1)
            dve.wait_ge(r_tflip, layer + 1)
            own(dve, nc.vector.tensor_scalar(idx_i[:, 2, :], ps[:, 6, 0:NE], -1.0, float(KEY0), ALU.mult, ALU.add))
            own(dve, nc.vector.tensor_scalar(rt[0].rearrange("p t e -> p (t e)")[:, 0:NE], ps[:, 6, 0:NE],
                                             -2.0, float(2 * KEY0), ALU.mult, ALU.add))
            own(dve, nc.vector.tensor_scalar(idx_i[:, 0, :], rt[0].rearrange("p t e -> p (t e)")[:, 0:NE],
                                             cst[:, C_HALF:C_HALF + 1], None, ALU.add))
            nc.vector.tensor_scalar(idx_i[:, 1, :], idx_i[:, 2, :], 1, None, ALU.arith_shift_right).then_inc(r_idx, 1)

            def mult(e, b):
                dve.wait_ge(silu, NE * layer + e + 1)
                if not isinstance(e, int) or e >= 2 or layer:
                    dve.wait_ge(h_flip, NE * layer + e - 1)
                nc.vector.tensor_tensor(hmul[b][CAP:P, :], sil[b][CAP:P, :], ps[CAP:P, b, 0:F], ALU.mult) \
                    .then_inc(h_sb, 1)

            def ht_copy(e, b):
                dve.wait_ge(h_flip, NE * layer + e + 1)
                if not isinstance(e, int) or e >= 2 or layer:
                    dve.wait_ge(d_mm, NE * layer + e - 1)
                nc.vector.tensor_copy(hts[b].rearrange("p c q -> p (c q)"), ps[:, 4 + b, 0:2 * CAP]).then_inc(ht_sb, 1)

            def y_copy(e, b, count=None):
                dve.wait_ge(d_mm, NE * layer + e + 1)
                if count is not None:
                    dve.wait_ge(scat[b], count)
                nc.vector.tensor_copy(yout[b], ps[:, 6 + b, :]).then_inc(ye_sb, 1)

            half = NE // 2 * layer
            for e in range(2):
                mult(e, e)
                ht_copy(e, e)
                if e:
                    y_copy(0, 0, 16 * half if layer else None)

            def two(i, before):
                mult(2 * i, 0)
                ht_copy(2 * i, 0)
                y_copy(2 * i - 1, 1, before)
                mult(2 * i + 1, 1)
                ht_copy(2 * i + 1, 1)
                y_copy(2 * i, 0, 16 * (half + i))

            two(1, 16 * half if layer else None)
            with dve.Fori(2, NE // 2) as i:
                two(i, 16 * (half + i - 1))
            y_copy(NE - 1, 1, 16 * (half + NE // 2 - 1))

            dve.wait_ge(s["count"], 1)
            for b in range(2):
                dve.wait_ge(scat[b], 16 * NE // 2 * (layer + 1))
            extra = dve.value_load(ov_i[0:1, layer:layer + 1], min_val=0, max_val=MAX_EXTRA)
            STEPS = 28
            with dve.If(extra > 0):
                with dve.Fori(0, extra) as o:
                    k = [0]

                    def link(ins):
                        k[0] += 1
                        ins.then_inc(s["own"], 1)
                        wait_apart(dve, s["own"], o * STEPS + k[0])

                    best, hot = ovs[0:1, 40:48], ovs[0:1, 64:96]
                    link(nc.vector.max(best, cnt))
                    link(nc.vector.max_index(ov_u[:, :], best, cnt))
                    link(nc.vector.tensor_copy(ovs[0:1, 48:49], ov_u[0:1, 0:1]))
                    link(nc.vector.tensor_scalar(hot, cst[0:1, C_IOTA:C_IOTA + NE], ovs[0:1, 48:49], None, ALU.is_equal))
                    nc.vector.scalar_tensor_tensor(cnt, hot, float(-CAP), cnt, ALU.mult, ALU.add).then_inc(s["pick"], 1)
                    mcol, mnot = ovs[0:NE, 96:97], ovs[0:NE, 97:98]
                    dve.wait_ge(s["mask"], o + 1)
                    link(nc.vector.tensor_copy(mcol, ps[0:NE, 7, 0:1]))
                    link(nc.vector.tensor_scalar(mnot, mcol, -1.0, 1.0, ALU.mult, ALU.add))
                    link(nc.vector.tensor_scalar(keytmp[0:NE, :], keytab[0:NE, :], mcol, None, ALU.mult))
                    take, strike = top64(keytmp)
                    for r in range(CAP // 8):
                        link(take[r]())
                        link(strike[r]())
                    link(nc.vector.tensor_scalar(keytmp[0:NE, :], keytmp[0:NE, :], mcol, None, ALU.mult))
                    link(nc.vector.scalar_tensor_tensor(keytab[0:NE, :], keytab[0:NE, :], mnot, keytmp[0:NE, :],
                                                        ALU.mult, ALU.add))
                    nc.vector.tensor_copy(topk[0:NE, CAP:P], topk[0:NE, 0:CAP]).then_inc(s["list"], 1)
                    dve.wait_ge(s["irow"], o + 1)
                    link(nc.vector.tensor_scalar(ov_i[:, 6:7], ps[:, 7, 8:9], -1.0, float(KEY0), ALU.mult, ALU.add))
                    link(nc.vector.tensor_scalar(ovs[:, 98:99], ps[:, 7, 8:9], -2.0, float(2 * KEY0), ALU.mult, ALU.add))
                    link(nc.vector.tensor_scalar(ov_i[:, 5:6], ovs[:, 98:99], cst[:, C_HALF:C_HALF + 1], None, ALU.add))
                    nc.vector.tensor_scalar(ov_i[:, 4:5], ov_i[:, 6:7], 1, None, ALU.arith_shift_right) \
                        .then_inc(s["idx"], 1)
                    dve.wait_ge(s["silu"], o + 1)
                    nc.vector.tensor_tensor(hmul[0][CAP:P, :], sil[0][CAP:P, :], ps[CAP:P, 0, 0:F], ALU.mult) \
                        .then_inc(s["h"], 1)
                    dve.wait_ge(s["hf"], o + 1)
                    nc.vector.tensor_copy(hts[0].rearrange("p c q -> p (c q)"), ps[:, 4, 0:2 * CAP]).then_inc(s["ht"], 1)
                    dve.wait_ge(s["d"], o + 1)
                    nc.vector.tensor_copy(yout[0], ps[:, 6, :]).then_inc(s["y"], 1)
                    wait_apart(dve, s["scat"], 16 * o + 16)
                    assert k[0] == STEPS, k
            for t in range(NT):
                r = ROWS[t]
                dve.wait_ge(y2_in[t % 2], 16 * ((3, 2)[t % 2] * layer + t // 2 + 1))
                h = hid[:r, t, :]
                own(dve, nc.vector.scalar_tensor_tensor(h, y2b[t % 2][:r, 0, :], gw[:r, 0, t:t + 1], h, ALU.mult, ALU.add))
                nc.vector.scalar_tensor_tensor(h, y2b[t % 2][:r, 1, :], gw[:r, 1, t:t + 1], h, ALU.mult, ALU.add) \
                    .then_inc(hid_moe[layer], 1)

        moe(0)
        norm(2)
        dve.wait_ge(lam_in, 32)
        own(dve, nc.vector.tensor_tensor(lamb[:, 0, :], lamb[:, 0, :], lamb[:, 1, :], ALU.mult))
        own(dve, nc.vector.tensor_tensor(lamb[:, 2, :], lamb[:, 2, :], lamb[:, 3, :], ALU.mult))
        own(dve, nc.vector.tensor_scalar(subg, subg, 1.0 - LAM_INIT, None, ALU.mult))
        nc.vector.tensor_reduce(lam4[:, 0:2], lamb.rearrange("p (a b) d -> p a b d", b=2)[:, :, 0, :], AX, ALU.add) \
            .then_inc(lam_sum, 1)
        for m in range(8):
            dve.wait_ge(q_mm, 8 + m + 1)
            nc.vector.tensor_copy(qT[:, m, HALF_N:N], ps[:, 2 * (m % 2) + 1, 0:HALF_N]).then_inc(q_dve, 1)
        dve.wait_ge(r_d, 3)
        own(dve, nc.vector.tensor_tensor(neglam, lam4[:, 3:4], lam4[:, 2:3], ALU.subtract))
        own(dve, nc.vector.tensor_scalar(neglam, neglam, -LAM_INIT, None, ALU.add))
        for i in range(8 * NT):
            sl, t = divmod(i, NT)
            r = ROWS[t]
            dve.wait_ge(kv_mm, 2 * NT + i + 1)
            if sl < 4:
                if i == 0:
                    dve.wait_ge(tab_ready, 2)
                dst = kbt[:r, t, F * sl:F * sl + F]
            else:
                if i == 4 * NT:
                    dve.wait_ge(k_flip, 10)
                dst = vb[:r, t if t < 4 else 6, F * (sl - 4):F * (sl - 4) + F]
            nc.vector.tensor_copy(dst, ps[:r, 4 + i % 2, 0:F]).then_inc(kv_sb, 1)
        dve.wait_ge(k_out, 16 * (6 + NT))
        dve.wait_ge(k_flip, 10 + 4 * NT)
        for step in range(UNITS + 5):
            if step < UNITS:
                bias_max("b", b_unit, E_B, step, lambda u, g: (g, 0), tabB, lambda j, g: 2 * j + g // 2)
            u = step - 1
            if 0 <= u < UNITS:
                r = ROWS[b_unit(u)[0]]
                sm = st[u % 3]
                dve.wait_ge(at["b", "exp"], u + 1)
                own(dve, nc.vector.reciprocal(sm[:r, 12:16], sm[:r, 8:12]))
                nc.vector.tensor_scalar(sm[:r, 16:18], sm[:r, 12:16].rearrange("p (h c) -> p h c", c=2)[:, :, 1],
                                        neglam[:r, :], None, ALU.mult).then_inc(at["b", "recip"], 1)
            u = step - 2
            if 0 <= u < UNITS:
                t, hp, kc, nk, tc, vt = b_unit(u)
                r = ROWS[t]
                Eu = E_B[u % 3]
                dve.wait_ge(at["b", "scaled"], u + 1)
                for hh in range(2):
                    ins = nc.vector.scalar_tensor_tensor(Eu[:r, 2 * hh, 0:nk], Eu[:r, 2 * hh, 0:nk],
                                                         st[u % 3][:r, 12 + 2 * hh:13 + 2 * hh],
                                                         Eu[:r, 2 * hh + 1, 0:nk], ALU.mult, ALU.add)
                ins.then_inc(at["b", "probs"], 1)
            u = step - 2
            if 0 <= u < UNITS:
                t, hp, kc, nk, tc, vt = b_unit(u)
                r = ROWS[t]
                dve.wait_ge(at["b", "flip"], u + 1)
                if u >= 1:
                    dve.wait_ge(at["b", "pv"], u)
                for kb, (_, kr) in enumerate(vt):
                    if kb == 0 or kr < P:
                        nb = sum(1 for _, x in vt if x == P) if kb == 0 else 1
                        ins = nc.vector.tensor_copy(
                            PT_B[0:kr, 1, kb:kb + nb, 0:r],
                            ps[0:kr, 5, :].rearrange("p (k c) -> p k c", c=P)[:, kb:kb + nb, 0:r])
                ins.then_inc(ptd["b"], 1)
            u = step - 3
            if 0 <= u < UNITS:
                r = ROWS[b_unit(u)[0]]
                dve.wait_ge(at["b", "rms"], u + 1)
                for hh in range(2):
                    ins = nc.vector.scalar_tensor_tensor(ON[u % 2][:r, hh, :], ps[:r, 6 + u % 2, hh * P:hh * P + P],
                                                         st[u % 3][:r, 24 + hh:25 + hh], subg[:r, :], ALU.mult, ALU.mult)
                ins.then_inc(at["b", "on"], 1)
        residual(1)
        moe(1)
        norm(4)

    @block.tensor
    def _(pe):
        def norm(n):
            for t in range(NT):
                r = ROWS[t]
                b = 2 * (t % 2)
                pe.wait_ge(y_ready, NT * n + t + 1)
                if t == 0 and n == 0:
                    pe.wait_ge(const_in, 16)
                if t >= 2:
                    pe.wait_ge(xt_act, NT * n + t - 1)
                    pe.wait_ge(xt_dve, NT * n + t - 1)
                y = ynorm[t % 2][:r, :].rearrange("p (c k) -> p k c", k=KD)
                for k in range(KD):
                    ins = nc.tensor.transpose(ps[:, b + k // 4, (k % 4) * P:(k % 4) * P + r], y[:, k, :], ident[:r, :r])
                ins.then_inc(y_flip, 1)
            pe.wait_ge(xt_act, NT * n + NT)
            pe.wait_ge(xt_dve, NT * n + NT)

        def ring_k(n):
            return ring[:, slot(n), :].rearrange("p (k f) -> p k f", f=F)

        def arrived(n):
            pe.wait_ge(w_ready[slot(n)], landed(n))

        def q_proj(layer, n0):
            for m in range(8):
                n = n0 + m // 2
                if m % 2 == 0:
                    arrived(n)
                if m >= 2 or layer:
                    pe.wait_ge(q_act, 8 * layer + m - 1)
                    pe.wait_ge(q_dve, 8 * layer + m - 1)
                w = ring_k(n)[:, :, (m % 2) * P:(m % 2) * P + P]
                for h in range(2):
                    for k in range(KD):
                        ins = nc.tensor.matmul(ps[:, 2 * (m % 2) + h, 0:HALF_N], w[:, k, :],
                                               xT[:, k, HALF_N * h:HALF_N * h + HALF_N], start=k == 0, stop=k == KD - 1)
                        if h and k == KD - 1:
                            ins.then_inc(q_mm, 1)

        def rows_mm(bank, t, n):
            r = ROWS[t]
            for k in range(KD):
                ins = nc.tensor.matmul(ps[:r, bank, 0:F], xT[:, k, COL[t]:COL[t] + r], ring_k(n)[:, k, :],
                                       start=k == 0, stop=k == KD - 1)
            return ins

        norm(0)
        q_proj(0, 0)
        pe.wait_ge(cachek_sb, 1)

        def flip_a(i, order):
            r = (P, P, P, P, DEC, P)[i]
            if order >= 2:
                pe.wait_ge(k_sb, order - 1)
            for j in range(A_KV):
                ins = nc.tensor.transpose(ps[:, 6 + order % 2, j * P:j * P + r], kst[:r, i, j * P:j * P + P], ident[:r, :r])
            ins.then_inc(k_flip, 1)

        arrived(4)
        for t in range(NT + 1):
            if t < NT:
                if t >= 2:
                    pe.wait_ge(kv_sb, t - 1)
                rows_mm(4 + t % 2, t, 4).then_inc(kv_mm, 1)
            if t > 0:
                pe.wait_ge(kv_sb, t)
                flip_a(t - 1, t - 1)
        flip_a(5, 5)
        arrived(5)
        for t in range(NT):
            pe.wait_ge(kv_sb, NT + t - 1)
            rows_mm(4 + (NT + t) % 2, t, 5).then_inc(kv_mm, 1)
        pe.wait_ge(q_act, 8)
        pe.wait_ge(q_dve, 8)
        pe.wait_ge(k_sb, 6)
        pe.wait_ge(kv_sb, 2 * NT)
        pe.wait_ge(cache_a_in, 48)
        for step in range(UNITS + 3):
            if step < UNITS:
                u = step
                t, j, kc, nk, tc, vt = a_unit(u)
                r = ROWS[t]
                if u >= 2:
                    pe.wait_ge(at["a", "biased"], u - 1)
                for g in range(4):
                    lo = HD * (g % 2)
                    ins = nc.tensor.matmul(ps[:r, 2 * (u % 2) + g % 2, (g // 2) * 2 * P:(g // 2) * 2 * P + nk],
                                           qT[lo:lo + HD, 2 * j + g // 2, COL[t]:COL[t] + r],
                                           kTa[lo:lo + HD, j, kc:kc + nk], start=True, stop=True)
                ins.then_inc(at["a", "scores"], 1)
            u = step - 3
            if 0 <= u < UNITS:
                t, j, kc, nk, tc, vt = a_unit(u)
                r = ROWS[t]
                pe.wait_ge(at["a", "pt"], u + 1)
                if u >= 4:
                    pe.wait_ge(ptd["a"], u - 3)
                if u >= 2:
                    pe.wait_ge(at["a", "o"], u - 1)
                for gp in range(2):
                    for kb, (v, kr) in enumerate(vt):
                        for gh in range(2):
                            ins = nc.tensor.matmul(ps[HD * gh:HD * gh + HD, 6 + u % 2, gp * P:gp * P + r],
                                                   va[:kr, v, j * HD:j * HD + HD],
                                                   PT_A[u % 2][:kr, 2 * gp + gh, kb, 0:r],
                                                   start=kb == 0, stop=kb == len(vt) - 1)
                ins.then_inc(at["a", "pv"], 1)
            u = step - 2
            if 0 <= u < UNITS:
                t, j, kc, nk, tc, vt = a_unit(u)
                r = ROWS[t]
                pe.wait_ge(at["a", "probs"], u + 1)
                if u >= 1:
                    pe.wait_ge(at["a", "pt"], u)
                if u >= 5:
                    pe.wait_ge(ptd["a"], u - 4)
                for g in range(4):
                    for kb, (v, kr) in enumerate(vt):
                        ins = nc.tensor.transpose(ps[:kr, 4 + kb, g * P:g * P + r], E_A[u % 3][:r, g, kb * P:kb * P + kr],
                                                  ident[:r, :r])
                ins.then_inc(at["a", "flip"], 1)

        def out_proj(layer, n0):
            pe.wait_ge(at["ab"[layer], "o"], UNITS)
            for s in range(4):
                arrived(n0 + s)
            for t in range(NT):
                for s in range(4):
                    i = 4 * t + s
                    if i >= 4 or layer:
                        pe.wait_ge(hid_attn, 4 * NT * layer + i - 3)
                    rows_mm(4 + i % 4, t, n0 + s).then_inc(o_mm, 1)

        out_proj(0, 6)

        def moe(layer):
            norm(1 + 2 * layer)
            s = ov[layer]
            pe.wait_ge(router_packed, 1)
            pe.wait_ge(hid_attn, 4 * NT * (layer + 1))
            for h in range(2):
                for k in range(KD):
                    ins = nc.tensor.matmul(ps[0:36, 4 + h, 0:HALF_N], wr_sb[:, layer, k, :],
                                           xT[:, k, HALF_N * h:HALF_N * h + HALF_N], start=k == 0, stop=k == KD - 1)
            ins.then_inc(r_mm, 1)
            pe.wait_ge(r_sb, layer + 1)
            for t in range(NT):
                r = ROWS[t]
                ins = nc.tensor.transpose(ps[:r, 6, 36 * t:36 * t + 36], rT[0:36, COL[t]:COL[t] + r], ident[0:36, 0:36])
            ins.then_inc(r_flip, 1)
            pe.wait_ge(r_key, layer + 1)
            for t in range(NT):
                r = ROWS[t]
                b, c = (5, COL[t]) if t < 4 else (4, 0)
                nc.tensor.transpose(ps[0:NE, b, c:c + r], key[:r, t, :], ident[:r, :r])
            for t in range(NT):
                r = ROWS[t]
                ins = nc.tensor.matmul(ps[0:1, 7, 0:NE], ones[:r, 0:1], rt[4][:r, t, :], start=t == 0, stop=t == NT - 1)
            ins.then_inc(r_kflip, 1)
            pe.wait_ge(r_top, layer + 1)
            nc.tensor.transpose(ps[:, 6, 0:NE], topk[0:NE, :], ident[0:NE, 0:NE]).then_inc(r_tflip, 1)

            base = MOE_STREAM0[layer]

            def x_transpose(e, b, seen):
                pe.wait_ge(gath[b], seen)
                if not isinstance(e, int) or e >= 2 or layer:
                    wait_apart(pe, x_sb, NE * layer + e - 1)
                x = xg[b][0:CAP, :].rearrange("p (c k) -> p k c", k=KD)
                for k in range(KD):
                    ins = nc.tensor.transpose(ps[:, 2 + b, k * CAP:k * CAP + CAP], x[:, k, :], ident[0:CAP, 0:CAP])
                ins.then_inc(x_flip, 1)

            def gate_up(e, b, turn):
                pe.wait_ge(x_sb, NE * layer + e + 1)
                n = base + 3 * b
                for j in range(2):
                    pe.wait_ge(w_ready[slot(n + j)], 16 * ((n + j) // RING + 1 + turn))
                if not isinstance(e, int) or e >= 2 or layer:
                    pe.wait_ge(h_sb, NE * layer + e - 1)
                expert_gu(xts[b], ring_k(n), ring_k(n + 1), b).then_inc(gu_mm, 1)

            def expert_gu(x, wg, wu, bank):
                for k in range(KD):
                    nc.tensor.matmul(ps[0:CAP, bank, 0:F], x[:, k, :], wg[:, k, :], start=k == 0, stop=k == KD - 1)
                    ins = nc.tensor.matmul(ps[CAP:P, bank, 0:F], x[:, k, :], wu[:, k, :], start=k == 0, stop=k == KD - 1)
                return ins

            def expert_ht(h, bank):
                for c in range(2):
                    ins = nc.tensor.transpose(ps[:, bank, c * CAP:c * CAP + CAP], h[CAP:P, c * P:c * P + P],
                                              ident[CAP:P, CAP:P])
                return ins

            def expert_down(ht, wd, bank):
                for c in range(2):
                    nc.tensor.matmul(ps[0:CAP, bank, :], ht[:, c, :], wd[:, c, 0:OUT_HALF], start=c == 0, stop=c == 1)
                    ins = nc.tensor.matmul(ps[CAP:P, bank, :], ht[:, c, :], wd[:, c, OUT_HALF:D], start=c == 0, stop=c == 1)
                return ins

            def h_transpose(e, b):
                pe.wait_ge(h_sb, NE * layer + e + 1)
                if not isinstance(e, int) or e >= 2 or layer:
                    wait_apart(pe, ht_sb, NE * layer + e - 1)
                expert_ht(hmul[b], 4 + b).then_inc(h_flip, 1)

            def down(e, b, turn):
                pe.wait_ge(ht_sb, NE * layer + e + 1)
                n = base + 3 * b + 2
                pe.wait_ge(w_ready[slot(n)], 16 * (n // RING + 1 + turn))
                if not isinstance(e, int) or e >= 2 or layer:
                    pe.wait_ge(ye_sb, NE * layer + e - 1)
                expert_down(hts[b], ring[:, slot(n), :].rearrange("p (c d) -> p c d", d=D), 6 + b).then_inc(d_mm, 1)

            half = NE // 2 * layer
            pe.wait_ge(r_idx, layer + 1)
            x_transpose(0, 0, 16 * (half + 1))
            gate_up(0, 0, 0)
            x_transpose(1, 1, 16 * (half + 1))
            h_transpose(0, 0)
            gate_up(1, 1, 0)
            x_transpose(2, 0, 16 * (half + 2))
            down(0, 0, 0)
            h_transpose(1, 1)
            with pe.Fori(1, NE // 2 - 1) as i:
                gate_up(2 * i, 0, i)
                x_transpose(2 * i + 1, 1, 16 * (half + 1 + i))
                down(2 * i - 1, 1, i - 1)
                h_transpose(2 * i, 0)
                gate_up(2 * i + 1, 1, i)
                x_transpose(2 * i + 2, 0, 16 * (half + 2 + i))
                down(2 * i, 0, i)
                h_transpose(2 * i + 1, 1)
            last = NE // 2 - 1
            gate_up(NE - 2, 0, last)
            x_transpose(NE - 1, 1, 16 * (half + 1 + last))
            down(NE - 3, 1, last - 1)
            h_transpose(NE - 2, 0)
            gate_up(NE - 1, 1, last)
            down(NE - 2, 0, last)
            h_transpose(NE - 1, 1)
            down(NE - 1, 1, last)
            pe.wait_ge(s["count"], 1)
            pe.wait_ge(ye_sb, NE * (layer + 1))
            extra = pe.value_load(ov_i[0:1, layer:layer + 1], min_val=0, max_val=MAX_EXTRA)
            with pe.If(extra > 0):
                with pe.Fori(0, extra) as o:
                    wait_apart(pe, s["pick"], o + 1)
                    nc.tensor.matmul(ps[0:NE, 7, 0:1], ovs[0:1, 64:96], ident[0:1, 0:1], start=True, stop=True) \
                        .then_inc(s["mask"], 1)
                    pe.wait_ge(s["list"], o + 1)
                    nc.tensor.matmul(ps[:, 7, 8:9], topk[0:NE, :], ovs[0:NE, 96:97], start=True, stop=True) \
                        .then_inc(s["irow"], 1)
                    wait_apart(pe, s["gath"], 16 * (o + 1))
                    x = xg[0][0:CAP, :].rearrange("p (c k) -> p k c", k=KD)
                    for k in range(KD):
                        ins = nc.tensor.transpose(ps[:, 2, k * CAP:k * CAP + CAP], x[:, k, :], ident[0:CAP, 0:CAP])
                    ins.then_inc(s["xf"], 1)
                    pe.wait_ge(s["xs"], o + 1)
                    pe.wait_ge(s["w"], 48 * (o + 1))
                    wv = ovw[:, :, :].rearrange("p j (k f) -> p j k f", f=F)
                    expert_gu(xts[0], wv[:, 0], wv[:, 1], 0).then_inc(s["gu"], 1)
                    wait_apart(pe, s["h"], o + 1)
                    expert_ht(hmul[0], 4).then_inc(s["hf"], 1)
                    pe.wait_ge(s["ht"], o + 1)
                    expert_down(hts[0], ovw[:, 2, :].rearrange("p (c d) -> p c d", d=D), 6).then_inc(s["d"], 1)

        moe(0)
        norm(2)
        q_proj(1, B_STREAM0)
        pe.wait_ge(cache_b_in, 64)
        for i in range(4):
            tile, quad = divmod(i, 2)
            if i >= 2:
                pe.wait_ge(k_sb, 6 + i - 1)
            for h in range(4):
                c = (4 * quad + h) * P
                ins = nc.tensor.transpose(ps[:, 6 + i % 2, h * P:h * P + P], kcb[:, tile, c:c + P], ident)
            ins.then_inc(k_flip, 1)
        for i in range(8 * NT + 1):
            sl, t = divmod(i, NT)
            if i < 8 * NT:
                if t == 0:
                    arrived(B_STREAM0 + 4 + sl)
                if i >= 2:
                    pe.wait_ge(kv_sb, 2 * NT + i - 1)
                rows_mm(4 + i % 2, t, B_STREAM0 + 4 + sl).then_inc(kv_mm, 1)
            b = i - 1
            if 0 <= b < 4 * NT:
                sl, t = divmod(b, NT)
                r = ROWS[t]
                pe.wait_ge(kv_sb, 2 * NT + b + 1)
                pe.wait_ge(k_sb, 10 + b - 1)
                for h in range(2):
                    ins = nc.tensor.transpose(ps[:, 6 + b % 2, h * P:h * P + r], kbt[:r, t, (2 * sl + h) * P:(2 * sl + h) * P + P],
                                              ident[:r, :r])
                ins.then_inc(k_flip, 1)
        pe.wait_ge(q_act, 16)
        pe.wait_ge(q_dve, 16)
        pe.wait_ge(k_sb, 10 + 4 * NT)
        pe.wait_ge(kv_sb, 10 * NT)
        for step in range(UNITS + 5):
            if step < UNITS:
                u = step
                t, hp, kc, nk, tc, vt = b_unit(u)
                r = ROWS[t]
                if u >= 1:
                    pe.wait_ge(at["b", "biased"], u)
                for g in range(4):
                    lo = HD * (g % 2)
                    ins = nc.tensor.matmul(ps[:r, g, 0:nk], qT[lo:lo + HD, 2 * hp + g // 2, COL[t]:COL[t] + r],
                                           kTb[lo:lo + HD, 2 * hp + g // 2, kc:kc + nk], start=True, stop=True)
                ins.then_inc(at["b", "scores"], 1)
            u = step - 3
            if 0 <= u < UNITS:
                t, hp, kc, nk, tc, vt = b_unit(u)
                r = ROWS[t]
                pe.wait_ge(at["b", "pt"], u + 1)
                pe.wait_ge(ptd["b"], u + 1)
                if u >= 2:
                    pe.wait_ge(at["b", "on"], u - 1)
                    pe.wait_ge(at["b", "sq"], u - 1)
                    pe.wait_ge(at["b", "o"], u - 1)
                for hh in range(2):
                    for kb, (v, kr) in enumerate(vt):
                        ins = nc.tensor.matmul(ps[:r, 6 + u % 2, hh * P:hh * P + P], PT_B[:kr, hh, kb, 0:r],
                                               vb[:kr, v, (2 * hp + hh) * P:(2 * hp + hh) * P + P],
                                               start=kb == 0, stop=kb == len(vt) - 1)
                ins.then_inc(at["b", "pv"], 1)
            u = step - 2
            if 0 <= u < UNITS:
                t, hp, kc, nk, tc, vt = b_unit(u)
                r = ROWS[t]
                pe.wait_ge(at["b", "probs"], u + 1)
                if u >= 1:
                    pe.wait_ge(at["b", "pt"], u)
                    pe.wait_ge(ptd["b"], u)
                for hh in range(2):
                    for kb, (v, kr) in enumerate(vt):
                        ins = nc.tensor.transpose(ps[:kr, 4 + hh, kb * P:kb * P + r],
                                                  E_B[u % 3][:r, 2 * hh, kb * P:kb * P + kr], ident[:r, :r])
                ins.then_inc(at["b", "flip"], 1)
            u = step - 4
            if 0 <= u < UNITS:
                t, hp = b_unit(u)[:2]
                r = ROWS[t]
                pe.wait_ge(at["b", "on"], u + 1)
                for hh in range(2):
                    ins = nc.tensor.transpose(ps[:, 6 + u % 2, (2 + hh) * P:(2 + hh) * P + r], ON[u % 2][:r, hh, :],
                                              ident[:r, :r])
                ins.then_inc(at["b", "onflip"], 1)
        out_proj(1, B_STREAM0 + 12)
        moe(1)


_INS = ["x_prompt", "x_sample", "cache_a_k", "cache_a_v", "cache_b_k", "cache_b_v", "norm_mix", "norm_ffn", "norm_final",
        "w_a_qkv", "b_a_qkv", "a_sinks", "w_a_o", "w_b_qkv", "b_lambda", "b_subln", "w_b_o", "w_route_group",
        "b_route_group", "w_route_expert", "b_route_expert", "w_gate", "w_up", "w_down"]
_OUTS = [(1, SEQ, D), (1, DEC, D), (1, 1, WINDOW, A_KV, HD), (1, 1, WINDOW, A_KV, HD), (1, 1, WINDOW, A_KV, HD),
         (1, 1, WINDOW, A_KV, HD), (1, 1, SEQ, B_HEADS, BHD), (1, 1, SEQ, B_HEADS, BHD), (1, 1, DEC, B_HEADS, BHD),
         (1, 1, DEC, B_HEADS, BHD)]


def kernel(**inputs):
    import concourse.bacc as bacc
    from concourse.bass_utils import run_bass_kernel_spmd

    nc = bacc.Bacc("TRN2", target_bir_lowering=False, num_devices=1)
    arrays, I = {}, {}
    const, dist_a, dist_b = shape_constants()
    given = {name: np.ascontiguousarray(inputs[name]) for name in _INS}
    given.update(const=const, dist_a=dist_a, dist_b=dist_b)
    for name, a in given.items():
        arrays[f"in_{name}"] = a
        I[name] = nc.dram_tensor(f"in_{name}", a.shape, mybir.dt.from_np(a.dtype), kind="ExternalInput").ap()
    O = [nc.dram_tensor(f"out_{i}", list(s), F32, kind="ExternalOutput").ap() for i, s in enumerate(_OUTS)]
    build(nc, I, O)
    r = run_bass_kernel_spmd(nc, [arrays], core_ids=[0])
    return tuple(r.results[0][f"out_{i}"] for i in range(len(_OUTS)))
```

```python
from contextlib import ExitStack

import numpy as np

import concourse.bass as bass
from concourse import mybir

F32 = mybir.dt.float32
I32 = mybir.dt.int32
U32 = mybir.dt.uint32
ALU = mybir.AluOpType
ACT = mybir.ActivationFunctionType
AX = mybir.AxisListType.X

D = 1024
SEQ, DEC, PAST = 512, 32, 256
CHUNK, WINDOW = 64, 128
N = SEQ + DEC
P = 128
KD = D // P
NT = 5
ROWS = [P, P, P, P, DEC]
COL = [P * t for t in range(NT)]
HALF_N = N // 2
assert DEC == 32
O_ITEMS = 17
KV_ITEMS = 17

A_HEADS, A_KV, HD = 16, 4, 64
A_GROUP = A_HEADS // A_KV
AQ, AKV = A_HEADS * HD, A_KV * HD
B_HEADS, BHD = 8, 128
SCALE = HD ** -0.5
LAM_INIT = 0.8 - 0.6 * float(np.exp(-0.3))
EPS, SUB_EPS = 1e-6, 1e-5
MASKED = 1e32
BIG = 1e30

G, EPG, F = 4, 8, 256
NE = G * EPG
CAP = 64
MAX_EXTRA = 17
KEY0 = 2048
OUT_HALF = D // 2

RING, SLOT = 6, 2048
A_STREAM0, A_SLOTS = 0, (AQ + 2 * AKV) // F + D // F
B_SLOTS = 3 * D // F + D // F
DEEP = 4
MOE_STREAMS = RING * NE // DEEP
B_STREAM0 = A_SLOTS + MOE_STREAMS
MOE_STREAM0 = [A_SLOTS, B_STREAM0 + B_SLOTS]

C_ID, C_REV, C_K1, C_K2, C_HALF, C_THR, C_IOTA, C_END = 0, 128, 160, 165, 170, 171, 179, 211


def a_slopes():
    return [float(np.float32(2.0 ** (-8.0 * (h + 1) / A_HEADS))) for h in range(A_HEADS)]


def b_slopes():
    return [float(np.float32(2.0 ** (-8.0 * (h + 1) / B_HEADS))) for h in range(B_HEADS)]


def shape_constants():
    c = np.zeros((P, C_END), np.float32)
    c[:, C_ID:C_ID + P] = np.eye(P)
    c[:, C_REV:C_REV + NE] = NE - np.arange(NE)
    tok = np.arange(NT)[None, :] * P + np.arange(P)[:, None]
    c[:, C_K1:C_K1 + NT] = KEY0 - 2 * tok
    c[:, C_K2:C_K2 + NT] = KEY0 - 2 * tok - 1
    c[:, C_HALF] = np.arange(P) // CAP
    c[:, C_THR:C_THR + 8] = CAP * np.arange(1, 9)
    c[:, C_IOTA:C_IOTA + NE] = np.arange(NE)
    q = np.arange(P)[:, None]
    ka = np.arange(2 * P)[None, :]
    da = np.abs(q - (ka - P)).astype(np.float32)
    seen = (ka // CHUNK >= q // CHUNK) & (ka // CHUNK <= q // CHUNK + WINDOW // CHUNK)
    da = np.where(seen, da, np.float32(MASKED))
    kb = np.arange(4 * P)[None, :]
    db = np.abs(q + 3 * P - kb).astype(np.float32)
    seen = (kb - 3 * P) // CHUNK <= q // CHUNK
    db = np.where(seen, db, np.float32(MASKED))
    return c, da.astype(np.float32), db.astype(np.float32)


class Link:

    def __init__(self, sem):
        self.sem, self.n = sem, 0

    def __call__(self, eng, instruction):
        self.n += 1
        instruction.then_inc(self.sem, 1)
        eng.wait_ge(self.sem, self.n)


def build(nc, I, O):
    ctx = ExitStack()
    with ctx:
        program(nc, ctx, I, O)


def program(nc, ctx, I, O):
    def sb(name, shape, dt=F32):
        return ctx.enter_context(nc.sbuf_tensor(name, shape, dt))

    def sem(name):
        return ctx.enter_context(nc.semaphore(name))

    hn_dram = nc.dram_tensor("hn_scratch", [N, D], F32).ap()
    y2_dram = nc.dram_tensor("y2_scratch", [4 * N, OUT_HALF], F32).ap()

    ring = sb("ring", [P, RING, SLOT])
    hid = sb("hid", [P, NT, D])
    xT = sb("xT", [P, KD, N])
    oT = xT
    cst = sb("cst", [P, C_END])
    ident = cst[:, C_ID:C_ID + P]
    small = sb("small", [P, 160])
    wr_sb = sb("wr", [P, 2, KD, 36])
    AREA = 29696
    area = sb("area", [P, AREA])

    def part(at, *shape):
        n = int(np.prod(shape))
        v = area[:, at:at + n]
        if len(shape) == 2:
            v = v.rearrange("p (a b) -> p a b", b=shape[1])
        if len(shape) == 3:
            v = v.rearrange("p (a b c) -> p a b c", b=shape[1], c=shape[2])
        return v

    qT = part(0, KD, N)
    R_K = KD * N
    kTa = part(R_K, A_KV, SEQ + WINDOW + DEC)
    kTb = part(R_K, B_HEADS, SEQ + PAST + DEC)
    R_V = R_K + B_HEADS * (SEQ + PAST + DEC)
    va = part(R_V, 6, AKV)
    vb = part(R_V, 7, D)
    R_TAB = R_V + 7 * D
    tabA = part(R_TAB, A_HEADS, 2 * P)
    tabB = part(R_TAB, B_HEADS, 4 * P)
    R_W = R_TAB + 4096
    dist_a = part(R_W, 2 * P)
    dist_b = part(R_W + 5632, 4 * P)
    kst = part(R_W + 512, 6, A_KV * 2 * HD)
    kca = part(R_W + 512 + 3072, AKV)
    kbt = part(R_W, NT, D)
    kcb = part(R_V, 2, D)
    E_A = [part(R_W + 1024 * i, 4, 2 * P) for i in range(3)]
    PT_A = [part(R_W + 3072 + 1024 * i, 4, 2, P) for i in range(2)]
    E_B = [part(R_W + 2048 * i, 4, 4 * P) for i in range(3)]
    PT_B = part(R_W + 6144, 2, 4, P)
    ON = [part(R_W + 7168 + 256 * i, 2, P) for i in range(2)]
    R_N = R_W + 1024
    gbc = part(R_N, D)
    ynorm = [part(R_N + D * (1 + i), D) for i in range(2)]
    junk = part(R_N + 3 * D, D)
    xg = [part(1024 * i, D) for i in range(DEEP)]
    M1 = DEEP * D
    xts = [part(M1 + 512 * i, KD, CAP) for i in range(2)]
    sil = [part(M1 + 1024 + 256 * i, F) for i in range(2)]
    hmul = [part(M1 + 1536 + 256 * i, F) for i in range(2)]
    hts = [part(M1 + 2048 + 128 * i, 2, CAP) for i in range(2)]
    yout = [part(M1 + 2304 + 512 * i, OUT_HALF) for i in range(2)]
    M0 = M1 + 3328
    R_X = M0 + 3248
    extra_slots = part(R_X, RING, SLOT)
    assert R_X + RING * SLOT <= R_N
    ovw = part(R_X, 3, SLOT)
    y2b = [part(R_X + 3 * SLOT + 2 * D * i, 2, D) for i in range(2)]
    rT = part(M0, N)
    lg = part(M0 + 544, NT, 36)
    keytab = part(M0 + 736, N)
    topk = part(M0 + 1280, P)
    key = part(M0 + 1408, NT, NE)
    rt = [part(M0 + 1568 + 160 * i, NT, NE) for i in range(5)]
    rs = part(M0 + 2368, 24, 8)
    gw = part(M0 + 2560, 2, 8)
    keytmp = part(M0 + 2576, N)
    ovs = part(M0 + 3120, 128)
    idx_i = sb("idx_i", [P, 3, NE], I32)
    cur_i = sb("cur_i", [P, DEEP + 2], I32)
    ov_i = sb("ov_i", [P, 8], I32)
    ov_u = sb("ov_u", [1, 8], U32)
    ss, rstd, pbase = small[:, 0:8], small[:, 8:16], small[:, 16:24]
    neghalf = small[:, 24:28]
    bq = small[:, 28:36]
    sink8 = small[:, 36:52]
    brT = small[:, 52:54]
    lam4 = small[:, 54:58]
    neglam = small[:, 58:59]
    st = [small[:, 60 + 32 * i:92 + 32 * i] for i in range(3)]
    bkv = sb("bkv", [P, 2 * AKV])
    subg = bkv[:, 0:BHD]
    lamb = bkv[:, 128:384].rearrange("p (a b) -> p a b", b=HD)

    ps = ctx.enter_context(nc.psum_tensor("ps", [P, 8, 512], F32))

    w_ready = [sem(f"w_ready{i}") for i in range(RING)]
    x_ready = [sem(f"x_ready{i}") for i in range(RING)]
    const_in = sem("const_in")
    passed = sem("passed")
    x_in = [sem(f"x_in{i}") for i in range(2)]
    bias_in = sem("bias_in")
    cache_a_in, cache_b_in, lam_in, dist_b_in = sem("cache_a_in"), sem("cache_b_in"), sem("lam_in"), sem("dist_b_in")
    router_in = sem("router_in")
    router_packed = sem("router_packed")
    g_in = sem("g_in")
    sumsq, rstd_ready, y_ready, y_flip, xt_act, xt_dve = (
        sem("sumsq"), sem("rstd_ready"), sem("y_ready"), sem("y_flip"), sem("xt_act"), sem("xt_dve"))
    y_out = [sem(f"y_out{i}") for i in range(2)]
    hid_attn = sem("hid_attn")
    hid_moe = [sem(f"hid_moe{l}") for l in range(2)]
    k_out, v_out = sem("k_out"), sem("v_out")
    pool_own, dve_own, act_own = sem("pool_own"), sem("dve_own"), sem("act_own")
    q_mm, q_act, q_dve = sem("q_mm"), sem("q_act"), sem("q_dve")
    kv_mm, kv_sb, k_flip, k_sb = sem("kv_mm"), sem("kv_sb"), sem("k_flip"), sem("k_sb")
    cachek_sb = sem("cachek_sb")
    tab_ready = sem("tab_ready")
    at = {}
    for layer in "ab":
        for name in ("scores", "biased", "exp", "recip", "probs", "flip", "pt", "pv", "o", "scaled",
                     "sq", "rms", "on", "onflip"):
            if layer == "b" or name not in ("scaled", "sq", "rms", "on", "onflip"):
                at[layer, name] = sem(f"{layer}_{name}")
    ptd = {c: sem(f"{c}_pt_dve") for c in "ab"}
    o_mm = sem("o_mm")
    r_mm, r_sb, r_flip, r_exp, r_key, r_kflip, r_top, r_idx = (
        sem("r_mm"), sem("r_sb"), sem("r_flip"), sem("r_exp"), sem("r_key"), sem("r_kflip"), sem("r_top"), sem("r_idx"))
    r_d = sem("r_d")
    r_tflip = sem("r_tflip")
    lam_sum = sem("lam_sum")
    ones = cst[:, C_REV + NE - 1:C_REV + NE]
    zeroed, ix_cur = sem("zeroed"), sem("ix_cur")
    ix_s = sem("ix_s")
    gath = [sem(f"gath{i}") for i in range(DEEP)]
    scat = [sem(f"scat{i}") for i in range(2)]
    x_flip, x_sb, gu_mm, silu, h_sb, h_flip, ht_sb, d_mm, ye_sb = (
        sem("x_flip"), sem("x_sb"), sem("gu_mm"), sem("silu"), sem("h_sb"), sem("h_flip"), sem("ht_sb"),
        sem("d_mm"), sem("ye_sb"))
    ov = [{k: sem(f"ov{k}{l}") for k in ("count", "own", "pick", "mask", "list", "idx", "w", "gath", "xf", "xs", "gu",
                                         "silu", "h", "hf", "ht", "d", "y", "scat", "irow")} for l in range(2)]
    y2_in = [sem(f"y2_in{i}") for i in range(2)]

    def wait_apart(eng, s, value):
        eng.wait_ge(s, value)
        eng.sem_inc(passed, 1)

    def slot(n):
        return n % RING

    def landed(n):
        return 16 * (n // RING + 1)

    def expert_slot(layer, u, j, turn):
        if u < DEEP // 2:
            n = MOE_STREAM0[layer] + 3 * u + j
            return ring[:, slot(n), :], w_ready[slot(n)], 16 * (n // RING + 1 + turn)
        n = 3 * (u - DEEP // 2) + j
        return extra_slots[:, n, :], x_ready[n], 16 * (NE // DEEP * layer + 1 + turn)

    def slot_left(n):
        layer, i = (0, n) if n < A_SLOTS else (1, n - B_STREAM0)
        if i < 4:
            return q_mm, 8 * layer + 2 * i + 2
        if layer == 0 and i < 6:
            return kv_mm, NT * (i - 3)
        if layer and i < 12:
            return kv_mm, 2 * NT + KV_ITEMS * (1 + (i - 4) // 4)
        return o_mm, O_ITEMS * (layer + 1)

    def kv_item(i):
        q, j = divmod(i, KV_ITEMS)
        return (4 * q + j // 4, j % 4) if j < 16 else (4 * q, None)

    def o_item(layer, step):
        i = step - (7, 8)[layer]
        return i if 0 <= i < O_ITEMS - 1 else None

    def a_unit(u):
        t, j = divmod(u, A_KV)
        if t == 0:
            return t, j, 0, P, P, [(0, P)]
        if t < 4:
            return t, j, (t - 1) * P, 2 * P, 0, [(t - 1, P), (t, P)]
        return t, j, SEQ, WINDOW + DEC, 0, [(4, P), (5, DEC)]

    def b_unit(u):
        t, hp = divmod(u, B_HEADS // 2)
        if t < 4:
            return t, hp, 0, P * (t + 1), (3 - t) * P, [(i, P) for i in range(t + 1)]
        return t, hp, SEQ, PAST + DEC, P, [(4, P), (5, P), (6, DEC)]

    UNITS = NT * 4

    def blk(kb, total):
        return min(P, total - kb * P)

    block = ctx.enter_context(nc.Block())

    @block.sync
    def _(sp):
        def load(n, src):
            sp.dma_start(ring[:, slot(n), :].rearrange("p (k f) -> p k f", f=src.shape[-1]), src) \
              .then_inc(w_ready[slot(n)], 16)

        def rows8(w, lo, hi):
            return w[:, lo:hi].rearrange("(p k) f -> p k f", k=KD)

        def rows128(w, lo, hi):
            return w[:, lo:hi].rearrange("(k p) f -> p k f", p=P)

        wa, wao = I["w_a_qkv"][0], I["w_a_o"][0]
        wb, wbo = I["w_b_qkv"][0], I["w_b_o"][0]
        a_src = [rows8(wa, F * i, F * i + F) for i in range(6)] + [rows128(wao, F * i, F * i + F) for i in range(4)]
        b_src = [rows8(wb, F * i, F * i + F) for i in range(12)] + [rows128(wbo, F * i, F * i + F) for i in range(4)]

        gate = [I["w_gate"][l].rearrange("g e (p k) f -> (g e) p k f", k=KD) for l in range(2)]
        up = [I["w_up"][l].rearrange("g e (p k) f -> (g e) p k f", k=KD) for l in range(2)]
        down = [I["w_down"][l].rearrange("g e (c p) d -> (g e) p c d", p=P) for l in range(2)]

        def expert_loads(layer, turn, u):
            e = DEEP * turn + u
            for j, w in enumerate((gate, up, down)):
                if not isinstance(turn, int):
                    sp.wait_ge(d_mm if j == 2 else gu_mm, NE * layer + e - DEEP + 1)
                elif u < DEEP // 2:
                    sp.wait_ge(*slot_left(MOE_STREAM0[layer] + 3 * u + j - RING))
                else:
                    sp.wait_ge(at["ab"[layer], "o"], UNITS)
                    if layer:
                        sp.wait_ge(v_out, 16 * NT)
                src = w[layer][e] if isinstance(e, int) else w[layer][bass.ds(e, 1)].rearrange("o p k f -> p (o k) f")
                dst, landed_sem, _ = expert_slot(layer, u, j, 0)
                sp.dma_start(dst.rearrange("p (k f) -> p k f", f=src.shape[-1]), src).then_inc(landed_sem, 16)

        def moe_loads(layer):
            for u in range(DEEP):
                expert_loads(layer, 0, u)
            with sp.Fori(1, NE // DEEP) as i:
                for u in range(DEEP):
                    expert_loads(layer, i, u)
            s = ov[layer]
            sp.wait_ge(s["count"], 1)
            extra = sp.value_load(ov_i[0:1, layer:layer + 1], min_val=0, max_val=MAX_EXTRA)
            with sp.If(extra > 0):
                with sp.Fori(0, extra) as o:
                    wait_apart(sp, s["pick"], o + 1)
                    e = sp.value_load(ov_u[0:1, 0:1], min_val=0, max_val=NE - 1)
                    for j, w in enumerate((gate, up, down)):
                        src = w[layer][bass.ds(e, 1)].rearrange("o p k f -> p (o k) f")
                        sp.dma_start(ovw[:, j, :].rearrange("p (k f) -> p k f", f=src.shape[-1]), src) \
                          .then_inc(s["w"], 16)

        for n in range(A_SLOTS):
            if n >= RING:
                sp.wait_ge(*slot_left(n - RING))
            load(n, a_src[n])
        moe_loads(0)
        for i in range(B_SLOTS):
            n = B_STREAM0 + i
            if i < RING:
                sp.wait_ge(d_mm if i % 3 == 2 else gu_mm, NE - DEEP + 1 + i // 3)
            else:
                sp.wait_ge(*slot_left(n - RING))
            load(n, b_src[i])
        moe_loads(1)

    @block.gpsimd
    def _(pool):
        own = Link(pool_own)

        def bcast(dst, src, s):
            pool.dma_start(dst, src).then_inc(s, 16)

        def norm_small(n, rows=None):
            for t in range(NT):
                r = ROWS[t]
                pool.wait_ge(sumsq, NT * n + t + 1)
                own(pool, nc.gpsimd.tensor_scalar(pbase[:r, t:t + 1], ss[:r, t:t + 1], 1.0 / D, EPS, ALU.mult, ALU.add))
                nc.gpsimd.tensor_tensor(rstd[:r, t:t + 1], pbase[:r, t:t + 1], neghalf[:r, 0:1], ALU.pow) \
                    .then_inc(rstd_ready, 1)
                if rows and t > 0:
                    rows(t - 1)
            if rows:
                rows(NT - 1)

        def rows_out(n):
            def rows(t):
                r = ROWS[t]
                pool.wait_ge(y_ready, NT * n + t + 1)
                if n == 4:
                    dst = O[0][0, COL[t]:COL[t] + P, :] if t < 4 else O[1][0]
                else:
                    dst = hn_dram[COL[t]:COL[t] + r, :]
                pool.dma_start(dst, ynorm[t % 2][:r, :]).then_inc(y_out[t % 2], 16)
            norm_small(n, rows)

        def g_load(w, after=None):
            if after is not None:
                pool.wait_ge(*after)
            pool.dma_start(gbc, w.rearrange("(o d) -> o d", o=1).broadcast_to([P, D])).then_inc(g_in, 16)

        pool.dma_start(cst[:, :], I["const"]).then_inc(const_in, 16)
        g_load(I["norm_mix"][0])
        own(pool, nc.gpsimd.memset(neghalf, -0.5))
        pool.dma_start(bq, I["b_a_qkv"][0, 0:AQ].rearrange("(m p) -> p m", p=P),
                       allow_slow_non_contiguous=True).then_inc(bias_in, 16)
        pool.dma_start(bkv[:, :], I["b_a_qkv"][0:1, AQ:AQ + 2 * AKV].broadcast_to([P, 2 * AKV])).then_inc(bias_in, 16)
        pool.dma_start(st[0][:, 0:16], I["a_sinks"][0:1, :].broadcast_to([P, A_HEADS])).then_inc(bias_in, 16)
        norm_small(0)
        pool.wait_ge(xt_act, NT)
        pool.wait_ge(xt_dve, NT)
        pool.wait_ge(y_flip, NT)
        pool.dma_start(dist_a, I["dist_a"]).then_inc(cache_a_in, 16)
        pool.dma_start(kca, I["cache_a_k"][0, 0].rearrange("s h d -> s (h d)")).then_inc(cache_a_in, 16)
        pool.dma_start(va[:, 4, :], I["cache_a_v"][0, 0].rearrange("s h d -> s (h d)")).then_inc(cache_a_in, 16)
        stage_g, stage_e = part(R_K + 2688, 2, KD, G), part(R_K + 2688 + 64, 2, KD, NE)
        for l in range(2):
            pool.dma_start(stage_g[:, l], I["w_route_group"][l].rearrange("(p k) g -> p k g", k=KD)).then_inc(router_in, 16)
            pool.dma_start(stage_e[:, l], I["w_route_expert"][l].rearrange("(p k) g -> p k g", k=KD)).then_inc(router_in, 16)
            pool.dma_start(brT[0:G, l:l + 1], I["b_route_group"][l].rearrange("(g o) -> g o", o=1),
                           allow_slow_non_contiguous=True).then_inc(router_in, 16)
            pool.dma_start(brT[G:G + NE, l:l + 1], I["b_route_expert"][l].rearrange("(g o) -> g o", o=1),
                           allow_slow_non_contiguous=True).then_inc(router_in, 16)
        pool.wait_ge(cache_a_in, 48)
        for h, slope in enumerate(a_slopes()):
            ins = nc.gpsimd.tensor_scalar(tabA[:, h, :], dist_a, -slope / SCALE, 1.0, ALU.mult, ALU.mult)
        ins.then_inc(tab_ready, 1)
        pool.wait_ge(router_in, 128)
        for l in range(2):
            nc.gpsimd.tensor_copy(wr_sb[:, l, :, 0:G], stage_g[:, l])
            ins = nc.gpsimd.tensor_copy(wr_sb[:, l, :, G:G + NE], stage_e[:, l])
        ins.then_inc(router_packed, 1)
        kview = [kst[:, i, :].rearrange("p (h c d) -> p h c d", c=2, d=HD)[:, :, 0, :] for i in range(6)]
        pool.wait_ge(kv_sb, NT)
        pool.wait_ge(cachek_sb, 1)
        pool.dma_start(O[2][0, 0], kview[3]).then_inc(k_out, 16)
        pool.dma_start(O[4][0, 0, 0:WINDOW - DEC], I["cache_a_k"][0, 0, DEC:WINDOW]).then_inc(k_out, 16)
        pool.dma_start(O[4][0, 0, WINDOW - DEC:WINDOW], kview[4][0:DEC]).then_inc(k_out, 16)
        pool.dma_start(O[5][0, 0, 0:WINDOW - DEC], I["cache_a_v"][0, 0, DEC:WINDOW]).then_inc(k_out, 16)
        pool.wait_ge(kv_sb, 2 * NT)
        pool.dma_start(O[3][0, 0].rearrange("s h d -> s (h d)"), va[:, 3, :]).then_inc(k_out, 16)
        pool.dma_start(O[5][0, 0, WINDOW - DEC:WINDOW].rearrange("s h d -> s (h d)"), va[0:DEC, 5, :]).then_inc(k_out, 16)
        for u in range(UNITS):
            t, j, kc, nk, tc, vt = a_unit(u)
            r = ROWS[t]
            pool.wait_ge(at["a", "recip"], u + 1)
            for g in range(4):
                ins = nc.gpsimd.tensor_scalar(E_A[u % 3][:r, g, 0:nk], E_A[u % 3][:r, g, 0:nk],
                                              st[u % 3][:r, 24 + g:25 + g], 1.0, ALU.mult, ALU.mult)
            ins.then_inc(at["a", "probs"], 1)

        def moe(layer):
            n = 1 + 2 * layer
            c0 = "ab"[layer]
            g_load(I["norm_ffn"][layer], (at[c0, "o"], UNITS))
            rows_out(n)
            for x in xg:
                ins = nc.gpsimd.memset(x, 0.0)
            own(pool, ins)
            for b in range(2):
                pool.wait_ge(y_out[b], 16 * (3, 2)[b] * (layer + 1))
            pool.wait_ge(r_idx, layer + 1)

            def gather(e, u):
                nc.gpsimd.tensor_copy(cur_i[:, u:u + 1], idx_i[:, 1, bass.ds(e, 1)]).then_inc(ix_cur, 1)
                wait_apart(pool, ix_cur, NE * layer + e + 1)
                nc.gpsimd.indirect_dma_start(xg[u][0:CAP, :], None, hn_dram,
                                             bass.IndirectOffsetOnAxis(ap=cur_i[0:CAP, u:u + 1], axis=0),
                                             bounds_check=N - 1, oob_is_err=False).then_inc(gath[u], 16)

            def scatter(e, b, before):
                if before is not None:
                    pool.wait_ge(scat[b], before)
                c = DEEP + b
                nc.gpsimd.tensor_copy(cur_i[:, c:c + 1], idx_i[:, 0, bass.ds(e, 1)]).then_inc(ix_s, 1)
                pool.wait_ge(ye_sb, NE * layer + e + 1)
                wait_apart(pool, ix_s, NE * layer + e + 1)
                nc.gpsimd.indirect_dma_start(y2_dram, bass.IndirectOffsetOnAxis(ap=cur_i[:, c:c + 1], axis=0),
                                             yout[b], None, bounds_check=4 * N - 1, oob_is_err=False) \
                    .then_inc(scat[b], 16)

            half = NE // 2 * layer

            def step(turn, u, last=False):
                e = DEEP * turn + u
                if not last:
                    pool.wait_ge(x_flip, NE * layer + e + 1)
                    gather(e + DEEP, u)
                before = half + DEEP // 2 * turn + u // 2
                first = isinstance(turn, int) and turn == 0 and u < 2
                scatter(e, u % 2, None if first else 16 * before)

            for u in range(DEEP):
                gather(u, u)
            for u in range(DEEP):
                step(0, u)
            with pool.Fori(1, NE // DEEP - 1) as i:
                for u in range(DEEP):
                    step(i, u)
            for u in range(DEEP):
                step(NE // DEEP - 1, u, last=True)
            s = ov[layer]
            for b in range(2):
                pool.wait_ge(scat[b], NE // 2 * (layer + 1) * 16)
            pool.wait_ge(s["count"], 1)
            extra = pool.value_load(ov_i[0:1, layer:layer + 1], min_val=0, max_val=MAX_EXTRA)
            with pool.If(extra > 0):
                with pool.Fori(0, extra) as o:
                    wait_apart(pool, s["idx"], o + 1)
                    nc.gpsimd.indirect_dma_start(xg[0][0:CAP, :], None, hn_dram,
                                                 bass.IndirectOffsetOnAxis(ap=ov_i[0:CAP, 4:5], axis=0),
                                                 bounds_check=N - 1, oob_is_err=False).then_inc(s["gath"], 16)
                    wait_apart(pool, s["y"], o + 1)
                    nc.gpsimd.indirect_dma_start(y2_dram,
                                                 bass.IndirectOffsetOnAxis(ap=ov_i[:, 5:6], axis=0),
                                                 yout[0], None, bounds_check=4 * N - 1, oob_is_err=False) \
                        .then_inc(s["scat"], 16)

        moe(0)
        g_load(I["norm_mix"][1], (hid_moe[0], NT))
        pool.dma_start(subg, I["b_subln"][0:1, :].broadcast_to([P, BHD])).then_inc(lam_in, 16)
        pool.dma_start(lamb, I["b_lambda"][0:1].rearrange("o a b -> o (a b)").broadcast_to([P, 4 * HD])
                       .rearrange("p (a b) -> p a b", b=HD)).then_inc(lam_in, 16)
        for i in range(2):
            pool.dma_start(kcb[:, i, :], I["cache_b_k"][0, 0, P * i:P * i + P].rearrange("s h d -> s (h d)")) \
                .then_inc(cache_b_in, 16)
            pool.dma_start(vb[:, 4 + i, :], I["cache_b_v"][0, 0, P * i:P * i + P].rearrange("s h d -> s (h d)")) \
                .then_inc(cache_b_in, 16)
        pool.dma_start(dist_b, I["dist_b"]).then_inc(dist_b_in, 16)
        norm_small(2)
        pool.wait_ge(dist_b_in, 16)
        for h, slope in enumerate(b_slopes()):
            ins = nc.gpsimd.tensor_scalar(tabB[:, h, :], dist_b, -slope / SCALE, 1.0, ALU.mult, ALU.mult)
        ins.then_inc(tab_ready, 1)
        pool.wait_ge(kv_sb, 2 * NT + KV_ITEMS)
        for t in range(NT):
            dst = O[6][0, 0, COL[t]:COL[t] + P] if t < 4 else O[8][0, 0]
            pool.dma_start(dst.rearrange("s h d -> s (h d)"), kbt[:ROWS[t], t, :]).then_inc(k_out, 16)
        pool.wait_ge(kv_sb, 2 * NT + 2 * KV_ITEMS)
        for t in range(NT):
            dst = O[7][0, 0, COL[t]:COL[t] + P] if t < 4 else O[9][0, 0]
            pool.dma_start(dst.rearrange("s h d -> s (h d)"), vb[:ROWS[t], t if t < 4 else 6, :]).then_inc(v_out, 16)

        def rms(u):
            t = b_unit(u)[0]
            r = ROWS[t]
            pool.wait_ge(at["b", "sq"], u + 1)
            sm = st[u % 3]
            own(pool, nc.gpsimd.tensor_scalar(sm[:r, 22:24], sm[:r, 20:22], 1.0 / BHD, SUB_EPS, ALU.mult, ALU.add))
            nc.gpsimd.tensor_tensor(sm[:r, 24:26], sm[:r, 22:24], neghalf[:r, 0:2], ALU.pow).then_inc(at["b", "rms"], 1)

        for s in range(UNITS + 4):
            if s < UNITS:
                t, hp, kc, nk, tc, vt = b_unit(s)
                r = ROWS[t]
                pool.wait_ge(at["b", "recip"], s + 1)
                for hh in range(2):
                    ins = nc.gpsimd.tensor_scalar(E_B[s % 3][:r, 2 * hh + 1, 0:nk], E_B[s % 3][:r, 2 * hh + 1, 0:nk],
                                                  st[s % 3][:r, 16 + hh:17 + hh], 1.0, ALU.mult, ALU.mult)
                ins.then_inc(at["b", "scaled"], 1)
            if 0 <= s - 2 < UNITS:
                rms(s - 2)
        moe(1)
        g_load(I["norm_final"], (hid_moe[1], NT))
        rows_out(4)
        pool.wait_ge(y_out[0], 16 * 9)
        pool.wait_ge(y_out[1], 16 * 6)
        pool.wait_ge(v_out, 16 * NT)
        pool.wait_ge(k_out, 16 * (6 + NT))

    @block.scalar
    def _(act):
        own = Link(act_own)

        def norm(n):
            for t in range(NT):
                r = ROWS[t]
                if n == 0:
                    act.wait_ge(x_in[t // 2 % 2], 16 if t < 4 else 32)
                elif n % 2:
                    act.wait_ge(hid_attn, 4 * NT * (n // 2) + 4 * t + 4)
                else:
                    act.wait_ge(hid_moe[n // 2 - 1], t + 1)
                if n in (1, 3) and t == 0:
                    act.wait_ge(at["ab"[n // 2], "o"], UNITS)
                if n or t:
                    act.wait_ge(sumsq, NT * n + t)
                nc.scalar.activation(junk[:r, :], hid[:r, t, :], ACT.Square, accum_out=ss[:r, t:t + 1]) \
                    .then_inc(sumsq, 1)
                if n < 4:
                    if t > 0:
                        xt_copy(n, t - 1)
            if n < 4:
                xt_copy(n, NT - 1)

        def xt_copy(n, t):
            r = ROWS[t]
            b = 2 * (t % 2)
            act.wait_ge(y_flip, NT * n + t + 1)
            nc.scalar.activation(xT[:, 0:4, COL[t]:COL[t] + r],
                                 ps[:, b, :].rearrange("p (k c) -> p k c", c=P)[:, :, 0:r], ACT.Copy).then_inc(xt_act, 1)

        act.dma_start(hid[:, 0:2, :], I["x_prompt"][0, 0:2 * P].rearrange("(t p) d -> p t d", p=P)).then_inc(x_in[0], 16)
        act.dma_start(hid[:, 2:4, :], I["x_prompt"][0, 2 * P:4 * P].rearrange("(t p) d -> p t d", p=P)).then_inc(x_in[1], 16)
        act.wait_ge(x_in[0], 16)
        act.dma_start(hid[0:DEC, 4, :], I["x_sample"][0]).then_inc(x_in[0], 16)
        norm(0)
        act.wait_ge(bias_in, 48)
        for m in range(8):
            act.wait_ge(q_mm, m + 1)
            nc.scalar.activation(qT[:, m, 0:HALF_N], ps[:, 2 * (m % 2), 0:HALF_N], ACT.Identity,
                                 bias=bq[:, m:m + 1]).then_inc(q_act, 1)
        for i in range(6):
            act.wait_ge(k_flip, i + 1)
            r = (P, P, P, P, DEC, P)[i]
            c = (0, P, 2 * P, 3 * P, SEQ + WINDOW, SEQ)[i]
            nc.scalar.activation(kTa[:, :, c:c + r], ps[:, 6 + i % 2, :].rearrange("p (h c) -> p h c", c=P)[:, :, 0:r],
                                 ACT.Copy).then_inc(k_sb, 1)

        def attention(layer, unit, E, step):
            nh = 4
            if step < UNITS:
                u = step
                t, j, kc, nk, tc, vt = unit(u)
                r = ROWS[t]
                sm = st[u % 3]
                act.wait_ge(at[layer, "biased"], u + 1)
                for g in range(nh):
                    ins = nc.scalar.activation(E[u % 3][:r, g, 0:nk], E[u % 3][:r, g, 0:nk], ACT.Exp,
                                               bias=sm[:r, 4 + g:5 + g], scale=SCALE, accum_out=sm[:r, 8 + g:9 + g])
                if layer == "a":
                    ins = nc.scalar.activation(sm[:r, 16:20], sm[:r, 12:16], ACT.Exp, scale=SCALE)
                ins.then_inc(at[layer, "exp"], 1)

        for step in range(UNITS + 2):
            attention("a", a_unit, E_A, step)
            u = step - 2
            if 0 <= u < UNITS:
                t, j, kc, nk, tc, vt = a_unit(u)
                r = ROWS[t]
                act.wait_ge(at["a", "flip"], u + 1)
                if u >= 2:
                    act.wait_ge(at["a", "pv"], u - 1)
                nc.scalar.activation(PT_A[u % 2][:, :, 0, 0:r],
                                     ps[:, 4, :].rearrange("p (g c) -> p g c", c=P)[:, :, 0:r],
                                     ACT.Copy).then_inc(at["a", "pt"], 1)

        def moe(layer):
            norm(1 + 2 * layer)
            act.wait_ge(r_exp, 2 * layer + 1)
            nc.scalar.activation(rt[0][:, :, 0:G], rt[0][:, :, 0:G], ACT.Exp).then_inc(r_d, 1)
            act.wait_ge(r_exp, 2 * layer + 2)
            nc.scalar.activation(rs[:, 5, 0:NT], rs[:, 4, 0:NT], ACT.Exp).then_inc(r_d, 1)

            def x_copy(e, b):
                act.wait_ge(x_flip, NE * layer + e + 1)
                if not isinstance(e, int) or e >= 2 or layer:
                    act.wait_ge(gu_mm, NE * layer + e - 1)
                nc.scalar.activation(xts[b].rearrange("p k c -> p (k c)"), ps[:, 2 + b, :], ACT.Copy).then_inc(x_sb, 1)

            def silu_step(e, b):
                act.wait_ge(gu_mm, NE * layer + e + 1)
                if not isinstance(e, int) or e >= 2 or layer:
                    act.wait_ge(h_sb, NE * layer + e - 1)
                nc.scalar.activation(sil[b][CAP:P, :], ps[0:CAP, b, 0:F], ACT.Silu).then_inc(silu, 1)

            x_copy(0, 0)
            for e in range(2):
                silu_step(e, e)
                x_copy(e + 1, 1 - e)
            with act.Fori(1, NE // 2 - 1) as i:
                for u in range(2):
                    silu_step(2 * i + u, u)
                    x_copy(2 * i + u + 1, 1 - u)
            silu_step(NE - 2, 0)
            x_copy(NE - 1, 1)
            silu_step(NE - 1, 1)
            s = ov[layer]
            act.wait_ge(s["count"], 1)
            extra = act.value_load(ov_i[0:1, layer:layer + 1], min_val=0, max_val=MAX_EXTRA)
            with act.If(extra > 0):
                with act.Fori(0, extra) as o:
                    act.wait_ge(s["xf"], o + 1)
                    nc.scalar.activation(xts[0].rearrange("p k c -> p (k c)"), ps[:, 2, :], ACT.Copy).then_inc(s["xs"], 1)
                    act.wait_ge(s["gu"], o + 1)
                    nc.scalar.activation(sil[0][CAP:P, :], ps[0:CAP, 0, 0:F], ACT.Silu).then_inc(s["silu"], 1)
                wait_apart(act, s["scat"], 16 * extra)
            for b in range(2):
                act.wait_ge(scat[b], NE // 2 * (layer + 1) * 16)
            for t in range(NT):
                if t >= 2:
                    act.wait_ge(hid_moe[layer], t - 1)
                r = ROWS[t]
                act.dma_start(y2b[t % 2][:r, :, :],
                              y2_dram[4 * COL[t]:4 * COL[t] + 4 * r, :].rearrange("(p c) d -> p (c d)", c=4)
                              .rearrange("p (a b) -> p a b", b=D)).then_inc(y2_in[t % 2], 16)

        moe(0)
        norm(2)
        act.wait_ge(lam_in, 32)
        act.wait_ge(lam_sum, 1)
        nc.scalar.activation(lam4[:, 2:4], lam4[:, 0:2], ACT.Exp).then_inc(r_d, 1)
        for m in range(8):
            act.wait_ge(q_mm, 8 + m + 1)
            nc.scalar.activation(qT[:, m, 0:HALF_N], ps[:, 2 * (m % 2), 0:HALF_N], ACT.Copy).then_inc(q_act, 1)
        for i in range(4):
            tile, quad = divmod(i, 2)
            act.wait_ge(k_flip, 6 + i + 1)
            nc.scalar.activation(kTb[:, 4 * quad:4 * quad + 4, SEQ + P * tile:SEQ + P * tile + P],
                                 ps[:, 6 + i % 2, :].rearrange("p (h c) -> p h c", c=P), ACT.Copy).then_inc(k_sb, 1)
        for i in range(KV_ITEMS):
            sl, t = kv_item(i)
            act.wait_ge(k_flip, 10 + i + 1)
            if t is None:
                dst, r, h = kTb[:, :, SEQ + PAST:SEQ + PAST + DEC], DEC, B_HEADS
            else:
                dst, r, h = kTb[:, 2 * sl:2 * sl + 2, COL[t]:COL[t] + P], P, 2
            nc.scalar.activation(dst, ps[:, 6 + i % 2, 0:h * r].rearrange("p (h c) -> p h c", c=r),
                                 ACT.Copy).then_inc(k_sb, 1)
        for step in range(UNITS + 4):
            u = step - 4
            if 0 <= u < UNITS:
                t, hp = b_unit(u)[:2]
                r = ROWS[t]
                act.wait_ge(at["b", "onflip"], u + 1)
                nc.scalar.activation(oT[:, 2 * hp:2 * hp + 2, COL[t]:COL[t] + r],
                                     ps[:, 6, 2 * P:4 * P].rearrange("p (h c) -> p h c", c=P)[:, :, 0:r],
                                     ACT.Copy).then_inc(at["b", "o"], 1)
            attention("b", b_unit, E_B, step)
            u = step - 2
            if 0 <= u < UNITS:
                t, hp, kc, nk, tc, vt = b_unit(u)
                r = ROWS[t]
                act.wait_ge(at["b", "flip"], u + 1)
                if u >= 1:
                    act.wait_ge(at["b", "pv"], u)
                for kb, (_, kr) in enumerate(vt):
                    if kb == 0 or kr < P:
                        nb = sum(1 for _, x in vt if x == P) if kb == 0 else 1
                        ins = nc.scalar.activation(
                            PT_B[0:kr, 0, kb:kb + nb, 0:r],
                            ps[0:kr, 4, :].rearrange("p (k c) -> p k c", c=P)[:, kb:kb + nb, 0:r], ACT.Copy)
                ins.then_inc(at["b", "pt"], 1)
            u = step - 3
            if 0 <= u < UNITS:
                r = ROWS[b_unit(u)[0]]
                act.wait_ge(at["b", "pv"], u + 1)
                if u >= 2:
                    act.wait_ge(at["b", "onflip"], u - 1)
                for hh in range(2):
                    ins = nc.scalar.activation(ON[u % 2][:r, hh, :], ps[:r, 6, hh * P:hh * P + P], ACT.Square,
                                               accum_out=st[u % 3][:r, 20 + hh:21 + hh])
                ins.then_inc(at["b", "sq"], 1)
        moe(1)
        norm(4)

    @block.vector
    def _(dve):
        own = Link(dve_own)

        def norm(n):
            def rows(t):
                r = ROWS[t]
                dve.wait_ge(rstd_ready, NT * n + t + 1)
                if t == 0:
                    dve.wait_ge(g_in, 16 * (n + 1))
                if t >= 2 and n < 4:
                    dve.wait_ge(y_flip, NT * n + t - 1)
                if t >= 2 and n in (1, 3):
                    before = 3 * (n // 2), 2 * (n // 2)
                    dve.wait_ge(y_out[t % 2], 16 * (before[t % 2] + t // 2))
                if t >= 2 and n == 4:
                    dve.wait_ge(y_out[t % 2], 16 * ((6, 4)[t % 2] + t // 2))
                nc.vector.scalar_tensor_tensor(ynorm[t % 2][:r, :], hid[:r, t, :], rstd[:r, t:t + 1], gbc[:r, :],
                                               ALU.mult, ALU.mult).then_inc(y_ready, 1)

            def xt_copy(t):
                r = ROWS[t]
                b = 2 * (t % 2) + 1
                dve.wait_ge(y_flip, NT * n + t + 1)
                nc.vector.tensor_copy(xT[:, 4:8, COL[t]:COL[t] + r],
                                      ps[:, b, :].rearrange("p (k c) -> p k c", c=P)[:, :, 0:r]).then_inc(xt_dve, 1)

            for t in range(NT):
                rows(t)
                if t > 0 and n < 4:
                    xt_copy(t - 1)
            if n < 4:
                xt_copy(NT - 1)

        norm(0)
        dve.wait_ge(bias_in, 48)
        own(dve, nc.vector.tensor_scalar(sink8, st[0][:, 0:16], 1.0 / SCALE, None, ALU.mult))
        for m in range(8):
            dve.wait_ge(q_mm, m + 1)
            nc.vector.tensor_scalar(qT[:, m, HALF_N:N], ps[:, 2 * (m % 2) + 1, 0:HALF_N], bq[:, m:m + 1], None,
                                    ALU.add).then_inc(q_dve, 1)
        dve.wait_ge(cache_a_in, 48)

        def twice(x):
            return x.rearrange("p (h d) -> p h d", d=HD).unsqueeze(2).broadcast_to([x.shape[0], A_KV, 2, HD])

        def dup(i, r):
            return kst[:r, i, :].rearrange("p (h c d) -> p h c d", c=2, d=HD)

        nc.vector.tensor_copy(dup(5, P), twice(kca)).then_inc(cachek_sb, 1)
        for t in range(NT):
            r = ROWS[t]
            dve.wait_ge(kv_mm, t + 1)
            for c in range(2):
                ins = nc.vector.tensor_tensor(dup(t, r)[:, :, c, :],
                                              ps[:r, 4 + t % 2, 0:AKV].rearrange("p (h d) -> p h d", d=HD),
                                              bkv[:r, 0:AKV].rearrange("p (h d) -> p h d", d=HD), ALU.add)
            ins.then_inc(kv_sb, 1)
        for t in range(NT):
            r = ROWS[t]
            i = NT + t
            dve.wait_ge(kv_mm, i + 1)
            nc.vector.tensor_tensor(va[:r, t if t < 4 else 5, :], ps[:r, 4 + i % 2, 0:AKV], bkv[:r, AKV:2 * AKV],
                                    ALU.add).then_inc(kv_sb, 1)

        def bias_max(layer, unit, E, u, bank, tab, head):
            t, j, kc, nk, tc, vt = unit(u)
            r = ROWS[t]
            sm = st[u % 3]
            dve.wait_ge(at[layer, "scores"], u + 1)
            if u >= 3:
                dve.wait_ge(at[layer, "flip"], u - 2)
            for g in range(4):
                b, c = bank(u, g)
                ins = nc.vector.tensor_tensor_reduce(
                    out=E[u % 3][:r, g, 0:nk], in0=ps[:r, b, c:c + nk], in1=tab[:r, head(j, g), tc:tc + nk],
                    scale=1.0, scalar=-3e38, op0=ALU.add, op1=ALU.max, accum_out=sm[:r, g:g + 1])
            own(dve, ins)
            if layer == "a":
                own(dve, nc.vector.tensor_tensor(sm[:r, 0:4], sm[:r, 0:4], sink8[:r, 4 * j:4 * j + 4], ALU.max))
                nc.vector.tensor_tensor(sm[:r, 12:16], sink8[:r, 4 * j:4 * j + 4], sm[:r, 0:4], ALU.subtract)
            nc.vector.tensor_scalar(sm[:r, 4:8], sm[:r, 0:4], -SCALE, None, ALU.mult).then_inc(at[layer, "biased"], 1)

        def residual(layer, i):
            if i is not None:
                dve.wait_ge(o_mm, O_ITEMS * layer + i + 1)
                h = hid[:, i // 4, F * (i % 4):F * (i % 4) + F]
                nc.vector.tensor_tensor(h, h, ps[:, 7, 0:F], ALU.add).then_inc(hid_attn, 1)

        def residual_sample(layer):
            dve.wait_ge(o_mm, O_ITEMS * (layer + 1))
            for s in range(4):
                h = hid[0:DEC, 4, F * s:F * s + F]
                nc.vector.tensor_tensor(h, h, ps[DEC * s:DEC * s + DEC, 6, 0:F], ALU.add).then_inc(hid_attn, 1)

        def bank_a(u, g):
            return 2 * (u % 2) + g % 2, (g // 2) * 2 * P

        dve.wait_ge(tab_ready, 1)
        dve.wait_ge(k_out, 16 * 6)
        dve.wait_ge(k_flip, 6)
        dve.wait_ge(router_packed, 1)
        for step in range(UNITS + 3):
            residual(0, o_item(0, step - 1))
            if step < UNITS:
                bias_max("a", a_unit, E_A, step, bank_a, tabA, lambda j, g: 4 * j + g)
            u = step - 1
            if 0 <= u < UNITS:
                r = ROWS[a_unit(u)[0]]
                sm = st[u % 3]
                dve.wait_ge(at["a", "exp"], u + 1)
                own(dve, nc.vector.tensor_tensor(sm[:r, 20:24], sm[:r, 8:12], sm[:r, 16:20], ALU.add))
                nc.vector.reciprocal(sm[:r, 24:28], sm[:r, 20:24]).then_inc(at["a", "recip"], 1)
            u = step - 2
            if 0 <= u < UNITS:
                t, j, kc, nk, tc, vt = a_unit(u)
                if len(vt) > 1:
                    r, kr = ROWS[t], vt[1][1]
                    dve.wait_ge(at["a", "flip"], u + 1)
                    if u >= 2:
                        dve.wait_ge(at["a", "pv"], u - 1)
                    nc.vector.tensor_copy(
                        PT_A[u % 2][:kr, :, 1, 0:r],
                        ps[:kr, 5, :].rearrange("p (g c) -> p g c", c=P)[:, :, 0:r]) \
                        .then_inc(ptd["a"], 1)
            u = step - 3
            if 0 <= u < UNITS:
                t, j = a_unit(u)[:2]
                r = ROWS[t]
                dve.wait_ge(at["a", "pv"], u + 1)
                nc.vector.tensor_copy(oT[:, 2 * j:2 * j + 2, COL[t]:COL[t] + r],
                                      ps[:, 6, 0:2 * P].rearrange("p (m c) -> p m c", c=P)[:, :, 0:r]) \
                    .then_inc(at["a", "o"], 1)
        residual(0, o_item(0, UNITS + 2))
        residual_sample(0)

        def moe(layer):
            norm(1 + 2 * layer)
            s = ov[layer]
            own(dve, nc.vector.memset(lg, 0.0))
            dve.wait_ge(r_mm, layer + 1)
            dve.wait_ge(router_in, 128)
            for h in range(2):
                ins = nc.vector.tensor_scalar(rT[0:36, HALF_N * h:HALF_N * h + HALF_N], ps[0:36, 4 + h, 0:HALF_N],
                                              brT[0:36, layer:layer + 1], None, ALU.add)
            ins.then_inc(r_sb, 1)
            dve.wait_ge(r_flip, layer + 1)
            pr = ps[:, 6, 0:NT * 36].rearrange("p (t c) -> p t c", c=36)
            nc.vector.tensor_copy(lg[:, 0:4, :], pr[:, 0:4, :])
            own(dve, nc.vector.tensor_copy(lg[0:DEC, 4, :], pr[0:DEC, 4, :]))

            def per_tile(i):
                return rs[:, i, 0:NT]

            def over(x, w):
                return x.unsqueeze(2).broadcast_to([P, NT, w])

            gl, el = lg[:, :, 0:G], lg[:, :, G:G + NE]
            own(dve, nc.vector.tensor_reduce(per_tile(0), gl, AX, ALU.max))
            nc.vector.tensor_tensor(rt[0][:, :, 0:G], gl, over(per_tile(0), G), ALU.subtract).then_inc(r_exp, 1)
            ghot = rt[1][:, :, 0:G]
            own(dve, nc.vector.tensor_tensor(rt[2][:, :, 0:G], gl, over(per_tile(0), G), ALU.is_equal))
            own(dve, nc.vector.tensor_tensor(rt[2][:, :, 0:G], rt[2][:, :, 0:G],
                                             cst[:, C_REV:C_REV + G].unsqueeze(1).broadcast_to([P, NT, G]), ALU.mult))
            own(dve, nc.vector.tensor_reduce(per_tile(1), rt[2][:, :, 0:G], AX, ALU.max))
            own(dve, nc.vector.tensor_tensor(ghot, rt[2][:, :, 0:G], over(per_tile(1), G), ALU.is_equal))
            own(dve, nc.vector.tensor_scalar(ghot, ghot, BIG, -BIG, ALU.mult, ALU.add))
            em = rt[3]
            own(dve, nc.vector.tensor_tensor(
                em.rearrange("p t (g e) -> p t g e", e=EPG), el.rearrange("p t (g e) -> p t g e", e=EPG),
                ghot.unsqueeze(3).broadcast_to([P, NT, G, EPG]), ALU.add))

            def top(dst, best, free):
                own(dve, nc.vector.tensor_reduce(per_tile(best), em, AX, ALU.max))
                own(dve, nc.vector.tensor_tensor(rt[4], em, over(per_tile(best), NE), ALU.is_equal))
                own(dve, nc.vector.tensor_tensor(
                    rt[4], rt[4], cst[:, C_REV:C_REV + NE].unsqueeze(1).broadcast_to([P, NT, NE]), ALU.mult))
                own(dve, nc.vector.tensor_reduce(per_tile(free), rt[4], AX, ALU.max))
                own(dve, nc.vector.tensor_tensor(dst, rt[4], over(per_tile(free), NE), ALU.is_equal))

            h1, h2 = rt[1], rt[2]
            top(h1, 2, 6)
            own(dve, nc.vector.scalar_tensor_tensor(em, h1, -2 * BIG, em, ALU.mult, ALU.add))
            top(h2, 3, 7)
            nc.vector.tensor_tensor(per_tile(4), per_tile(3), per_tile(2), ALU.subtract).then_inc(r_exp, 1)
            own(dve, nc.vector.tensor_tensor(h1, h1, over(cst[:, C_K1:C_K1 + NT], NE), ALU.mult))
            own(dve, nc.vector.tensor_tensor(h2, h2, over(cst[:, C_K2:C_K2 + NT], NE), ALU.mult))
            own(dve, nc.vector.tensor_tensor(key, h1, h2, ALU.add))
            nc.vector.tensor_scalar(rt[4], key, 0.0, None, ALU.is_gt).then_inc(r_key, 1)
            dve.wait_ge(r_d, 2 * layer + 2 + layer)
            own(dve, nc.vector.tensor_reduce(per_tile(8), rt[0][:, :, 0:G], AX, ALU.add))
            own(dve, nc.vector.reciprocal(per_tile(9), per_tile(8)))
            own(dve, nc.vector.tensor_scalar(per_tile(10), per_tile(5), 1.0, None, ALU.add))
            own(dve, nc.vector.reciprocal(per_tile(11), per_tile(10)))
            own(dve, nc.vector.tensor_tensor(gw[:, 0, 0:NT], per_tile(9), per_tile(11), ALU.mult))
            own(dve, nc.vector.tensor_tensor(gw[:, 1, 0:NT], gw[:, 0, 0:NT], per_tile(5), ALU.mult))
            dve.wait_ge(r_kflip, layer + 1)
            nc.vector.tensor_copy(keytab[0:NE, 0:SEQ], ps[0:NE, 5, :])
            own(dve, nc.vector.tensor_copy(keytab[0:NE, SEQ:N], ps[0:NE, 4, 0:DEC]))
            cnt = ovs[0:1, 0:NE]
            own(dve, nc.vector.tensor_scalar(cnt, ps[0:1, 7, 0:NE], float(-CAP), None, ALU.add))
            own(dve, nc.vector.tensor_tensor(
                keytmp[0:1, 0:NE * 8].rearrange("p (e j) -> p e j", j=8),
                cnt.unsqueeze(2).broadcast_to([1, NE, 8]),
                cst[0:1, C_THR:C_THR + 8].unsqueeze(1).broadcast_to([1, NE, 8]), ALU.subtract))
            own(dve, nc.vector.tensor_scalar(keytmp[0:1, 0:NE * 8], keytmp[0:1, 0:NE * 8], float(-CAP), None, ALU.is_gt))
            own(dve, nc.vector.tensor_reduce(ovs[0:1, 32:33], keytmp[0:1, 0:NE * 8], AX, ALU.add))
            nc.vector.tensor_copy(ov_i[0:1, layer:layer + 1], ovs[0:1, 32:33]).then_inc(s["count"], 1)

            def top64(table):
                return [lambda r=r: nc.vector.max(topk[0:NE, 8 * r:8 * r + 8], table[0:NE, :]) for r in range(CAP // 8)], \
                       [lambda r=r: nc.vector.match_replace(table[0:NE, :], topk[0:NE, 8 * r:8 * r + 8],
                                                            table[0:NE, :], -1.0) for r in range(CAP // 8)]

            take, strike = top64(keytab)
            for r in range(CAP // 8):
                own(dve, take[r]())
                own(dve, strike[r]())
            nc.vector.tensor_copy(topk[0:NE, CAP:P], topk[0:NE, 0:CAP]).then_inc(r_top, 1)
            dve.wait_ge(r_tflip, layer + 1)
            own(dve, nc.vector.tensor_scalar(idx_i[:, 2, :], ps[:, 6, 0:NE], -1.0, float(KEY0), ALU.mult, ALU.add))
            own(dve, nc.vector.tensor_scalar(rt[0].rearrange("p t e -> p (t e)")[:, 0:NE], ps[:, 6, 0:NE],
                                             -2.0, float(2 * KEY0), ALU.mult, ALU.add))
            own(dve, nc.vector.tensor_scalar(idx_i[:, 0, :], rt[0].rearrange("p t e -> p (t e)")[:, 0:NE],
                                             cst[:, C_HALF:C_HALF + 1], None, ALU.add))
            nc.vector.tensor_scalar(idx_i[:, 1, :], idx_i[:, 2, :], 1, None, ALU.arith_shift_right).then_inc(r_idx, 1)

            def mult(e, b):
                dve.wait_ge(silu, NE * layer + e + 1)
                if not isinstance(e, int) or e >= 2 or layer:
                    dve.wait_ge(h_flip, NE * layer + e - 1)
                nc.vector.tensor_tensor(hmul[b][CAP:P, :], sil[b][CAP:P, :], ps[CAP:P, b, 0:F], ALU.mult) \
                    .then_inc(h_sb, 1)

            def ht_copy(e, b):
                dve.wait_ge(h_flip, NE * layer + e + 1)
                if not isinstance(e, int) or e >= 2 or layer:
                    dve.wait_ge(d_mm, NE * layer + e - 1)
                nc.vector.tensor_copy(hts[b].rearrange("p c q -> p (c q)"), ps[:, 4 + b, 0:2 * CAP]).then_inc(ht_sb, 1)

            def y_copy(e, b, count=None):
                dve.wait_ge(d_mm, NE * layer + e + 1)
                if count is not None:
                    dve.wait_ge(scat[b], count)
                nc.vector.tensor_copy(yout[b], ps[:, 6 + b, :]).then_inc(ye_sb, 1)

            half = NE // 2 * layer
            for e in range(2):
                mult(e, e)
                ht_copy(e, e)
                if e:
                    y_copy(0, 0, 16 * half if layer else None)

            def two(i, before):
                mult(2 * i, 0)
                ht_copy(2 * i, 0)
                y_copy(2 * i - 1, 1, before)
                mult(2 * i + 1, 1)
                ht_copy(2 * i + 1, 1)
                y_copy(2 * i, 0, 16 * (half + i))

            two(1, 16 * half if layer else None)
            with dve.Fori(2, NE // 2) as i:
                two(i, 16 * (half + i - 1))
            y_copy(NE - 1, 1, 16 * (half + NE // 2 - 1))

            dve.wait_ge(s["count"], 1)
            for b in range(2):
                dve.wait_ge(scat[b], 16 * NE // 2 * (layer + 1))
            extra = dve.value_load(ov_i[0:1, layer:layer + 1], min_val=0, max_val=MAX_EXTRA)
            STEPS = 28
            with dve.If(extra > 0):
                with dve.Fori(0, extra) as o:
                    k = [0]

                    def link(ins):
                        k[0] += 1
                        ins.then_inc(s["own"], 1)
                        wait_apart(dve, s["own"], o * STEPS + k[0])

                    best, hot = ovs[0:1, 40:48], ovs[0:1, 64:96]
                    link(nc.vector.max(best, cnt))
                    link(nc.vector.max_index(ov_u[:, :], best, cnt))
                    link(nc.vector.tensor_copy(ovs[0:1, 48:49], ov_u[0:1, 0:1]))
                    link(nc.vector.tensor_scalar(hot, cst[0:1, C_IOTA:C_IOTA + NE], ovs[0:1, 48:49], None, ALU.is_equal))
                    nc.vector.scalar_tensor_tensor(cnt, hot, float(-CAP), cnt, ALU.mult, ALU.add).then_inc(s["pick"], 1)
                    mcol, mnot = ovs[0:NE, 96:97], ovs[0:NE, 97:98]
                    dve.wait_ge(s["mask"], o + 1)
                    link(nc.vector.tensor_copy(mcol, ps[0:NE, 7, 0:1]))
                    link(nc.vector.tensor_scalar(mnot, mcol, -1.0, 1.0, ALU.mult, ALU.add))
                    link(nc.vector.tensor_scalar(keytmp[0:NE, :], keytab[0:NE, :], mcol, None, ALU.mult))
                    take, strike = top64(keytmp)
                    for r in range(CAP // 8):
                        link(take[r]())
                        link(strike[r]())
                    link(nc.vector.tensor_scalar(keytmp[0:NE, :], keytmp[0:NE, :], mcol, None, ALU.mult))
                    link(nc.vector.scalar_tensor_tensor(keytab[0:NE, :], keytab[0:NE, :], mnot, keytmp[0:NE, :],
                                                        ALU.mult, ALU.add))
                    nc.vector.tensor_copy(topk[0:NE, CAP:P], topk[0:NE, 0:CAP]).then_inc(s["list"], 1)
                    dve.wait_ge(s["irow"], o + 1)
                    link(nc.vector.tensor_scalar(ov_i[:, 6:7], ps[:, 7, 8:9], -1.0, float(KEY0), ALU.mult, ALU.add))
                    link(nc.vector.tensor_scalar(ovs[:, 98:99], ps[:, 7, 8:9], -2.0, float(2 * KEY0), ALU.mult, ALU.add))
                    link(nc.vector.tensor_scalar(ov_i[:, 5:6], ovs[:, 98:99], cst[:, C_HALF:C_HALF + 1], None, ALU.add))
                    nc.vector.tensor_scalar(ov_i[:, 4:5], ov_i[:, 6:7], 1, None, ALU.arith_shift_right) \
                        .then_inc(s["idx"], 1)
                    dve.wait_ge(s["silu"], o + 1)
                    nc.vector.tensor_tensor(hmul[0][CAP:P, :], sil[0][CAP:P, :], ps[CAP:P, 0, 0:F], ALU.mult) \
                        .then_inc(s["h"], 1)
                    dve.wait_ge(s["hf"], o + 1)
                    nc.vector.tensor_copy(hts[0].rearrange("p c q -> p (c q)"), ps[:, 4, 0:2 * CAP]).then_inc(s["ht"], 1)
                    dve.wait_ge(s["d"], o + 1)
                    nc.vector.tensor_copy(yout[0], ps[:, 6, :]).then_inc(s["y"], 1)
                    wait_apart(dve, s["scat"], 16 * o + 16)
                    assert k[0] == STEPS, k
            for t in range(NT):
                r = ROWS[t]
                dve.wait_ge(y2_in[t % 2], 16 * ((3, 2)[t % 2] * layer + t // 2 + 1))
                h = hid[:r, t, :]
                own(dve, nc.vector.scalar_tensor_tensor(h, y2b[t % 2][:r, 0, :], gw[:r, 0, t:t + 1], h, ALU.mult, ALU.add))
                nc.vector.scalar_tensor_tensor(h, y2b[t % 2][:r, 1, :], gw[:r, 1, t:t + 1], h, ALU.mult, ALU.add) \
                    .then_inc(hid_moe[layer], 1)

        moe(0)
        norm(2)
        dve.wait_ge(lam_in, 32)
        own(dve, nc.vector.tensor_tensor(lamb[:, 0, :], lamb[:, 0, :], lamb[:, 1, :], ALU.mult))
        own(dve, nc.vector.tensor_tensor(lamb[:, 2, :], lamb[:, 2, :], lamb[:, 3, :], ALU.mult))
        own(dve, nc.vector.tensor_scalar(subg, subg, 1.0 - LAM_INIT, None, ALU.mult))
        nc.vector.tensor_reduce(lam4[:, 0:2], lamb.rearrange("p (a b) d -> p a b d", b=2)[:, :, 0, :], AX, ALU.add) \
            .then_inc(lam_sum, 1)
        for m in range(8):
            dve.wait_ge(q_mm, 8 + m + 1)
            nc.vector.tensor_copy(qT[:, m, HALF_N:N], ps[:, 2 * (m % 2) + 1, 0:HALF_N]).then_inc(q_dve, 1)
        dve.wait_ge(r_d, 3)
        own(dve, nc.vector.tensor_tensor(neglam, lam4[:, 3:4], lam4[:, 2:3], ALU.subtract))
        own(dve, nc.vector.tensor_scalar(neglam, neglam, -LAM_INIT, None, ALU.add))
        for i in range(2 * KV_ITEMS):
            sl, t = kv_item(i)
            dve.wait_ge(kv_mm, 2 * NT + i + 1)
            if i == 0:
                dve.wait_ge(tab_ready, 2)
            if i == KV_ITEMS:
                dve.wait_ge(k_flip, 10)
            if t is None:
                for j in range(4):
                    c = F * j
                    dst = kbt[0:DEC, 4, c:c + F] if sl < 4 else vb[0:DEC, 6, c:c + F]
                    ins = nc.vector.tensor_copy(dst, ps[DEC * j:DEC * j + DEC, 4 + i % 2, 0:F])
            else:
                c = F * (sl % 4)
                dst = kbt[:, t, c:c + F] if sl < 4 else vb[:, t, c:c + F]
                ins = nc.vector.tensor_copy(dst, ps[:, 4 + i % 2, 0:F])
            ins.then_inc(kv_sb, 1)
        dve.wait_ge(k_out, 16 * (6 + NT))
        dve.wait_ge(k_flip, 10 + KV_ITEMS)
        for step in range(UNITS + 4):
            residual(1, o_item(1, step - 1))
            if step < UNITS:
                bias_max("b", b_unit, E_B, step, lambda u, g: (g, 0), tabB, lambda j, g: 2 * j + g // 2)
            u = step - 1
            if 0 <= u < UNITS:
                r = ROWS[b_unit(u)[0]]
                sm = st[u % 3]
                dve.wait_ge(at["b", "exp"], u + 1)
                own(dve, nc.vector.reciprocal(sm[:r, 12:16], sm[:r, 8:12]))
                nc.vector.tensor_scalar(sm[:r, 16:18], sm[:r, 12:16].rearrange("p (h c) -> p h c", c=2)[:, :, 1],
                                        neglam[:r, :], None, ALU.mult).then_inc(at["b", "recip"], 1)
            u = step - 2
            if 0 <= u < UNITS:
                t, hp, kc, nk, tc, vt = b_unit(u)
                r = ROWS[t]
                Eu = E_B[u % 3]
                dve.wait_ge(at["b", "scaled"], u + 1)
                for hh in range(2):
                    ins = nc.vector.scalar_tensor_tensor(Eu[:r, 2 * hh, 0:nk], Eu[:r, 2 * hh, 0:nk],
                                                         st[u % 3][:r, 12 + 2 * hh:13 + 2 * hh],
                                                         Eu[:r, 2 * hh + 1, 0:nk], ALU.mult, ALU.add)
                ins.then_inc(at["b", "probs"], 1)
            u = step - 2
            if 0 <= u < UNITS:
                t, hp, kc, nk, tc, vt = b_unit(u)
                r = ROWS[t]
                dve.wait_ge(at["b", "flip"], u + 1)
                if u >= 1:
                    dve.wait_ge(at["b", "pv"], u)
                for kb, (_, kr) in enumerate(vt):
                    if kb == 0 or kr < P:
                        nb = sum(1 for _, x in vt if x == P) if kb == 0 else 1
                        ins = nc.vector.tensor_copy(
                            PT_B[0:kr, 1, kb:kb + nb, 0:r],
                            ps[0:kr, 5, :].rearrange("p (k c) -> p k c", c=P)[:, kb:kb + nb, 0:r])
                ins.then_inc(ptd["b"], 1)
            u = step - 3
            if 0 <= u < UNITS:
                r = ROWS[b_unit(u)[0]]
                dve.wait_ge(at["b", "rms"], u + 1)
                for hh in range(2):
                    ins = nc.vector.scalar_tensor_tensor(ON[u % 2][:r, hh, :], ps[:r, 6, hh * P:hh * P + P],
                                                         st[u % 3][:r, 24 + hh:25 + hh], subg[:r, :], ALU.mult, ALU.mult)
                ins.then_inc(at["b", "on"], 1)
        residual(1, o_item(1, UNITS + 3))
        residual_sample(1)
        moe(1)
        norm(4)

    @block.tensor
    def _(pe):
        def norm(n):
            for t in range(NT):
                r = ROWS[t]
                b = 2 * (t % 2)
                pe.wait_ge(y_ready, NT * n + t + 1)
                if t == 0 and n == 0:
                    pe.wait_ge(const_in, 16)
                if t >= 2:
                    pe.wait_ge(xt_act, NT * n + t - 1)
                    pe.wait_ge(xt_dve, NT * n + t - 1)
                y = ynorm[t % 2][:r, :].rearrange("p (c k) -> p k c", k=KD)
                for k in range(KD):
                    ins = nc.tensor.transpose(ps[:, b + k // 4, (k % 4) * P:(k % 4) * P + r], y[:, k, :], ident[:r, :r])
                ins.then_inc(y_flip, 1)
            pe.wait_ge(xt_act, NT * n + NT)
            pe.wait_ge(xt_dve, NT * n + NT)

        def ring_k(n):
            return ring[:, slot(n), :].rearrange("p (k f) -> p k f", f=F)

        def arrived(n):
            pe.wait_ge(w_ready[slot(n)], landed(n))

        def q_proj(layer, n0):
            for m in range(8):
                n = n0 + m // 2
                if m % 2 == 0:
                    arrived(n)
                if m >= 2 or layer:
                    pe.wait_ge(q_act, 8 * layer + m - 1)
                    pe.wait_ge(q_dve, 8 * layer + m - 1)
                w = ring_k(n)[:, :, (m % 2) * P:(m % 2) * P + P]
                for h in range(2):
                    for k in range(KD):
                        ins = nc.tensor.matmul(ps[:, 2 * (m % 2) + h, 0:HALF_N], w[:, k, :],
                                               xT[:, k, HALF_N * h:HALF_N * h + HALF_N], start=k == 0, stop=k == KD - 1)
                        if h and k == KD - 1:
                            ins.then_inc(q_mm, 1)

        def rows_mm(bank, t, n):
            r = ROWS[t]
            for k in range(KD):
                ins = nc.tensor.matmul(ps[:r, bank, 0:F], xT[:, k, COL[t]:COL[t] + r], ring_k(n)[:, k, :],
                                       start=k == 0, stop=k == KD - 1)
            return ins

        def sample_mm(bank, src, n0):
            for k in range(KD):
                for s in range(4):
                    ins = nc.tensor.matmul(ps[DEC * s:DEC * s + DEC, bank, 0:F], src[:, k, SEQ:N], ring_k(n0 + s)[:, k, :],
                                           start=k == 0, stop=k == KD - 1)
            return ins

        def out_item(layer, i):
            if i is None:
                return
            n0 = (A_SLOTS, B_STREAM0 + B_SLOTS)[layer] - 4
            t, s = divmod(i, 4)
            if s == 0:
                pe.wait_ge(at["ab"[layer], "o"], 4 * t + 4)
            if t == 0:
                arrived(n0 + s)
            if i >= 1:
                pe.wait_ge(hid_attn, 4 * NT * layer + i)
            rows_mm(7, t, n0 + s).then_inc(o_mm, 1)

        def out_sample(layer):
            pe.wait_ge(at["ab"[layer], "o"], UNITS)
            sample_mm(6, oT, (A_SLOTS, B_STREAM0 + B_SLOTS)[layer] - 4).then_inc(o_mm, 1)

        norm(0)
        q_proj(0, 0)
        pe.wait_ge(cachek_sb, 1)

        def flip_a(i, order):
            r = (P, P, P, P, DEC, P)[i]
            if order >= 2:
                pe.wait_ge(k_sb, order - 1)
            for j in range(A_KV):
                ins = nc.tensor.transpose(ps[:, 6 + order % 2, j * P:j * P + r], kst[:r, i, j * P:j * P + P], ident[:r, :r])
            ins.then_inc(k_flip, 1)

        arrived(4)
        for t in range(NT + 1):
            if t < NT:
                if t >= 2:
                    pe.wait_ge(kv_sb, t - 1)
                rows_mm(4 + t % 2, t, 4).then_inc(kv_mm, 1)
            if t > 0:
                pe.wait_ge(kv_sb, t)
                flip_a(t - 1, t - 1)
        flip_a(5, 5)
        arrived(5)
        for t in range(NT):
            pe.wait_ge(kv_sb, NT + t - 1)
            rows_mm(4 + (NT + t) % 2, t, 5).then_inc(kv_mm, 1)
        pe.wait_ge(q_act, 8)
        pe.wait_ge(q_dve, 8)
        pe.wait_ge(k_sb, 6)
        pe.wait_ge(kv_sb, 2 * NT)
        pe.wait_ge(cache_a_in, 48)
        for step in range(UNITS + 3):
            if step < UNITS:
                u = step
                t, j, kc, nk, tc, vt = a_unit(u)
                r = ROWS[t]
                if u >= 2:
                    pe.wait_ge(at["a", "biased"], u - 1)
                for g in range(4):
                    lo = HD * (g % 2)
                    ins = nc.tensor.matmul(ps[:r, 2 * (u % 2) + g % 2, (g // 2) * 2 * P:(g // 2) * 2 * P + nk],
                                           qT[lo:lo + HD, 2 * j + g // 2, COL[t]:COL[t] + r],
                                           kTa[lo:lo + HD, j, kc:kc + nk], start=True, stop=True)
                ins.then_inc(at["a", "scores"], 1)
            u = step - 3
            if 0 <= u < UNITS:
                t, j, kc, nk, tc, vt = a_unit(u)
                r = ROWS[t]
                pe.wait_ge(at["a", "pt"], u + 1)
                if u >= 4:
                    pe.wait_ge(ptd["a"], u - 3)
                if u >= 1:
                    pe.wait_ge(at["a", "o"], u)
                for gp in range(2):
                    for kb, (v, kr) in enumerate(vt):
                        for gh in range(2):
                            ins = nc.tensor.matmul(ps[HD * gh:HD * gh + HD, 6, gp * P:gp * P + r],
                                                   va[:kr, v, j * HD:j * HD + HD],
                                                   PT_A[u % 2][:kr, 2 * gp + gh, kb, 0:r],
                                                   start=kb == 0, stop=kb == len(vt) - 1)
                ins.then_inc(at["a", "pv"], 1)
            u = step - 2
            if 0 <= u < UNITS:
                t, j, kc, nk, tc, vt = a_unit(u)
                r = ROWS[t]
                pe.wait_ge(at["a", "probs"], u + 1)
                if u >= 1:
                    pe.wait_ge(at["a", "pt"], u)
                if u >= 5:
                    pe.wait_ge(ptd["a"], u - 4)
                for g in range(4):
                    for kb, (v, kr) in enumerate(vt):
                        ins = nc.tensor.transpose(ps[:kr, 4 + kb, g * P:g * P + r], E_A[u % 3][:r, g, kb * P:kb * P + kr],
                                                  ident[:r, :r])
                ins.then_inc(at["a", "flip"], 1)
            out_item(0, o_item(0, step))
        out_sample(0)

        def moe(layer):
            norm(1 + 2 * layer)
            s = ov[layer]
            pe.wait_ge(router_packed, 1)
            pe.wait_ge(hid_attn, 4 * NT * (layer + 1))
            for h in range(2):
                for k in range(KD):
                    ins = nc.tensor.matmul(ps[0:36, 4 + h, 0:HALF_N], wr_sb[:, layer, k, :],
                                           xT[:, k, HALF_N * h:HALF_N * h + HALF_N], start=k == 0, stop=k == KD - 1)
            ins.then_inc(r_mm, 1)
            pe.wait_ge(r_sb, layer + 1)
            for t in range(NT):
                r = ROWS[t]
                ins = nc.tensor.transpose(ps[:r, 6, 36 * t:36 * t + 36], rT[0:36, COL[t]:COL[t] + r], ident[0:36, 0:36])
            ins.then_inc(r_flip, 1)
            pe.wait_ge(r_key, layer + 1)
            for t in range(NT):
                r = ROWS[t]
                b, c = (5, COL[t]) if t < 4 else (4, 0)
                nc.tensor.transpose(ps[0:NE, b, c:c + r], key[:r, t, :], ident[:r, :r])
            for t in range(NT):
                r = ROWS[t]
                ins = nc.tensor.matmul(ps[0:1, 7, 0:NE], ones[:r, 0:1], rt[4][:r, t, :], start=t == 0, stop=t == NT - 1)
            ins.then_inc(r_kflip, 1)
            pe.wait_ge(r_top, layer + 1)
            nc.tensor.transpose(ps[:, 6, 0:NE], topk[0:NE, :], ident[0:NE, 0:NE]).then_inc(r_tflip, 1)

            def x_transpose(turn, u):
                e, b = DEEP * turn + u, u % 2
                pe.wait_ge(gath[u], 16 * (NE // DEEP * layer + 1 + turn))
                if not isinstance(e, int) or e >= 2 or layer:
                    wait_apart(pe, x_sb, NE * layer + e - 1)
                x = xg[u][0:CAP, :].rearrange("p (c k) -> p k c", k=KD)
                for k in range(KD):
                    ins = nc.tensor.transpose(ps[:, 2 + b, k * CAP:k * CAP + CAP], x[:, k, :], ident[0:CAP, 0:CAP])
                ins.then_inc(x_flip, 1)

            def gate_up(turn, u):
                e, b = DEEP * turn + u, u % 2
                pe.wait_ge(x_sb, NE * layer + e + 1)
                w = []
                for j in range(2):
                    where, landed_sem, value = expert_slot(layer, u, j, turn)
                    pe.wait_ge(landed_sem, value)
                    w.append(where.rearrange("p (k f) -> p k f", f=F))
                if not isinstance(e, int) or e >= 2 or layer:
                    pe.wait_ge(h_sb, NE * layer + e - 1)
                expert_gu(xts[b], w[0], w[1], b).then_inc(gu_mm, 1)

            def expert_gu(x, wg, wu, bank):
                for k in range(KD):
                    nc.tensor.matmul(ps[0:CAP, bank, 0:F], x[:, k, :], wg[:, k, :], start=k == 0, stop=k == KD - 1)
                    ins = nc.tensor.matmul(ps[CAP:P, bank, 0:F], x[:, k, :], wu[:, k, :], start=k == 0, stop=k == KD - 1)
                return ins

            def expert_ht(h, bank):
                for c in range(2):
                    ins = nc.tensor.transpose(ps[:, bank, c * CAP:c * CAP + CAP], h[CAP:P, c * P:c * P + P],
                                              ident[CAP:P, CAP:P])
                return ins

            def expert_down(ht, wd, bank):
                for c in range(2):
                    nc.tensor.matmul(ps[0:CAP, bank, :], ht[:, c, :], wd[:, c, 0:OUT_HALF], start=c == 0, stop=c == 1)
                    ins = nc.tensor.matmul(ps[CAP:P, bank, :], ht[:, c, :], wd[:, c, OUT_HALF:D], start=c == 0, stop=c == 1)
                return ins

            def h_transpose(turn, u):
                e, b = DEEP * turn + u, u % 2
                pe.wait_ge(h_sb, NE * layer + e + 1)
                if not isinstance(e, int) or e >= 2 or layer:
                    wait_apart(pe, ht_sb, NE * layer + e - 1)
                expert_ht(hmul[b], 4 + b).then_inc(h_flip, 1)

            def down(turn, u):
                e, b = DEEP * turn + u, u % 2
                pe.wait_ge(ht_sb, NE * layer + e + 1)
                where, landed_sem, value = expert_slot(layer, u, 2, turn)
                pe.wait_ge(landed_sem, value)
                if not isinstance(e, int) or e >= 2 or layer:
                    pe.wait_ge(ye_sb, NE * layer + e - 1)
                expert_down(hts[b], where.rearrange("p (c d) -> p c d", d=D), 6 + b).then_inc(d_mm, 1)

            def step(turn, u, last=False):
                gate_up(turn, u)
                if not last:
                    x_transpose(*((turn, u + 1) if u < DEEP - 1 else (turn + 1, 0)))
                if not (isinstance(turn, int) and turn == 0 and u == 0):
                    down(*((turn, u - 1) if u else (turn - 1, DEEP - 1)))
                h_transpose(turn, u)

            pe.wait_ge(r_idx, layer + 1)
            x_transpose(0, 0)
            for u in range(DEEP):
                step(0, u)
            with pe.Fori(1, NE // DEEP - 1) as i:
                for u in range(DEEP):
                    step(i, u)
            for u in range(DEEP):
                step(NE // DEEP - 1, u, last=u == DEEP - 1)
            down(NE // DEEP - 1, DEEP - 1)
            pe.wait_ge(s["count"], 1)
            pe.wait_ge(ye_sb, NE * (layer + 1))
            extra = pe.value_load(ov_i[0:1, layer:layer + 1], min_val=0, max_val=MAX_EXTRA)
            with pe.If(extra > 0):
                with pe.Fori(0, extra) as o:
                    wait_apart(pe, s["pick"], o + 1)
                    nc.tensor.matmul(ps[0:NE, 7, 0:1], ovs[0:1, 64:96], ident[0:1, 0:1], start=True, stop=True) \
                        .then_inc(s["mask"], 1)
                    pe.wait_ge(s["list"], o + 1)
                    nc.tensor.matmul(ps[:, 7, 8:9], topk[0:NE, :], ovs[0:NE, 96:97], start=True, stop=True) \
                        .then_inc(s["irow"], 1)
                    wait_apart(pe, s["gath"], 16 * (o + 1))
                    x = xg[0][0:CAP, :].rearrange("p (c k) -> p k c", k=KD)
                    for k in range(KD):
                        ins = nc.tensor.transpose(ps[:, 2, k * CAP:k * CAP + CAP], x[:, k, :], ident[0:CAP, 0:CAP])
                    ins.then_inc(s["xf"], 1)
                    pe.wait_ge(s["xs"], o + 1)
                    pe.wait_ge(s["w"], 48 * (o + 1))
                    wv = ovw[:, :, :].rearrange("p j (k f) -> p j k f", f=F)
                    expert_gu(xts[0], wv[:, 0], wv[:, 1], 0).then_inc(s["gu"], 1)
                    wait_apart(pe, s["h"], o + 1)
                    expert_ht(hmul[0], 4).then_inc(s["hf"], 1)
                    pe.wait_ge(s["ht"], o + 1)
                    expert_down(hts[0], ovw[:, 2, :].rearrange("p (c d) -> p c d", d=D), 6).then_inc(s["d"], 1)

        moe(0)
        norm(2)
        q_proj(1, B_STREAM0)
        pe.wait_ge(cache_b_in, 64)
        for i in range(4):
            tile, quad = divmod(i, 2)
            if i >= 2:
                pe.wait_ge(k_sb, 6 + i - 1)
            for h in range(4):
                c = (4 * quad + h) * P
                ins = nc.tensor.transpose(ps[:, 6 + i % 2, h * P:h * P + P], kcb[:, tile, c:c + P], ident)
            ins.then_inc(k_flip, 1)
        for i in range(2 * KV_ITEMS + 1):
            if i < 2 * KV_ITEMS:
                sl, t = kv_item(i)
                if t == 0:
                    arrived(B_STREAM0 + 4 + sl)
                if i >= 2:
                    pe.wait_ge(kv_sb, 2 * NT + i - 1)
                if t is None:
                    sample_mm(4 + i % 2, xT, B_STREAM0 + 4 + sl).then_inc(kv_mm, 1)
                else:
                    rows_mm(4 + i % 2, t, B_STREAM0 + 4 + sl).then_inc(kv_mm, 1)
            b = i - 1
            if 0 <= b < KV_ITEMS:
                sl, t = kv_item(b)
                pe.wait_ge(kv_sb, 2 * NT + b + 1)
                pe.wait_ge(k_sb, 10 + b - 1)
                r, tile, h0, nh = (DEC, 4, 0, B_HEADS) if t is None else (P, t, 2 * sl, 2)
                for h in range(nh):
                    ins = nc.tensor.transpose(ps[:, 6 + b % 2, h * r:h * r + r], kbt[:r, tile, (h0 + h) * P:(h0 + h) * P + P],
                                              ident[:r, :r])
                ins.then_inc(k_flip, 1)
        pe.wait_ge(q_act, 16)
        pe.wait_ge(q_dve, 16)
        pe.wait_ge(k_sb, 10 + KV_ITEMS)
        pe.wait_ge(kv_sb, 2 * NT + 2 * KV_ITEMS)
        for step in range(UNITS + 4):
            if step < UNITS:
                u = step
                t, hp, kc, nk, tc, vt = b_unit(u)
                r = ROWS[t]
                if u >= 1:
                    pe.wait_ge(at["b", "biased"], u)
                for g in range(4):
                    lo = HD * (g % 2)
                    ins = nc.tensor.matmul(ps[:r, g, 0:nk], qT[lo:lo + HD, 2 * hp + g // 2, COL[t]:COL[t] + r],
                                           kTb[lo:lo + HD, 2 * hp + g // 2, kc:kc + nk], start=True, stop=True)
                ins.then_inc(at["b", "scores"], 1)
            u = step - 4
            if 0 <= u < UNITS:
                t, hp = b_unit(u)[:2]
                r = ROWS[t]
                pe.wait_ge(at["b", "on"], u + 1)
                for hh in range(2):
                    ins = nc.tensor.transpose(ps[:, 6, (2 + hh) * P:(2 + hh) * P + r], ON[u % 2][:r, hh, :],
                                              ident[:r, :r])
                ins.then_inc(at["b", "onflip"], 1)
            out_item(1, o_item(1, step))
            u = step - 3
            if 0 <= u < UNITS:
                t, hp, kc, nk, tc, vt = b_unit(u)
                r = ROWS[t]
                pe.wait_ge(at["b", "pt"], u + 1)
                pe.wait_ge(ptd["b"], u + 1)
                if u >= 1:
                    pe.wait_ge(at["b", "on"], u)
                    pe.wait_ge(at["b", "sq"], u)
                    pe.wait_ge(at["b", "o"], u)
                for hh in range(2):
                    for kb, (v, kr) in enumerate(vt):
                        ins = nc.tensor.matmul(ps[:r, 6, hh * P:hh * P + P], PT_B[:kr, hh, kb, 0:r],
                                               vb[:kr, v, (2 * hp + hh) * P:(2 * hp + hh) * P + P],
                                               start=kb == 0, stop=kb == len(vt) - 1)
                ins.then_inc(at["b", "pv"], 1)
            u = step - 2
            if 0 <= u < UNITS:
                t, hp, kc, nk, tc, vt = b_unit(u)
                r = ROWS[t]
                pe.wait_ge(at["b", "probs"], u + 1)
                if u >= 1:
                    pe.wait_ge(at["b", "pt"], u)
                    pe.wait_ge(ptd["b"], u)
                for hh in range(2):
                    for kb, (v, kr) in enumerate(vt):
                        ins = nc.tensor.transpose(ps[:kr, 4 + hh, kb * P:kb * P + r],
                                                  E_B[u % 3][:r, 2 * hh, kb * P:kb * P + kr], ident[:r, :r])
                ins.then_inc(at["b", "flip"], 1)
        out_sample(1)
        moe(1)


_INS = ["x_prompt", "x_sample", "cache_a_k", "cache_a_v", "cache_b_k", "cache_b_v", "norm_mix", "norm_ffn", "norm_final",
        "w_a_qkv", "b_a_qkv", "a_sinks", "w_a_o", "w_b_qkv", "b_lambda", "b_subln", "w_b_o", "w_route_group",
        "b_route_group", "w_route_expert", "b_route_expert", "w_gate", "w_up", "w_down"]
_OUTS = [(1, SEQ, D), (1, DEC, D), (1, 1, WINDOW, A_KV, HD), (1, 1, WINDOW, A_KV, HD), (1, 1, WINDOW, A_KV, HD),
         (1, 1, WINDOW, A_KV, HD), (1, 1, SEQ, B_HEADS, BHD), (1, 1, SEQ, B_HEADS, BHD), (1, 1, DEC, B_HEADS, BHD),
         (1, 1, DEC, B_HEADS, BHD)]


def kernel(**inputs):
    import concourse.bacc as bacc
    from concourse.bass_utils import run_bass_kernel_spmd

    nc = bacc.Bacc("TRN2", target_bir_lowering=False, num_devices=1)
    arrays, I = {}, {}
    const, dist_a, dist_b = shape_constants()
    given = {name: np.ascontiguousarray(inputs[name]) for name in _INS}
    given.update(const=const, dist_a=dist_a, dist_b=dist_b)
    for name, a in given.items():
        arrays[f"in_{name}"] = a
        I[name] = nc.dram_tensor(f"in_{name}", a.shape, mybir.dt.from_np(a.dtype), kind="ExternalInput").ap()
    O = [nc.dram_tensor(f"out_{i}", list(s), F32, kind="ExternalOutput").ap() for i, s in enumerate(_OUTS)]
    build(nc, I, O)
    r = run_bass_kernel_spmd(nc, [arrays], core_ids=[0])
    return tuple(r.results[0][f"out_{i}"] for i in range(len(_OUTS)))
```

```python
from contextlib import ExitStack

import numpy as np

import concourse.bass as bass
from concourse import mybir

F32 = mybir.dt.float32
I32 = mybir.dt.int32
U32 = mybir.dt.uint32
ALU = mybir.AluOpType
ACT = mybir.ActivationFunctionType
AX = mybir.AxisListType.X

D = 1024
SEQ, DEC, PAST = 512, 32, 256
CHUNK, WINDOW = 64, 128
N = SEQ + DEC
P = 128
KD = D // P
NT = 5
ROWS = [P, P, P, P, DEC]
COL = [P * t for t in range(NT)]
HALF_N = N // 2
assert DEC == 32
O_ITEMS = 17
KV_ITEMS = 17
KV_LATE = 8
KV_BEFORE = 2 * KV_ITEMS - KV_LATE

A_HEADS, A_KV, HD = 16, 4, 64
A_GROUP = A_HEADS // A_KV
AQ, AKV = A_HEADS * HD, A_KV * HD
B_HEADS, BHD = 8, 128
SCALE = HD ** -0.5
LAM_INIT = 0.8 - 0.6 * float(np.exp(-0.3))
EPS, SUB_EPS = 1e-6, 1e-5
MASKED = 1e32
BIG = 1e30

G, EPG, F = 4, 8, 256
NE = G * EPG
CAP = 64
MAX_EXTRA = 17
MASK_READ = 5
KEY0 = 2048
OUT_HALF = D // 2

RING, SLOT = 6, 2048
A_STREAM0, A_SLOTS = 0, (AQ + 2 * AKV) // F + D // F
B_SLOTS = 3 * D // F + D // F
HELD_TURN = 1
DEEP = 4
MOE_STREAMS = RING * NE // DEEP
B_STREAM0 = A_SLOTS + MOE_STREAMS
MOE_STREAM0 = [A_SLOTS, B_STREAM0 + B_SLOTS]

C_ID, C_REV, C_K1, C_K2, C_HALF, C_THR, C_IOTA, C_END = 0, 128, 160, 165, 170, 171, 179, 211


def a_slopes():
    return [float(np.float32(2.0 ** (-8.0 * (h + 1) / A_HEADS))) for h in range(A_HEADS)]


def b_slopes():
    return [float(np.float32(2.0 ** (-8.0 * (h + 1) / B_HEADS))) for h in range(B_HEADS)]


def shape_constants():
    c = np.zeros((P, C_END), np.float32)
    c[:, C_ID:C_ID + P] = np.eye(P)
    c[:, C_REV:C_REV + NE] = NE - np.arange(NE)
    tok = np.arange(NT)[None, :] * P + np.arange(P)[:, None]
    c[:, C_K1:C_K1 + NT] = KEY0 - 2 * tok
    c[:, C_K2:C_K2 + NT] = KEY0 - 2 * tok - 1
    c[:, C_HALF] = np.arange(P) // CAP
    c[:, C_THR:C_THR + 8] = CAP * np.arange(1, 9)
    c[:, C_IOTA:C_IOTA + NE] = np.arange(NE)
    q = np.arange(P)[:, None]
    ka = np.arange(2 * P)[None, :]
    da = np.abs(q - (ka - P)).astype(np.float32)
    seen = (ka // CHUNK >= q // CHUNK) & (ka // CHUNK <= q // CHUNK + WINDOW // CHUNK)
    da = np.where(seen, da, np.float32(MASKED))
    kb = np.arange(4 * P)[None, :]
    db = np.abs(q + 3 * P - kb).astype(np.float32)
    seen = (kb - 3 * P) // CHUNK <= q // CHUNK
    db = np.where(seen, db, np.float32(MASKED))
    return c, da.astype(np.float32), db.astype(np.float32)


class Link:

    def __init__(self, sem):
        self.sem, self.n = sem, 0

    def __call__(self, eng, instruction):
        self.n += 1
        instruction.then_inc(self.sem, 1)
        eng.wait_ge(self.sem, self.n)


def build(nc, I, O):
    ctx = ExitStack()
    with ctx:
        program(nc, ctx, I, O)


def program(nc, ctx, I, O):
    def sb(name, shape, dt=F32):
        return ctx.enter_context(nc.sbuf_tensor(name, shape, dt))

    def sem(name):
        return ctx.enter_context(nc.semaphore(name))

    hn_dram = nc.dram_tensor("hn_scratch", [N, D], F32).ap()
    y2_dram = nc.dram_tensor("y2_scratch", [4 * N, OUT_HALF], F32).ap()

    ring = sb("ring", [P, RING, SLOT])
    hid = sb("hid", [P, NT, D])
    xT = sb("xT", [P, KD, N])
    oT = xT
    cst = sb("cst", [P, C_END])
    ident = cst[:, C_ID:C_ID + P]
    small = sb("small", [P, 160])
    wr_sb = sb("wr", [P, 2, KD, 36])
    br_sb = sb("br", [P, 2, 36])
    AREA = 29696
    area = sb("area", [P, AREA])

    def part(at, *shape):
        n = int(np.prod(shape))
        v = area[:, at:at + n]
        if len(shape) == 2:
            v = v.rearrange("p (a b) -> p a b", b=shape[1])
        if len(shape) == 3:
            v = v.rearrange("p (a b c) -> p a b c", b=shape[1], c=shape[2])
        return v

    qT = part(0, KD, N)
    R_K = KD * N
    kTa = part(R_K, A_KV, SEQ + WINDOW + DEC)
    kTb = part(R_K, B_HEADS, SEQ + PAST + DEC)
    R_V = R_K + B_HEADS * (SEQ + PAST + DEC)
    va = part(R_V, 6, AKV)
    vb = part(R_V, 7, D)
    R_TAB = R_V + 7 * D
    tabA = part(R_TAB, A_HEADS, 2 * P)
    tabB = part(R_TAB, B_HEADS, 4 * P)
    R_W = R_TAB + 4096
    dist_a = part(R_W, 2 * P)
    dist_b = part(R_W + 5632, 4 * P)
    kst = part(R_W + 512, 6, A_KV * 2 * HD)
    kca = part(R_W + 512 + 3072, AKV)
    kbt = part(R_W, NT, D)
    kcb = part(R_V, 2, D)
    E_A = [part(R_W + 1024 * i, 4, 2 * P) for i in range(3)]
    PT_A = [part(R_W + 3072 + 1024 * i, 4, 2, P) for i in range(2)]
    E_B = [part(R_W + 2048 * i, 4, 4 * P) for i in range(3)]
    PT_B = part(R_W + 6144, 2, 4, P)
    ON = [part(R_W + 7168 + 256 * i, 2, P) for i in range(2)]
    R_N = R_W + 1024
    norm_at = [R_N, R_V + 2 * D, R_N, R_V, R_N]
    gbc = [part(a, D) for a in norm_at]
    ynorm = [[part(a + D * (1 + i), D) for i in range(2)] for a in norm_at]
    junk = [part(a + 3 * D, D) for a in norm_at]
    assert 6 * AKV <= 2 * D
    xg = [part(1024 * i, D) for i in range(DEEP)]
    M1 = DEEP * D
    xts = [part(M1 + 512 * i, KD, CAP) for i in range(2)]
    sil = [part(M1 + 1024 + 256 * i, F) for i in range(2)]
    hmul = [part(M1 + 1536 + 256 * i, F) for i in range(2)]
    hts = [part(M1 + 2048 + 128 * i, 2, CAP) for i in range(2)]
    yout = [part(M1 + 2304 + 512 * i, OUT_HALF) for i in range(2)]
    M0 = M1 + 3328
    R_X = M0 + 3248
    extra_slots = part(R_X, RING, SLOT)
    assert R_X + RING * SLOT <= R_N
    xT_flat = xT[:, :, :].rearrange("p k n -> p (k n)")
    held = {(2, 0): xT_flat[:, 0:SLOT], (2, 1): xT_flat[:, SLOT:2 * SLOT],
            (2, 2): part(R_N + D, SLOT), (3, 0): part(R_N + 4 * D, SLOT)}
    ovw = part(R_X, 3, SLOT)
    y2b = [part(R_X + SLOT * ((3 + i) % RING), 2, D) for i in range(NT)]
    lg = part(M0 + 544, NT, 36)
    keytab = part(M0 + 736, N)
    topk = part(M0 + 1280, P)
    key = part(M0 + 1408, NT, NE)
    rt = [part(M0 + 1568 + 160 * i, NT, NE) for i in range(5)]
    rs = part(M0 + 2368, 24, 8)
    gw = part(M0 + 2560, 2, 8)
    keytmp = part(M0 + 2576, N)
    ovs = part(M0 + 3120, 128)
    idx_i = sb("idx_i", [P, 3, NE], I32)
    cur_i = sb("cur_i", [P, DEEP + 2], I32)
    ov_i = sb("ov_i", [P, 8], I32)
    ov_u = sb("ov_u", [1, 8], U32)
    ss, rstd, pbase = small[:, 0:8], small[:, 8:16], small[:, 16:24]
    neghalf = small[:, 24:28]
    bq = small[:, 28:36]
    sink8 = small[:, 36:52]
    lam4 = small[:, 54:58]
    neglam = small[:, 58:59]
    st = [small[:, 60 + 32 * i:92 + 32 * i] for i in range(3)]
    bkv = sb("bkv", [P, 2 * AKV])
    subg = bkv[:, 0:BHD]
    lamb = bkv[:, 128:384].rearrange("p (a b) -> p a b", b=HD)

    ps = ctx.enter_context(nc.psum_tensor("ps", [P, 8, 512], F32))

    w_ready = [sem(f"w_ready{i}") for i in range(RING)]
    x_ready = [sem(f"x_ready{i}") for i in range(RING)]
    held_ready = sem("held_ready")
    const_in = sem("const_in")
    passed = sem("passed")
    x_in = [sem(f"x_in{i}") for i in range(3)]
    bias_in = sem("bias_in")
    cache_a_in, cache_b_in, lam_in, dist_b_in = sem("cache_a_in"), sem("cache_b_in"), sem("lam_in"), sem("dist_b_in")
    router_in = sem("router_in")
    router_packed = sem("router_packed")
    g_in = sem("g_in")
    sumsq, rstd_ready, y_ready, y_flip, xt_act, xt_dve = (
        sem("sumsq"), sem("rstd_ready"), sem("y_ready"), sem("y_flip"), sem("xt_act"), sem("xt_dve"))
    y_out = [sem(f"y_out{i}") for i in range(2)]
    hid_attn = sem("hid_attn")
    hid_moe = [sem(f"hid_moe{l}") for l in range(2)]
    k_out, v_out = sem("k_out"), sem("v_out")
    pool_own, dve_own, act_own = sem("pool_own"), sem("dve_own"), sem("act_own")
    q_mm, q_act, q_dve = sem("q_mm"), sem("q_act"), sem("q_dve")
    kv_mm, kv_sb, k_flip, k_sb = sem("kv_mm"), sem("kv_sb"), sem("k_flip"), sem("k_sb")
    cachek_sb = sem("cachek_sb")
    tab_ready = sem("tab_ready")
    at = {}
    for layer in "ab":
        for name in ("scores", "biased", "exp", "recip", "probs", "flip", "pt", "pv", "o", "scaled",
                     "sq", "rms", "on", "onflip"):
            if layer == "b" or name not in ("scaled", "sq", "rms", "on", "onflip"):
                at[layer, name] = sem(f"{layer}_{name}")
    ptd = {c: sem(f"{c}_pt_dve") for c in "ab"}
    o_mm = sem("o_mm")
    r_mm, r_exp, r_key, r_kflip, r_top, r_idx = (
        sem("r_mm"), sem("r_exp"), sem("r_key"), sem("r_kflip"), sem("r_top"), sem("r_idx"))
    r_d = sem("r_d")
    r_tflip = sem("r_tflip")
    lam_sum = sem("lam_sum")
    ones = cst[:, C_REV + NE - 1:C_REV + NE]
    zeroed, ix_cur = sem("zeroed"), sem("ix_cur")
    ix_s = sem("ix_s")
    gath = [sem(f"gath{i}") for i in range(DEEP)]
    scat = [sem(f"scat{i}") for i in range(2)]
    x_flip, x_sb, gu_mm, silu, h_sb, h_flip, ht_sb, d_mm, ye_sb = (
        sem("x_flip"), sem("x_sb"), sem("gu_mm"), sem("silu"), sem("h_sb"), sem("h_flip"), sem("ht_sb"),
        sem("d_mm"), sem("ye_sb"))
    ov = [{k: sem(f"ov{k}{l}") for k in ("count", "own", "pick", "mask", "list", "idx", "w", "gath", "xf", "xs", "gu",
                                         "silu", "h", "hf", "ht", "d", "y", "scat", "irow")} for l in range(2)]
    y2_in = [sem(f"y2_in{i}") for i in range(NT)]

    def wait_apart(eng, s, value):
        eng.wait_ge(s, value)
        eng.sem_inc(passed, 1)

    def slot(n):
        return n % RING

    def landed(n):
        return 16 * (n // RING + 1)

    def expert_slot(layer, u, j, turn):
        if u < DEEP // 2:
            n = MOE_STREAM0[layer] + 3 * u + j
            return ring[:, slot(n), :], w_ready[slot(n)], 16 * (n // RING + 1 + turn)
        late = not isinstance(turn, int) or turn > HELD_TURN
        if (u, j) in held and not late and turn == HELD_TURN:
            return held[u, j], held_ready, 16 * len(held) * (layer + 1)
        n = 3 * (u - DEEP // 2) + j
        skipped = (u, j) in held
        return extra_slots[:, n, :], x_ready[n], 16 * ((NE // DEEP - skipped) * layer + 1 - (skipped and late) + turn)

    def slot_left(n):
        layer, i = (0, n) if n < A_SLOTS else (1, n - B_STREAM0)
        if i < 4:
            return q_mm, 8 * layer + 2 * i + 2
        if layer == 0 and i < 6:
            return kv_mm, NT * (i - 3)
        if layer and i < 12:
            return kv_mm, 2 * NT + (KV_ITEMS if i < 8 else KV_BEFORE + 2 * (i - 7))
        return o_mm, O_ITEMS * (layer + 1)

    def kv_item(i):
        if i < KV_ITEMS - 1:
            return i // 4, i % 4
        i -= KV_ITEMS
        if i == -1:
            return 0, None
        if i < 8:
            return 4 + i // 2, i % 2
        if i == 8:
            return 4, None
        return 4 + (i - 9) // 2, 2 + (i - 9) % 2

    def o_item(layer, step):
        i = step - (7, 8)[layer]
        return i if 0 <= i < O_ITEMS - 1 else None

    def a_unit(u):
        t, j = divmod(u, A_KV)
        if t == 0:
            return t, j, 0, P, P, [(0, P)]
        if t < 4:
            return t, j, (t - 1) * P, 2 * P, 0, [(t - 1, P), (t, P)]
        return t, j, SEQ, WINDOW + DEC, 0, [(4, P), (5, DEC)]

    def b_unit(u):
        t, hp = divmod(u, B_HEADS // 2)
        if t < 4:
            return t, hp, 0, P * (t + 1), (3 - t) * P, [(i, P) for i in range(t + 1)]
        return t, hp, SEQ, PAST + DEC, P, [(4, P), (5, P), (6, DEC)]

    UNITS = NT * 4
    EARLY, EARLY_STEP = 3, UNITS

    def early(step):
        return step - EARLY_STEP if 0 <= step - EARLY_STEP < EARLY else None

    def blk(kb, total):
        return min(P, total - kb * P)

    block = ctx.enter_context(nc.Block())

    @block.sync
    def _(sp):
        def load(n, src):
            sp.dma_start(ring[:, slot(n), :].rearrange("p (k f) -> p k f", f=src.shape[-1]), src) \
              .then_inc(w_ready[slot(n)], 16)

        def rows8(w, lo, hi):
            return w[:, lo:hi].rearrange("(p k) f -> p k f", k=KD)

        def rows128(w, lo, hi):
            return w[:, lo:hi].rearrange("(k p) f -> p k f", p=P)

        wa, wao = I["w_a_qkv"][0], I["w_a_o"][0]
        wb, wbo = I["w_b_qkv"][0], I["w_b_o"][0]
        a_src = [rows8(wa, F * i, F * i + F) for i in range(6)] + [rows128(wao, F * i, F * i + F) for i in range(4)]
        b_src = [rows8(wb, F * i, F * i + F) for i in range(12)] + [rows128(wbo, F * i, F * i + F) for i in range(4)]

        gate = [I["w_gate"][l].rearrange("g e (p k) f -> (g e) p k f", k=KD) for l in range(2)]
        up = [I["w_up"][l].rearrange("g e (p k) f -> (g e) p k f", k=KD) for l in range(2)]
        down = [I["w_down"][l].rearrange("g e (c p) d -> (g e) p c d", p=P) for l in range(2)]

        def expert_loads(layer, turn, u):
            e = DEEP * turn + u
            for j, w in enumerate((gate, up, down)):
                if isinstance(turn, int) and turn and (u, j) in held:
                    continue
                if not isinstance(turn, int) or turn:
                    sp.wait_ge(d_mm if j == 2 else gu_mm, NE * layer + e - DEEP + 1)
                elif u < DEEP // 2:
                    sp.wait_ge(*slot_left(MOE_STREAM0[layer] + 3 * u + j - RING))
                else:
                    sp.wait_ge(at["ab"[layer], "o"], UNITS)
                    if layer:
                        sp.wait_ge(v_out, 16 * NT)
                    for b in range(2):
                        sp.wait_ge(y_out[b], 16 * (3, 2)[b] * (layer + 1))
                    sp.wait_ge(y_flip, NT * (2 * layer + 2))
                src = w[layer][e] if isinstance(e, int) else w[layer][bass.ds(e, 1)].rearrange("o p k f -> p (o k) f")
                dst, landed_sem, _ = expert_slot(layer, u, j, 0)
                sp.dma_start(dst.rearrange("p (k f) -> p k f", f=src.shape[-1]), src).then_inc(landed_sem, 16)

        def moe_loads(layer):
            for u in range(DEEP):
                expert_loads(layer, 0, u)
            sp.wait_ge(r_mm, layer + 1)
            for g in gath:
                sp.wait_ge(g, 16 * (NE // DEEP * layer + 1))
            for (u, j), dst in held.items():
                src = (gate, up, down)[j][layer][DEEP * HELD_TURN + u]
                sp.dma_start(dst.rearrange("p (k f) -> p k f", f=src.shape[-1]), src).then_inc(held_ready, 16)
            for u in range(DEEP):
                expert_loads(layer, HELD_TURN, u)
            with sp.Fori(HELD_TURN + 1, NE // DEEP) as i:
                for u in range(DEEP):
                    expert_loads(layer, i, u)
            s = ov[layer]
            sp.wait_ge(s["count"], 1)
            extra = sp.value_load(ov_i[0:1, layer:layer + 1], min_val=0, max_val=MAX_EXTRA)

            def overfull_weights(o):
                wait_apart(sp, s["pick"], o + 1)
                e = sp.value_load(ov_u[0:1, 0:1], min_val=0, max_val=NE - 1)
                for j, w in enumerate((gate, up, down)):
                    src = w[layer][bass.ds(e, 1)].rearrange("o p k f -> p (o k) f")
                    sp.dma_start(ovw[:, j, :].rearrange("p (k f) -> p k f", f=src.shape[-1]), src) \
                      .then_inc(s["w"], 16)

            with sp.If(extra > 0):
                sp.wait_ge(d_mm, NE * (layer + 1) - 1)
                overfull_weights(0)
            with sp.If(extra > 1):
                with sp.Fori(1, extra) as o:
                    overfull_weights(o)

        for n in range(A_SLOTS):
            if n >= RING:
                sp.wait_ge(*slot_left(n - RING))
            load(n, a_src[n])
        moe_loads(0)
        for i in range(B_SLOTS):
            n = B_STREAM0 + i
            if i < RING:
                sp.wait_ge(d_mm if i % 3 == 2 else gu_mm, NE - DEEP + 1 + i // 3)
                if i == 1:
                    sp.wait_ge(y2_in[0], 16)
                    sp.wait_ge(y2_in[1], 16)
            else:
                sp.wait_ge(*slot_left(n - RING))
            load(n, b_src[i])
        moe_loads(1)

    @block.gpsimd
    def _(pool):
        own = Link(pool_own)

        def bcast(dst, src, s):
            pool.dma_start(dst, src).then_inc(s, 16)

        def norm_small(n, rows=None, tiles=range(NT)):
            for t in tiles:
                r = ROWS[t]
                pool.wait_ge(sumsq, NT * n + t + 1)
                own(pool, nc.gpsimd.tensor_scalar(pbase[:r, t:t + 1], ss[:r, t:t + 1], 1.0 / D, EPS, ALU.mult, ALU.add))
                nc.gpsimd.tensor_tensor(rstd[:r, t:t + 1], pbase[:r, t:t + 1], neghalf[:r, 0:1], ALU.pow) \
                    .then_inc(rstd_ready, 1)
                if rows and t > 0:
                    rows(t - 1)
            if rows and NT - 1 in tiles:
                rows(NT - 1)

        def rows_out(n, tiles=range(NT)):
            def rows(t):
                r = ROWS[t]
                pool.wait_ge(y_ready, NT * n + t + 1)
                if n == 4:
                    dst = O[0][0, COL[t]:COL[t] + P, :] if t < 4 else O[1][0]
                else:
                    dst = hn_dram[COL[t]:COL[t] + r, :]
                pool.dma_start(dst, ynorm[n][t % 2][:r, :]).then_inc(y_out[t % 2], 16)
            norm_small(n, rows, tiles)

        def g_load(n, w, after=None):
            if after is not None:
                pool.wait_ge(*after)
            pool.dma_start(gbc[n], w.rearrange("(o d) -> o d", o=1).broadcast_to([P, D])).then_inc(g_in, 16)

        pool.dma_start(cst[:, :], I["const"]).then_inc(const_in, 16)
        g_load(0, I["norm_mix"][0])
        own(pool, nc.gpsimd.memset(neghalf, -0.5))
        pool.dma_start(bq, I["b_a_qkv"][0, 0:AQ].rearrange("(m p) -> p m", p=P),
                       allow_slow_non_contiguous=True).then_inc(bias_in, 16)
        pool.dma_start(bkv[:, :], I["b_a_qkv"][0:1, AQ:AQ + 2 * AKV].broadcast_to([P, 2 * AKV])).then_inc(bias_in, 16)
        pool.dma_start(st[0][:, 0:16], I["a_sinks"][0:1, :].broadcast_to([P, A_HEADS])).then_inc(bias_in, 16)
        norm_small(0)
        pool.wait_ge(xt_act, NT)
        pool.wait_ge(xt_dve, NT)
        pool.wait_ge(y_flip, NT)
        pool.dma_start(dist_a, I["dist_a"]).then_inc(cache_a_in, 16)
        pool.dma_start(kca, I["cache_a_k"][0, 0].rearrange("s h d -> s (h d)")).then_inc(cache_a_in, 16)
        pool.dma_start(va[:, 4, :], I["cache_a_v"][0, 0].rearrange("s h d -> s (h d)")).then_inc(cache_a_in, 16)
        stage_g, stage_e = part(R_K + 2688, 2, KD, G), part(R_K + 2688 + 64, 2, KD, NE)
        for l in range(2):
            pool.dma_start(stage_g[:, l], I["w_route_group"][l].rearrange("(p k) g -> p k g", k=KD)).then_inc(router_in, 16)
            pool.dma_start(stage_e[:, l], I["w_route_expert"][l].rearrange("(p k) g -> p k g", k=KD)).then_inc(router_in, 16)
            pool.dma_start(br_sb[:, l, 0:G], I["b_route_group"][l:l + 1].broadcast_to([P, G])).then_inc(router_in, 16)
            pool.dma_start(br_sb[:, l, G:G + NE], I["b_route_expert"][l:l + 1].broadcast_to([P, NE])) \
                .then_inc(router_in, 16)
        pool.wait_ge(cache_a_in, 48)
        for h, slope in enumerate(a_slopes()):
            ins = nc.gpsimd.tensor_scalar(tabA[:, h, :], dist_a, -slope / SCALE, 1.0, ALU.mult, ALU.mult)
        ins.then_inc(tab_ready, 1)
        pool.wait_ge(router_in, 128)
        for l in range(2):
            nc.gpsimd.tensor_copy(wr_sb[:, l, :, 0:G], stage_g[:, l])
            ins = nc.gpsimd.tensor_copy(wr_sb[:, l, :, G:G + NE], stage_e[:, l])
        ins.then_inc(router_packed, 1)
        kview = [kst[:, i, :].rearrange("p (h c d) -> p h c d", c=2, d=HD)[:, :, 0, :] for i in range(6)]
        pool.wait_ge(kv_sb, NT)
        pool.wait_ge(cachek_sb, 1)
        pool.dma_start(O[2][0, 0], kview[3]).then_inc(k_out, 16)
        pool.dma_start(O[4][0, 0, 0:WINDOW - DEC], I["cache_a_k"][0, 0, DEC:WINDOW]).then_inc(k_out, 16)
        pool.dma_start(O[4][0, 0, WINDOW - DEC:WINDOW], kview[4][0:DEC]).then_inc(k_out, 16)
        pool.dma_start(O[5][0, 0, 0:WINDOW - DEC], I["cache_a_v"][0, 0, DEC:WINDOW]).then_inc(k_out, 16)
        pool.wait_ge(kv_sb, 2 * NT)
        pool.dma_start(O[3][0, 0].rearrange("s h d -> s (h d)"), va[:, 3, :]).then_inc(k_out, 16)
        pool.dma_start(O[5][0, 0, WINDOW - DEC:WINDOW].rearrange("s h d -> s (h d)"), va[0:DEC, 5, :]).then_inc(k_out, 16)
        g_load(1, I["norm_ffn"][0])
        for u in range(UNITS):
            t, j, kc, nk, tc, vt = a_unit(u)
            r = ROWS[t]
            pool.wait_ge(at["a", "recip"], u + 1)
            for g in range(4):
                ins = nc.gpsimd.tensor_scalar(E_A[u % 3][:r, g, 0:nk], E_A[u % 3][:r, g, 0:nk],
                                              st[u % 3][:r, 24 + g:25 + g], 1.0, ALU.mult, ALU.mult)
            ins.then_inc(at["a", "probs"], 1)

        def moe(layer):
            n = 1 + 2 * layer
            c0 = "ab"[layer]
            rows_out(n, range(layer * EARLY, NT))
            pool.wait_ge(at[c0, "o"], UNITS)
            for x in xg:
                ins = nc.gpsimd.memset(x, 0.0)
            own(pool, ins)
            for b in range(2):
                pool.wait_ge(y_out[b], 16 * (3, 2)[b] * (layer + 1))
            pool.wait_ge(r_idx, layer + 1)
            g_load(n + 1, (I["norm_mix"][1], I["norm_final"])[layer])

            def gather(e, u):
                nc.gpsimd.tensor_copy(cur_i[:, u:u + 1], idx_i[:, 1, bass.ds(e, 1)]).then_inc(ix_cur, 1)
                wait_apart(pool, ix_cur, NE * layer + e + 1)
                nc.gpsimd.indirect_dma_start(xg[u][0:CAP, :], None, hn_dram,
                                             bass.IndirectOffsetOnAxis(ap=cur_i[0:CAP, u:u + 1], axis=0),
                                             bounds_check=N - 1, oob_is_err=False).then_inc(gath[u], 16)

            def scatter(e, b, before):
                if before is not None:
                    pool.wait_ge(scat[b], before)
                c = DEEP + b
                nc.gpsimd.tensor_copy(cur_i[:, c:c + 1], idx_i[:, 0, bass.ds(e, 1)]).then_inc(ix_s, 1)
                pool.wait_ge(ye_sb, NE * layer + e + 1)
                wait_apart(pool, ix_s, NE * layer + e + 1)
                nc.gpsimd.indirect_dma_start(y2_dram, bass.IndirectOffsetOnAxis(ap=cur_i[:, c:c + 1], axis=0),
                                             yout[b], None, bounds_check=4 * N - 1, oob_is_err=False) \
                    .then_inc(scat[b], 16)

            half = NE // 2 * layer

            def step(turn, u, last=False):
                e = DEEP * turn + u
                if not last:
                    pool.wait_ge(x_flip, NE * layer + e + 1)
                    gather(e + DEEP, u)
                before = half + DEEP // 2 * turn + u // 2
                first = isinstance(turn, int) and turn == 0 and u < 2
                scatter(e, u % 2, None if first else 16 * before)

            for u in range(DEEP):
                gather(u, u)
            for u in range(DEEP):
                step(0, u)
            with pool.Fori(1, NE // DEEP - 1) as i:
                for u in range(DEEP):
                    step(i, u)
            s = ov[layer]

            def overfull_gather(o):
                wait_apart(pool, s["idx"], o + 1)
                nc.gpsimd.indirect_dma_start(xg[0][0:CAP, :], None, hn_dram,
                                             bass.IndirectOffsetOnAxis(ap=ov_i[0:CAP, 4:5], axis=0),
                                             bounds_check=N - 1, oob_is_err=False).then_inc(s["gath"], 16)

            def overfull_scatter(o):
                wait_apart(pool, s["y"], o + 1)
                nc.gpsimd.indirect_dma_start(y2_dram, bass.IndirectOffsetOnAxis(ap=ov_i[:, 5:6], axis=0),
                                             yout[0], None, bounds_check=4 * N - 1, oob_is_err=False) \
                    .then_inc(s["scat"], 16)

            step(NE // DEEP - 1, 0, last=True)
            pool.wait_ge(s["count"], 1)
            extra = pool.value_load(ov_i[0:1, layer:layer + 1], min_val=0, max_val=MAX_EXTRA)
            with pool.If(extra > 0):
                pool.wait_ge(x_flip, NE * (layer + 1) - DEEP + 1)
                overfull_gather(0)
            for u in range(1, DEEP):
                step(NE // DEEP - 1, u, last=True)
            for b in range(2):
                pool.wait_ge(scat[b], NE // 2 * (layer + 1) * 16)
            with pool.If(extra > 0):
                overfull_scatter(0)
            with pool.If(extra > 1):
                with pool.Fori(1, extra) as o:
                    overfull_gather(o)
                    overfull_scatter(o)

        moe(0)
        norm_small(2)
        pool.dma_start(subg, I["b_subln"][0:1, :].broadcast_to([P, BHD])).then_inc(lam_in, 16)
        pool.dma_start(lamb, I["b_lambda"][0:1].rearrange("o a b -> o (a b)").broadcast_to([P, 4 * HD])
                       .rearrange("p (a b) -> p a b", b=HD)).then_inc(lam_in, 16)
        for i in range(2):
            pool.dma_start(kcb[:, i, :], I["cache_b_k"][0, 0, P * i:P * i + P].rearrange("s h d -> s (h d)")) \
                .then_inc(cache_b_in, 16)
            pool.dma_start(vb[:, 4 + i, :], I["cache_b_v"][0, 0, P * i:P * i + P].rearrange("s h d -> s (h d)")) \
                .then_inc(cache_b_in, 16)
        pool.dma_start(dist_b, I["dist_b"]).then_inc(dist_b_in, 16)
        pool.wait_ge(dist_b_in, 16)
        for h, slope in enumerate(b_slopes()):
            ins = nc.gpsimd.tensor_scalar(tabB[:, h, :], dist_b, -slope / SCALE, 1.0, ALU.mult, ALU.mult)
        ins.then_inc(tab_ready, 1)
        pool.wait_ge(kv_sb, 2 * NT + KV_ITEMS)
        for t in range(NT):
            dst = O[6][0, 0, COL[t]:COL[t] + P] if t < 4 else O[8][0, 0]
            pool.dma_start(dst.rearrange("s h d -> s (h d)"), kbt[:ROWS[t], t, :]).then_inc(k_out, 16)

        def v_rows_out():
            pool.wait_ge(kv_sb, 2 * NT + 2 * KV_ITEMS)
            for t in range(NT):
                dst = O[7][0, 0, COL[t]:COL[t] + P] if t < 4 else O[9][0, 0]
                pool.dma_start(dst.rearrange("s h d -> s (h d)"), vb[:ROWS[t], t if t < 4 else 6, :]).then_inc(v_out, 16)

        def rms(u):
            t = b_unit(u)[0]
            r = ROWS[t]
            pool.wait_ge(at["b", "sq"], u + 1)
            sm = st[u % 3]
            own(pool, nc.gpsimd.tensor_scalar(sm[:r, 22:24], sm[:r, 20:22], 1.0 / BHD, SUB_EPS, ALU.mult, ALU.add))
            nc.gpsimd.tensor_tensor(sm[:r, 24:26], sm[:r, 22:24], neghalf[:r, 0:2], ALU.pow).then_inc(at["b", "rms"], 1)

        for s in range(UNITS + 4):
            if s < UNITS:
                t, hp, kc, nk, tc, vt = b_unit(s)
                r = ROWS[t]
                pool.wait_ge(at["b", "recip"], s + 1)
                for hh in range(2):
                    ins = nc.gpsimd.tensor_scalar(E_B[s % 3][:r, 2 * hh + 1, 0:nk], E_B[s % 3][:r, 2 * hh + 1, 0:nk],
                                                  st[s % 3][:r, 16 + hh:17 + hh], 1.0, ALU.mult, ALU.mult)
                ins.then_inc(at["b", "scaled"], 1)
            if s == KV_LATE + 1:
                v_rows_out()
            if early(s + 1) is not None:
                rows_out(3, [early(s + 1)])
            if 0 <= s - 2 < UNITS:
                rms(s - 2)
            if s - 2 == UNITS - 5:
                g_load(3, I["norm_ffn"][1], (v_out, 16 * NT))
        moe(1)
        rows_out(4)
        pool.wait_ge(y_out[0], 16 * 9)
        pool.wait_ge(y_out[1], 16 * 6)
        pool.wait_ge(v_out, 16 * NT)
        pool.wait_ge(k_out, 16 * (6 + NT))

    @block.scalar
    def _(act):
        own = Link(act_own)

        def norm(n, tiles=range(NT)):
            for t in tiles:
                r = ROWS[t]
                if n == 0:
                    act.wait_ge(x_in[t // 2], 16)
                elif n % 2:
                    act.wait_ge(hid_attn, 4 * NT * (n // 2) + 4 * t + 4)
                else:
                    act.wait_ge(hid_moe[n // 2 - 1], t + 1)
                if n == 3 and t == 0:
                    act.wait_ge(v_out, 16 * NT)
                if n or t:
                    act.wait_ge(sumsq, NT * n + t)
                nc.scalar.activation(junk[n][:r, :], hid[:r, t, :], ACT.Square, accum_out=ss[:r, t:t + 1]) \
                    .then_inc(sumsq, 1)
                if n < 4:
                    if t > 0:
                        xt_copy(n, t - 1)
            if n < 4 and NT - 1 in tiles:
                xt_copy(n, NT - 1)

        def xt_copy(n, t):
            r = ROWS[t]
            b = 2 * (t % 2)
            act.wait_ge(y_flip, NT * n + t + 1)
            nc.scalar.activation(xT[:, 0:4, COL[t]:COL[t] + r],
                                 ps[:, b, :].rearrange("p (k c) -> p k c", c=P)[:, :, 0:r], ACT.Copy).then_inc(xt_act, 1)

        act.dma_start(hid[:, 0:2, :], I["x_prompt"][0, 0:2 * P].rearrange("(t p) d -> p t d", p=P)).then_inc(x_in[0], 16)
        act.dma_start(hid[:, 2:4, :], I["x_prompt"][0, 2 * P:4 * P].rearrange("(t p) d -> p t d", p=P)).then_inc(x_in[1], 16)
        act.dma_start(hid[0:DEC, 4, :], I["x_sample"][0]).then_inc(x_in[2], 16)
        norm(0)
        act.wait_ge(bias_in, 48)
        for m in range(8):
            act.wait_ge(q_mm, m + 1)
            nc.scalar.activation(qT[:, m, 0:HALF_N], ps[:, 2 * (m % 2), 0:HALF_N], ACT.Identity,
                                 bias=bq[:, m:m + 1]).then_inc(q_act, 1)
        for i in range(6):
            act.wait_ge(k_flip, i + 1)
            r = (P, P, P, P, DEC, P)[i]
            c = (0, P, 2 * P, 3 * P, SEQ + WINDOW, SEQ)[i]
            nc.scalar.activation(kTa[:, :, c:c + r], ps[:, 6 + i % 2, :].rearrange("p (h c) -> p h c", c=P)[:, :, 0:r],
                                 ACT.Copy).then_inc(k_sb, 1)

        def attention(layer, unit, E, step):
            nh = 4
            if step < UNITS:
                u = step
                t, j, kc, nk, tc, vt = unit(u)
                r = ROWS[t]
                sm = st[u % 3]
                act.wait_ge(at[layer, "biased"], u + 1)
                for g in range(nh):
                    ins = nc.scalar.activation(E[u % 3][:r, g, 0:nk], E[u % 3][:r, g, 0:nk], ACT.Exp,
                                               bias=sm[:r, 4 + g:5 + g], scale=SCALE, accum_out=sm[:r, 8 + g:9 + g])
                if layer == "a":
                    ins = nc.scalar.activation(sm[:r, 16:20], sm[:r, 12:16], ACT.Exp, scale=SCALE)
                ins.then_inc(at[layer, "exp"], 1)

        for step in range(UNITS + 3):
            attention("a", a_unit, E_A, step)
            u = step - 2
            if 0 <= u < UNITS:
                t, j, kc, nk, tc, vt = a_unit(u)
                r = ROWS[t]
                act.wait_ge(at["a", "flip"], u + 1)
                if u >= 2:
                    act.wait_ge(at["a", "pv"], u - 1)
                nc.scalar.activation(PT_A[u % 2][:, :, 0, 0:r],
                                     ps[:, 4, :].rearrange("p (g c) -> p g c", c=P)[:, :, 0:r],
                                     ACT.Copy).then_inc(at["a", "pt"], 1)
            if early(step) is not None:
                norm(1, [early(step)])

        def moe(layer):
            norm(1 + 2 * layer, range(EARLY, NT))
            act.wait_ge(r_exp, 2 * layer + 1)
            nc.scalar.activation(rt[0][:, :, 0:G], rt[0][:, :, 0:G], ACT.Exp).then_inc(r_d, 1)
            act.wait_ge(r_exp, 2 * layer + 2)
            nc.scalar.activation(rs[:, 5, 0:NT], rs[:, 4, 0:NT], ACT.Exp).then_inc(r_d, 1)

            def x_copy(e, b):
                act.wait_ge(x_flip, NE * layer + e + 1)
                if not isinstance(e, int) or e >= 2 or layer:
                    act.wait_ge(gu_mm, NE * layer + e - 1)
                nc.scalar.activation(xts[b].rearrange("p k c -> p (k c)"), ps[:, 2 + b, :], ACT.Copy).then_inc(x_sb, 1)

            def silu_step(e, b):
                act.wait_ge(gu_mm, NE * layer + e + 1)
                if not isinstance(e, int) or e >= 2 or layer:
                    act.wait_ge(h_sb, NE * layer + e - 1)
                nc.scalar.activation(sil[b][CAP:P, :], ps[0:CAP, b, 0:F], ACT.Silu).then_inc(silu, 1)

            x_copy(0, 0)
            for e in range(2):
                silu_step(e, e)
                x_copy(e + 1, 1 - e)
            with act.Fori(1, NE // 2 - 1) as i:
                for u in range(2):
                    silu_step(2 * i + u, u)
                    x_copy(2 * i + u + 1, 1 - u)
            silu_step(NE - 2, 0)
            x_copy(NE - 1, 1)
            silu_step(NE - 1, 1)
            s = ov[layer]
            act.wait_ge(s["count"], 1)
            extra = act.value_load(ov_i[0:1, layer:layer + 1], min_val=0, max_val=MAX_EXTRA)
            with act.If(extra > 0):
                with act.Fori(0, extra) as o:
                    act.wait_ge(s["xf"], o + 1)
                    nc.scalar.activation(xts[0].rearrange("p k c -> p (k c)"), ps[:, 2, :], ACT.Copy).then_inc(s["xs"], 1)
                    act.wait_ge(s["gu"], o + 1)
                    nc.scalar.activation(sil[0][CAP:P, :], ps[0:CAP, 0, 0:F], ACT.Silu).then_inc(s["silu"], 1)
                wait_apart(act, s["scat"], 16 * extra)
            for b in range(2):
                act.wait_ge(scat[b], NE // 2 * (layer + 1) * 16)
            for t in range(NT):
                r = ROWS[t]
                act.dma_start(y2b[t][:r, :, :],
                              y2_dram[4 * COL[t]:4 * COL[t] + 4 * r, :].rearrange("(p c) d -> p (c d)", c=4)
                              .rearrange("p (a b) -> p a b", b=D)).then_inc(y2_in[t], 16)

        moe(0)
        norm(2)
        act.wait_ge(lam_in, 32)
        act.wait_ge(lam_sum, 1)
        nc.scalar.activation(lam4[:, 2:4], lam4[:, 0:2], ACT.Exp).then_inc(r_d, 1)
        for m in range(8):
            act.wait_ge(q_mm, 8 + m + 1)
            nc.scalar.activation(qT[:, m, 0:HALF_N], ps[:, 2 * (m % 2), 0:HALF_N], ACT.Copy).then_inc(q_act, 1)
        for i in range(4):
            tile, quad = divmod(i, 2)
            act.wait_ge(k_flip, 6 + i + 1)
            nc.scalar.activation(kTb[:, 4 * quad:4 * quad + 4, SEQ + P * tile:SEQ + P * tile + P],
                                 ps[:, 6 + i % 2, :].rearrange("p (h c) -> p h c", c=P), ACT.Copy).then_inc(k_sb, 1)
        for i in range(KV_ITEMS):
            sl, t = kv_item(i)
            act.wait_ge(k_flip, 10 + i + 1)
            if t is None:
                dst, r, h = kTb[:, :, SEQ + PAST:SEQ + PAST + DEC], DEC, B_HEADS
            else:
                dst, r, h = kTb[:, 2 * sl:2 * sl + 2, COL[t]:COL[t] + P], P, 2
            nc.scalar.activation(dst, ps[:, 6 + i % 2, 0:h * r].rearrange("p (h c) -> p h c", c=r),
                                 ACT.Copy).then_inc(k_sb, 1)
        for step in range(UNITS + 4):
            u = step - 4
            if 0 <= u < UNITS:
                t, hp = b_unit(u)[:2]
                r = ROWS[t]
                act.wait_ge(at["b", "onflip"], u + 1)
                nc.scalar.activation(oT[:, 2 * hp:2 * hp + 2, COL[t]:COL[t] + r],
                                     ps[:, 6, 2 * P:4 * P].rearrange("p (h c) -> p h c", c=P)[:, :, 0:r],
                                     ACT.Copy).then_inc(at["b", "o"], 1)
            if early(step) is not None:
                norm(3, [early(step)])
            attention("b", b_unit, E_B, step)
            u = step - 2
            if 0 <= u < UNITS:
                t, hp, kc, nk, tc, vt = b_unit(u)
                r = ROWS[t]
                act.wait_ge(at["b", "flip"], u + 1)
                if u >= 1:
                    act.wait_ge(at["b", "pv"], u)
                for kb, (_, kr) in enumerate(vt):
                    if kb == 0 or kr < P:
                        nb = sum(1 for _, x in vt if x == P) if kb == 0 else 1
                        ins = nc.scalar.activation(
                            PT_B[0:kr, 0, kb:kb + nb, 0:r],
                            ps[0:kr, 4, :].rearrange("p (k c) -> p k c", c=P)[:, kb:kb + nb, 0:r], ACT.Copy)
                ins.then_inc(at["b", "pt"], 1)
            u = step - 3
            if 0 <= u < UNITS:
                r = ROWS[b_unit(u)[0]]
                act.wait_ge(at["b", "pv"], u + 1)
                if u >= 2:
                    act.wait_ge(at["b", "onflip"], u - 1)
                for hh in range(2):
                    ins = nc.scalar.activation(ON[u % 2][:r, hh, :], ps[:r, 6, hh * P:hh * P + P], ACT.Square,
                                               accum_out=st[u % 3][:r, 20 + hh:21 + hh])
                ins.then_inc(at["b", "sq"], 1)
        moe(1)
        norm(4)

    @block.vector
    def _(dve):
        own = Link(dve_own)

        def norm(n, tiles=range(NT)):
            def rows(t):
                r = ROWS[t]
                dve.wait_ge(rstd_ready, NT * n + t + 1)
                if t == 0:
                    dve.wait_ge(g_in, 16 * (n + 1))
                if t >= 2 and n < 4:
                    dve.wait_ge(y_flip, NT * n + t - 1)
                if t >= 2 and n in (1, 3):
                    before = 3 * (n // 2), 2 * (n // 2)
                    dve.wait_ge(y_out[t % 2], 16 * (before[t % 2] + t // 2))
                if t >= 2 and n == 4:
                    dve.wait_ge(y_out[t % 2], 16 * ((6, 4)[t % 2] + t // 2))
                if n == 3 and t == 0:
                    dve.wait_ge(v_out, 16 * NT)
                nc.vector.scalar_tensor_tensor(ynorm[n][t % 2][:r, :], hid[:r, t, :], rstd[:r, t:t + 1], gbc[n][:r, :],
                                               ALU.mult, ALU.mult).then_inc(y_ready, 1)

            def xt_copy(t):
                r = ROWS[t]
                b = 2 * (t % 2) + 1
                dve.wait_ge(y_flip, NT * n + t + 1)
                nc.vector.tensor_copy(xT[:, 4:8, COL[t]:COL[t] + r],
                                      ps[:, b, :].rearrange("p (k c) -> p k c", c=P)[:, :, 0:r]).then_inc(xt_dve, 1)

            experts = n in (2, 4)
            if experts:
                combine(n // 2 - 1, 0)
            for t in tiles:
                if experts and t + 1 < NT:
                    combine(n // 2 - 1, t + 1)
                rows(t)
                if t > 0 and n < 4:
                    xt_copy(t - 1)
            if n < 4 and NT - 1 in tiles:
                xt_copy(NT - 1)

        norm(0)
        dve.wait_ge(bias_in, 48)
        own(dve, nc.vector.tensor_scalar(sink8, st[0][:, 0:16], 1.0 / SCALE, None, ALU.mult))
        for m in range(8):
            dve.wait_ge(q_mm, m + 1)
            nc.vector.tensor_scalar(qT[:, m, HALF_N:N], ps[:, 2 * (m % 2) + 1, 0:HALF_N], bq[:, m:m + 1], None,
                                    ALU.add).then_inc(q_dve, 1)
        dve.wait_ge(cache_a_in, 48)

        def twice(x):
            return x.rearrange("p (h d) -> p h d", d=HD).unsqueeze(2).broadcast_to([x.shape[0], A_KV, 2, HD])

        def dup(i, r):
            return kst[:r, i, :].rearrange("p (h c d) -> p h c d", c=2, d=HD)

        nc.vector.tensor_copy(dup(5, P), twice(kca)).then_inc(cachek_sb, 1)
        for t in range(NT):
            r = ROWS[t]
            dve.wait_ge(kv_mm, t + 1)
            for c in range(2):
                ins = nc.vector.tensor_tensor(dup(t, r)[:, :, c, :],
                                              ps[:r, 4 + t % 2, 0:AKV].rearrange("p (h d) -> p h d", d=HD),
                                              bkv[:r, 0:AKV].rearrange("p (h d) -> p h d", d=HD), ALU.add)
            ins.then_inc(kv_sb, 1)
        for t in range(NT):
            r = ROWS[t]
            i = NT + t
            dve.wait_ge(kv_mm, i + 1)
            nc.vector.tensor_tensor(va[:r, t if t < 4 else 5, :], ps[:r, 4 + i % 2, 0:AKV], bkv[:r, AKV:2 * AKV],
                                    ALU.add).then_inc(kv_sb, 1)

        def bias_max(layer, unit, E, u, bank, tab, head):
            t, j, kc, nk, tc, vt = unit(u)
            r = ROWS[t]
            sm = st[u % 3]
            dve.wait_ge(at[layer, "scores"], u + 1)
            if u >= 3:
                dve.wait_ge(at[layer, "flip"], u - 2)
            for g in range(4):
                b, c = bank(u, g)
                ins = nc.vector.tensor_tensor_reduce(
                    out=E[u % 3][:r, g, 0:nk], in0=ps[:r, b, c:c + nk], in1=tab[:r, head(j, g), tc:tc + nk],
                    scale=1.0, scalar=-3e38, op0=ALU.add, op1=ALU.max, accum_out=sm[:r, g:g + 1])
            own(dve, ins)
            if layer == "a":
                own(dve, nc.vector.tensor_tensor(sm[:r, 0:4], sm[:r, 0:4], sink8[:r, 4 * j:4 * j + 4], ALU.max))
                nc.vector.tensor_tensor(sm[:r, 12:16], sink8[:r, 4 * j:4 * j + 4], sm[:r, 0:4], ALU.subtract)
            nc.vector.tensor_scalar(sm[:r, 4:8], sm[:r, 0:4], -SCALE, None, ALU.mult).then_inc(at[layer, "biased"], 1)

        def residual(layer, i):
            if i is not None:
                dve.wait_ge(o_mm, O_ITEMS * layer + i + 1)
                h = hid[:, i // 4, F * (i % 4):F * (i % 4) + F]
                nc.vector.tensor_tensor(h, h, ps[:, 7, 0:F], ALU.add).then_inc(hid_attn, 1)

        def residual_sample(layer):
            dve.wait_ge(o_mm, O_ITEMS * (layer + 1))
            for s in range(4):
                h = hid[0:DEC, 4, F * s:F * s + F]
                nc.vector.tensor_tensor(h, h, ps[DEC * s:DEC * s + DEC, 6, 0:F], ALU.add).then_inc(hid_attn, 1)

        def bank_a(u, g):
            return 2 * (u % 2) + g % 2, (g // 2) * 2 * P

        dve.wait_ge(tab_ready, 1)
        dve.wait_ge(k_out, 16 * 6)
        dve.wait_ge(k_flip, 6)
        dve.wait_ge(router_packed, 1)
        for step in range(UNITS + 3):
            residual(0, o_item(0, step - 1))
            if step < UNITS:
                bias_max("a", a_unit, E_A, step, bank_a, tabA, lambda j, g: 4 * j + g)
            u = step - 1
            if 0 <= u < UNITS:
                r = ROWS[a_unit(u)[0]]
                sm = st[u % 3]
                dve.wait_ge(at["a", "exp"], u + 1)
                own(dve, nc.vector.tensor_tensor(sm[:r, 20:24], sm[:r, 8:12], sm[:r, 16:20], ALU.add))
                nc.vector.reciprocal(sm[:r, 24:28], sm[:r, 20:24]).then_inc(at["a", "recip"], 1)
            u = step - 2
            if 0 <= u < UNITS:
                t, j, kc, nk, tc, vt = a_unit(u)
                if len(vt) > 1:
                    r, kr = ROWS[t], vt[1][1]
                    dve.wait_ge(at["a", "flip"], u + 1)
                    if u >= 2:
                        dve.wait_ge(at["a", "pv"], u - 1)
                    nc.vector.tensor_copy(
                        PT_A[u % 2][:kr, :, 1, 0:r],
                        ps[:kr, 5, :].rearrange("p (g c) -> p g c", c=P)[:, :, 0:r]) \
                        .then_inc(ptd["a"], 1)
            u = step - 3
            if 0 <= u < UNITS:
                t, j = a_unit(u)[:2]
                r = ROWS[t]
                dve.wait_ge(at["a", "pv"], u + 1)
                nc.vector.tensor_copy(oT[:, 2 * j:2 * j + 2, COL[t]:COL[t] + r],
                                      ps[:, 6, 0:2 * P].rearrange("p (m c) -> p m c", c=P)[:, :, 0:r]) \
                    .then_inc(at["a", "o"], 1)
            if early(step) is not None:
                norm(1, [early(step)])
        residual(0, o_item(0, UNITS + 2))
        residual_sample(0)

        def moe(layer):
            norm(1 + 2 * layer, range(EARLY, NT))
            s = ov[layer]
            own(dve, nc.vector.memset(lg, 0.0))
            dve.wait_ge(r_mm, layer + 1)
            dve.wait_ge(router_in, 128)
            pr = ps[:, 4, 0:NT * 36].rearrange("p (t c) -> p t c", c=36)
            bias = br_sb[:, layer, :].unsqueeze(1)
            nc.vector.tensor_tensor(lg[:, 0:4, :], pr[:, 0:4, :], bias.broadcast_to([P, 4, 36]), ALU.add)
            own(dve, nc.vector.tensor_tensor(lg[0:DEC, 4, :], pr[0:DEC, 4, :], br_sb[0:DEC, layer, :], ALU.add))

            def per_tile(i):
                return rs[:, i, 0:NT]

            def over(x, w):
                return x.unsqueeze(2).broadcast_to([P, NT, w])

            gl, el = lg[:, :, 0:G], lg[:, :, G:G + NE]
            own(dve, nc.vector.tensor_reduce(per_tile(0), gl, AX, ALU.max))
            nc.vector.tensor_tensor(rt[0][:, :, 0:G], gl, over(per_tile(0), G), ALU.subtract).then_inc(r_exp, 1)
            ghot = rt[1][:, :, 0:G]
            own(dve, nc.vector.tensor_tensor(rt[2][:, :, 0:G], gl, over(per_tile(0), G), ALU.is_equal))
            own(dve, nc.vector.tensor_tensor(rt[2][:, :, 0:G], rt[2][:, :, 0:G],
                                             cst[:, C_REV:C_REV + G].unsqueeze(1).broadcast_to([P, NT, G]), ALU.mult))
            own(dve, nc.vector.tensor_reduce(per_tile(1), rt[2][:, :, 0:G], AX, ALU.max))
            own(dve, nc.vector.tensor_tensor(ghot, rt[2][:, :, 0:G], over(per_tile(1), G), ALU.is_equal))
            own(dve, nc.vector.tensor_scalar(ghot, ghot, BIG, -BIG, ALU.mult, ALU.add))
            em = rt[3]
            own(dve, nc.vector.tensor_tensor(
                em.rearrange("p t (g e) -> p t g e", e=EPG), el.rearrange("p t (g e) -> p t g e", e=EPG),
                ghot.unsqueeze(3).broadcast_to([P, NT, G, EPG]), ALU.add))

            def top(dst, best, free):
                own(dve, nc.vector.tensor_reduce(per_tile(best), em, AX, ALU.max))
                own(dve, nc.vector.tensor_tensor(rt[4], em, over(per_tile(best), NE), ALU.is_equal))
                own(dve, nc.vector.tensor_tensor(
                    rt[4], rt[4], cst[:, C_REV:C_REV + NE].unsqueeze(1).broadcast_to([P, NT, NE]), ALU.mult))
                own(dve, nc.vector.tensor_reduce(per_tile(free), rt[4], AX, ALU.max))
                own(dve, nc.vector.tensor_tensor(dst, rt[4], over(per_tile(free), NE), ALU.is_equal))

            h1, h2 = rt[1], rt[2]
            top(h1, 2, 6)
            own(dve, nc.vector.scalar_tensor_tensor(em, h1, -2 * BIG, em, ALU.mult, ALU.add))
            top(h2, 3, 7)
            nc.vector.tensor_tensor(per_tile(4), per_tile(3), per_tile(2), ALU.subtract).then_inc(r_exp, 1)
            own(dve, nc.vector.tensor_tensor(h1, h1, over(cst[:, C_K1:C_K1 + NT], NE), ALU.mult))
            own(dve, nc.vector.tensor_tensor(h2, h2, over(cst[:, C_K2:C_K2 + NT], NE), ALU.mult))
            own(dve, nc.vector.tensor_tensor(key, h1, h2, ALU.add))
            nc.vector.tensor_scalar(rt[4], key, 0.0, None, ALU.is_gt).then_inc(r_key, 1)
            dve.wait_ge(r_kflip, layer + 1)
            nc.vector.tensor_copy(keytab[0:NE, 0:SEQ], ps[0:NE, 5, :])
            own(dve, nc.vector.tensor_copy(keytab[0:NE, SEQ:N], ps[0:NE, 4, 0:DEC]))
            cnt = ovs[0:1, 0:NE]
            own(dve, nc.vector.tensor_scalar(cnt, ps[0:1, 7, 0:NE], float(-CAP), None, ALU.add))
            own(dve, nc.vector.tensor_tensor(
                keytmp[0:1, 0:NE * 8].rearrange("p (e j) -> p e j", j=8),
                cnt.unsqueeze(2).broadcast_to([1, NE, 8]),
                cst[0:1, C_THR:C_THR + 8].unsqueeze(1).broadcast_to([1, NE, 8]), ALU.subtract))
            own(dve, nc.vector.tensor_scalar(keytmp[0:1, 0:NE * 8], keytmp[0:1, 0:NE * 8], float(-CAP), None, ALU.is_gt))
            own(dve, nc.vector.tensor_reduce(ovs[0:1, 32:33], keytmp[0:1, 0:NE * 8], AX, ALU.add))
            nc.vector.tensor_copy(ov_i[0:1, layer:layer + 1], ovs[0:1, 32:33]).then_inc(s["count"], 1)

            def top64(table):
                return [lambda r=r: nc.vector.max(topk[0:NE, 8 * r:8 * r + 8], table[0:NE, :]) for r in range(CAP // 8)], \
                       [lambda r=r: nc.vector.match_replace(table[0:NE, :], topk[0:NE, 8 * r:8 * r + 8],
                                                            table[0:NE, :], -1.0) for r in range(CAP // 8)]

            take, strike = top64(keytab)
            for r in range(CAP // 8):
                own(dve, take[r]())
                own(dve, strike[r]())
            nc.vector.tensor_copy(topk[0:NE, CAP:P], topk[0:NE, 0:CAP]).then_inc(r_top, 1)
            dve.wait_ge(r_tflip, layer + 1)
            own(dve, nc.vector.tensor_scalar(idx_i[:, 2, :], ps[:, 6, 0:NE], -1.0, float(KEY0), ALU.mult, ALU.add))
            own(dve, nc.vector.tensor_scalar(rt[3].rearrange("p t e -> p (t e)")[:, 0:NE], ps[:, 6, 0:NE],
                                             -2.0, float(2 * KEY0), ALU.mult, ALU.add))
            own(dve, nc.vector.tensor_scalar(idx_i[:, 0, :], rt[3].rearrange("p t e -> p (t e)")[:, 0:NE],
                                             cst[:, C_HALF:C_HALF + 1], None, ALU.add))
            nc.vector.tensor_scalar(idx_i[:, 1, :], idx_i[:, 2, :], 1, None, ALU.arith_shift_right).then_inc(r_idx, 1)
            dve.wait_ge(r_d, 2 * layer + 2 + layer)
            own(dve, nc.vector.tensor_reduce(per_tile(8), rt[0][:, :, 0:G], AX, ALU.add))
            own(dve, nc.vector.reciprocal(per_tile(9), per_tile(8)))
            own(dve, nc.vector.tensor_scalar(per_tile(10), per_tile(5), 1.0, None, ALU.add))
            own(dve, nc.vector.reciprocal(per_tile(11), per_tile(10)))
            own(dve, nc.vector.tensor_tensor(gw[:, 0, 0:NT], per_tile(9), per_tile(11), ALU.mult))
            own(dve, nc.vector.tensor_tensor(gw[:, 1, 0:NT], gw[:, 0, 0:NT], per_tile(5), ALU.mult))

            def mult(e, b):
                dve.wait_ge(silu, NE * layer + e + 1)
                if not isinstance(e, int) or e >= 2 or layer:
                    dve.wait_ge(h_flip, NE * layer + e - 1)
                nc.vector.tensor_tensor(hmul[b][CAP:P, :], sil[b][CAP:P, :], ps[CAP:P, b, 0:F], ALU.mult) \
                    .then_inc(h_sb, 1)

            def ht_copy(e, b):
                dve.wait_ge(h_flip, NE * layer + e + 1)
                if not isinstance(e, int) or e >= 2 or layer:
                    dve.wait_ge(d_mm, NE * layer + e - 1)
                nc.vector.tensor_copy(hts[b].rearrange("p c q -> p (c q)"), ps[:, 4 + b, 0:2 * CAP]).then_inc(ht_sb, 1)

            def y_copy(e, b, count=None):
                dve.wait_ge(d_mm, NE * layer + e + 1)
                if count is not None:
                    dve.wait_ge(scat[b], count)
                nc.vector.tensor_copy(yout[b], ps[:, 6 + b, :]).then_inc(ye_sb, 1)

            half = NE // 2 * layer
            for e in range(2):
                mult(e, e)
                ht_copy(e, e)
                if e:
                    y_copy(0, 0, 16 * half if layer else None)

            def two(i, before):
                mult(2 * i, 0)
                ht_copy(2 * i, 0)
                y_copy(2 * i - 1, 1, before)
                mult(2 * i + 1, 1)
                ht_copy(2 * i + 1, 1)
                y_copy(2 * i, 0, 16 * (half + i))

            STEPS = 28
            k = [0]

            def link(o, ins):
                k[0] += 1
                ins.then_inc(s["own"], 1)
                wait_apart(dve, s["own"], o * STEPS + k[0])

            def overfull_list(o):
                k[0] = 0
                best, hot = ovs[0:1, 40:48], ovs[0:1, 64:96]
                link(o, nc.vector.max(best, cnt))
                link(o, nc.vector.max_index(ov_u[:, :], best, cnt))
                link(o, nc.vector.tensor_copy(ovs[0:1, 48:49], ov_u[0:1, 0:1]))
                link(o, nc.vector.tensor_scalar(hot, cst[0:1, C_IOTA:C_IOTA + NE], ovs[0:1, 48:49], None, ALU.is_equal))
                nc.vector.scalar_tensor_tensor(cnt, hot, float(-CAP), cnt, ALU.mult, ALU.add).then_inc(s["pick"], 1)
                mcol, mnot = ovs[0:NE, 96:97], ovs[0:NE, 97:98]
                dve.wait_ge(s["mask"], o + 1)
                link(o, nc.vector.tensor_copy(mcol, ps[0:NE, 3, 0:1]))
                assert k[0] == MASK_READ, k
                link(o, nc.vector.tensor_scalar(mnot, mcol, -1.0, 1.0, ALU.mult, ALU.add))
                link(o, nc.vector.tensor_scalar(keytmp[0:NE, :], keytab[0:NE, :], mcol, None, ALU.mult))
                take, strike = top64(keytmp)
                for r in range(CAP // 8):
                    link(o, take[r]())
                    link(o, strike[r]())
                link(o, nc.vector.tensor_scalar(keytmp[0:NE, :], keytmp[0:NE, :], mcol, None, ALU.mult))
                link(o, nc.vector.scalar_tensor_tensor(keytab[0:NE, :], keytab[0:NE, :], mnot, keytmp[0:NE, :],
                                                       ALU.mult, ALU.add))
                nc.vector.tensor_copy(topk[0:NE, CAP:P], topk[0:NE, 0:CAP]).then_inc(s["list"], 1)

            def overfull_rows(o):
                dve.wait_ge(s["irow"], o + 1)
                link(o, nc.vector.tensor_scalar(ov_i[:, 6:7], ps[:, 3, 8:9], -1.0, float(KEY0), ALU.mult, ALU.add))
                link(o, nc.vector.tensor_scalar(ovs[:, 98:99], ps[:, 3, 8:9], -2.0, float(2 * KEY0), ALU.mult, ALU.add))
                link(o, nc.vector.tensor_scalar(ov_i[:, 5:6], ovs[:, 98:99], cst[:, C_HALF:C_HALF + 1], None, ALU.add))
                nc.vector.tensor_scalar(ov_i[:, 4:5], ov_i[:, 6:7], 1, None, ALU.arith_shift_right) \
                    .then_inc(s["idx"], 1)
                assert k[0] == STEPS, k

            def overfull_expert(o):
                dve.wait_ge(s["silu"], o + 1)
                nc.vector.tensor_tensor(hmul[0][CAP:P, :], sil[0][CAP:P, :], ps[CAP:P, 0, 0:F], ALU.mult) \
                    .then_inc(s["h"], 1)
                dve.wait_ge(s["hf"], o + 1)
                nc.vector.tensor_copy(hts[0].rearrange("p c q -> p (c q)"), ps[:, 4, 0:2 * CAP]).then_inc(s["ht"], 1)
                dve.wait_ge(s["d"], o + 1)
                nc.vector.tensor_copy(yout[0], ps[:, 6, :]).then_inc(s["y"], 1)
                wait_apart(dve, s["scat"], 16 * (o + 1))

            two(1, 16 * half if layer else None)
            two(2, 16 * (half + 1))
            dve.wait_ge(s["count"], 1)
            extra = dve.value_load(ov_i[0:1, layer:layer + 1], min_val=0, max_val=MAX_EXTRA)
            with dve.If(extra > 0):
                overfull_list(0)
            two(3, 16 * (half + 2))
            with dve.If(extra > 0):
                overfull_rows(0)
            with dve.Fori(4, NE // 2) as i:
                two(i, 16 * (half + i - 1))
            y_copy(NE - 1, 1, 16 * (half + NE // 2 - 1))
            with dve.If(extra > 0):
                dve.wait_ge(scat[0], 16 * NE // 2 * (layer + 1))
                overfull_expert(0)
            with dve.If(extra > 1):
                with dve.Fori(1, extra) as o:
                    overfull_list(o)
                    overfull_rows(o)
                    overfull_expert(o)

        def combine(layer, t):
            r = ROWS[t]
            dve.wait_ge(y2_in[t], 16 * (layer + 1))
            h = hid[:r, t, :]
            own(dve, nc.vector.scalar_tensor_tensor(h, y2b[t][:r, 0, :], gw[:r, 0, t:t + 1], h, ALU.mult, ALU.add))
            nc.vector.scalar_tensor_tensor(h, y2b[t][:r, 1, :], gw[:r, 1, t:t + 1], h, ALU.mult, ALU.add) \
                .then_inc(hid_moe[layer], 1)

        moe(0)
        norm(2)
        dve.wait_ge(lam_in, 32)
        own(dve, nc.vector.tensor_tensor(lamb[:, 0, :], lamb[:, 0, :], lamb[:, 1, :], ALU.mult))
        own(dve, nc.vector.tensor_tensor(lamb[:, 2, :], lamb[:, 2, :], lamb[:, 3, :], ALU.mult))
        own(dve, nc.vector.tensor_scalar(subg, subg, 1.0 - LAM_INIT, None, ALU.mult))
        nc.vector.tensor_reduce(lam4[:, 0:2], lamb.rearrange("p (a b) d -> p a b d", b=2)[:, :, 0, :], AX, ALU.add) \
            .then_inc(lam_sum, 1)
        for m in range(8):
            dve.wait_ge(q_mm, 8 + m + 1)
            nc.vector.tensor_copy(qT[:, m, HALF_N:N], ps[:, 2 * (m % 2) + 1, 0:HALF_N]).then_inc(q_dve, 1)
        dve.wait_ge(r_d, 3)
        own(dve, nc.vector.tensor_tensor(neglam, lam4[:, 3:4], lam4[:, 2:3], ALU.subtract))
        own(dve, nc.vector.tensor_scalar(neglam, neglam, -LAM_INIT, None, ALU.add))

        def kv_copy(i, bank):
            sl, t = kv_item(i)
            dve.wait_ge(kv_mm, 2 * NT + i + 1)
            if i == 0:
                dve.wait_ge(tab_ready, 2)
            if i == KV_ITEMS:
                dve.wait_ge(k_flip, 10)
            if t is None:
                for j in range(4):
                    c = F * j
                    dst = kbt[0:DEC, 4, c:c + F] if sl < 4 else vb[0:DEC, 6, c:c + F]
                    ins = nc.vector.tensor_copy(dst, ps[DEC * j:DEC * j + DEC, bank, 0:F])
            else:
                c = F * (sl % 4)
                dst = kbt[:, t, c:c + F] if sl < 4 else vb[:, t, c:c + F]
                ins = nc.vector.tensor_copy(dst, ps[:, bank, 0:F])
            ins.then_inc(kv_sb, 1)

        for i in range(KV_BEFORE):
            kv_copy(i, 4 + i % 2)
        dve.wait_ge(k_out, 16 * (6 + NT))
        dve.wait_ge(k_flip, 10 + KV_ITEMS)
        for step in range(UNITS + 4):
            if 1 <= step <= KV_LATE:
                kv_copy(KV_BEFORE + step - 1, 7)
            residual(1, o_item(1, step - 1))
            if step < UNITS:
                bias_max("b", b_unit, E_B, step, lambda u, g: (g, 0), tabB, lambda j, g: 2 * j + g // 2)
            u = step - 1
            if 0 <= u < UNITS:
                r = ROWS[b_unit(u)[0]]
                sm = st[u % 3]
                dve.wait_ge(at["b", "exp"], u + 1)
                own(dve, nc.vector.reciprocal(sm[:r, 12:16], sm[:r, 8:12]))
                nc.vector.tensor_scalar(sm[:r, 16:18], sm[:r, 12:16].rearrange("p (h c) -> p h c", c=2)[:, :, 1],
                                        neglam[:r, :], None, ALU.mult).then_inc(at["b", "recip"], 1)
            u = step - 2
            if 0 <= u < UNITS:
                t, hp, kc, nk, tc, vt = b_unit(u)
                r = ROWS[t]
                Eu = E_B[u % 3]
                dve.wait_ge(at["b", "scaled"], u + 1)
                for hh in range(2):
                    ins = nc.vector.scalar_tensor_tensor(Eu[:r, 2 * hh, 0:nk], Eu[:r, 2 * hh, 0:nk],
                                                         st[u % 3][:r, 12 + 2 * hh:13 + 2 * hh],
                                                         Eu[:r, 2 * hh + 1, 0:nk], ALU.mult, ALU.add)
                ins.then_inc(at["b", "probs"], 1)
            u = step - 2
            if 0 <= u < UNITS:
                t, hp, kc, nk, tc, vt = b_unit(u)
                r = ROWS[t]
                dve.wait_ge(at["b", "flip"], u + 1)
                if u >= 1:
                    dve.wait_ge(at["b", "pv"], u)
                for kb, (_, kr) in enumerate(vt):
                    if kb == 0 or kr < P:
                        nb = sum(1 for _, x in vt if x == P) if kb == 0 else 1
                        ins = nc.vector.tensor_copy(
                            PT_B[0:kr, 1, kb:kb + nb, 0:r],
                            ps[0:kr, 5, :].rearrange("p (k c) -> p k c", c=P)[:, kb:kb + nb, 0:r])
                ins.then_inc(ptd["b"], 1)
            u = step - 3
            if 0 <= u < UNITS:
                r = ROWS[b_unit(u)[0]]
                dve.wait_ge(at["b", "rms"], u + 1)
                for hh in range(2):
                    ins = nc.vector.scalar_tensor_tensor(ON[u % 2][:r, hh, :], ps[:r, 6, hh * P:hh * P + P],
                                                         st[u % 3][:r, 24 + hh:25 + hh], subg[:r, :], ALU.mult, ALU.mult)
                ins.then_inc(at["b", "on"], 1)
            if early(step) is not None:
                norm(3, [early(step)])
        residual(1, o_item(1, UNITS + 3))
        residual_sample(1)
        moe(1)
        norm(4)

    @block.tensor
    def _(pe):
        def norm(n, logits=None, tiles=range(NT)):
            for t in tiles:
                r = ROWS[t]
                b = 2 * (t % 2)
                pe.wait_ge(y_ready, NT * n + t + 1)
                if t == 0 and n == 0:
                    pe.wait_ge(const_in, 16)
                if t >= 2:
                    pe.wait_ge(xt_act, NT * n + t - 1)
                    pe.wait_ge(xt_dve, NT * n + t - 1)
                y = ynorm[n][t % 2][:r, :].rearrange("p (c k) -> p k c", k=KD)
                for k in range(KD):
                    ins = nc.tensor.transpose(ps[:, b + k // 4, (k % 4) * P:(k % 4) * P + r], y[:, k, :], ident[:r, :r])
                ins.then_inc(y_flip, 1)
                if logits and t >= 1:
                    pe.wait_ge(xt_act, NT * n + t)
                    pe.wait_ge(xt_dve, NT * n + t)
                    logits(t - 1)
            if NT - 1 not in tiles:
                return
            pe.wait_ge(xt_act, NT * n + NT)
            pe.wait_ge(xt_dve, NT * n + NT)
            if logits:
                logits(NT - 1)

        def ring_k(n):
            return ring[:, slot(n), :].rearrange("p (k f) -> p k f", f=F)

        def arrived(n):
            pe.wait_ge(w_ready[slot(n)], landed(n))

        def q_proj(layer, n0):
            for m in range(8):
                n = n0 + m // 2
                if m % 2 == 0:
                    arrived(n)
                if m >= 2 or layer:
                    pe.wait_ge(q_act, 8 * layer + m - 1)
                    pe.wait_ge(q_dve, 8 * layer + m - 1)
                w = ring_k(n)[:, :, (m % 2) * P:(m % 2) * P + P]
                for h in range(2):
                    for k in range(KD):
                        ins = nc.tensor.matmul(ps[:, 2 * (m % 2) + h, 0:HALF_N], w[:, k, :],
                                               xT[:, k, HALF_N * h:HALF_N * h + HALF_N], start=k == 0, stop=k == KD - 1)
                        if h and k == KD - 1:
                            ins.then_inc(q_mm, 1)

        def rows_mm(bank, t, n):
            r = ROWS[t]
            for k in range(KD):
                ins = nc.tensor.matmul(ps[:r, bank, 0:F], xT[:, k, COL[t]:COL[t] + r], ring_k(n)[:, k, :],
                                       start=k == 0, stop=k == KD - 1)
            return ins

        def sample_mm(bank, src, n0):
            for k in range(KD):
                for s in range(4):
                    ins = nc.tensor.matmul(ps[DEC * s:DEC * s + DEC, bank, 0:F], src[:, k, SEQ:N], ring_k(n0 + s)[:, k, :],
                                           start=k == 0, stop=k == KD - 1)
            return ins

        def out_item(layer, i):
            if i is None:
                return
            n0 = (A_SLOTS, B_STREAM0 + B_SLOTS)[layer] - 4
            t, s = divmod(i, 4)
            if s == 0:
                pe.wait_ge(at["ab"[layer], "o"], 4 * t + 4)
            if t == 0:
                arrived(n0 + s)
            if i >= 1:
                pe.wait_ge(hid_attn, 4 * NT * layer + i)
            rows_mm(7, t, n0 + s).then_inc(o_mm, 1)

        def out_sample(layer):
            pe.wait_ge(at["ab"[layer], "o"], UNITS)
            sample_mm(6, oT, (A_SLOTS, B_STREAM0 + B_SLOTS)[layer] - 4).then_inc(o_mm, 1)

        def logits(layer, t):
            r = ROWS[t]
            if t == 0:
                pe.wait_ge(router_packed, 1)
                pe.wait_ge(at["ab"[layer], "pt"], UNITS)
            for k in range(KD):
                ins = nc.tensor.matmul(ps[:r, 4, 36 * t:36 * t + 36], xT[:, k, COL[t]:COL[t] + r], wr_sb[:, layer, k, :],
                                       start=k == 0, stop=k == KD - 1)
            if t == NT - 1:
                ins.then_inc(r_mm, 1)

        def moe_norm(layer, tiles):
            norm(1 + 2 * layer, lambda t: logits(layer, t), tiles)

        norm(0)
        q_proj(0, 0)
        pe.wait_ge(cachek_sb, 1)

        def flip_a(i, order):
            r = (P, P, P, P, DEC, P)[i]
            if order >= 2:
                pe.wait_ge(k_sb, order - 1)
            for j in range(A_KV):
                ins = nc.tensor.transpose(ps[:, 6 + order % 2, j * P:j * P + r], kst[:r, i, j * P:j * P + P], ident[:r, :r])
            ins.then_inc(k_flip, 1)

        arrived(4)
        for t in range(NT + 1):
            if t < NT:
                if t >= 2:
                    pe.wait_ge(kv_sb, t - 1)
                rows_mm(4 + t % 2, t, 4).then_inc(kv_mm, 1)
            if t > 0:
                pe.wait_ge(kv_sb, t)
                flip_a(t - 1, t - 1)
        flip_a(5, 5)
        arrived(5)
        for t in range(NT):
            pe.wait_ge(kv_sb, NT + t - 1)
            rows_mm(4 + (NT + t) % 2, t, 5).then_inc(kv_mm, 1)
        pe.wait_ge(q_act, 8)
        pe.wait_ge(q_dve, 8)
        pe.wait_ge(k_sb, 6)
        pe.wait_ge(kv_sb, 2 * NT)
        pe.wait_ge(cache_a_in, 48)
        for step in range(UNITS + 3):
            if step < UNITS:
                u = step
                t, j, kc, nk, tc, vt = a_unit(u)
                r = ROWS[t]
                if u >= 2:
                    pe.wait_ge(at["a", "biased"], u - 1)
                for g in range(4):
                    lo = HD * (g % 2)
                    ins = nc.tensor.matmul(ps[:r, 2 * (u % 2) + g % 2, (g // 2) * 2 * P:(g // 2) * 2 * P + nk],
                                           qT[lo:lo + HD, 2 * j + g // 2, COL[t]:COL[t] + r],
                                           kTa[lo:lo + HD, j, kc:kc + nk], start=True, stop=True)
                ins.then_inc(at["a", "scores"], 1)
            u = step - 3
            if 0 <= u < UNITS:
                t, j, kc, nk, tc, vt = a_unit(u)
                r = ROWS[t]
                pe.wait_ge(at["a", "pt"], u + 1)
                if u >= 4:
                    pe.wait_ge(ptd["a"], u - 3)
                if u >= 1:
                    pe.wait_ge(at["a", "o"], u)
                for gp in range(2):
                    for kb, (v, kr) in enumerate(vt):
                        for gh in range(2):
                            ins = nc.tensor.matmul(ps[HD * gh:HD * gh + HD, 6, gp * P:gp * P + r],
                                                   va[:kr, v, j * HD:j * HD + HD],
                                                   PT_A[u % 2][:kr, 2 * gp + gh, kb, 0:r],
                                                   start=kb == 0, stop=kb == len(vt) - 1)
                ins.then_inc(at["a", "pv"], 1)
            u = step - 2
            if 0 <= u < UNITS:
                t, j, kc, nk, tc, vt = a_unit(u)
                r = ROWS[t]
                pe.wait_ge(at["a", "probs"], u + 1)
                if u >= 1:
                    pe.wait_ge(at["a", "pt"], u)
                if u >= 5:
                    pe.wait_ge(ptd["a"], u - 4)
                for g in range(4):
                    for kb, (v, kr) in enumerate(vt):
                        ins = nc.tensor.transpose(ps[:kr, 4 + kb, g * P:g * P + r], E_A[u % 3][:r, g, kb * P:kb * P + kr],
                                                  ident[:r, :r])
                ins.then_inc(at["a", "flip"], 1)
            out_item(0, o_item(0, step))
            if early(step - 1) is not None and early(step - 1) < EARLY - 1:
                moe_norm(0, [early(step - 1)])
        out_sample(0)

        def moe(layer):
            moe_norm(layer, range(EARLY - 1, NT))
            s = ov[layer]
            pe.wait_ge(r_key, layer + 1)
            for t in range(NT):
                r = ROWS[t]
                b, c = (5, COL[t]) if t < 4 else (4, 0)
                nc.tensor.transpose(ps[0:NE, b, c:c + r], key[:r, t, :], ident[:r, :r])
            for t in range(NT):
                r = ROWS[t]
                ins = nc.tensor.matmul(ps[0:1, 7, 0:NE], ones[:r, 0:1], rt[4][:r, t, :], start=t == 0, stop=t == NT - 1)
            ins.then_inc(r_kflip, 1)
            pe.wait_ge(r_top, layer + 1)
            nc.tensor.transpose(ps[:, 6, 0:NE], topk[0:NE, :], ident[0:NE, 0:NE]).then_inc(r_tflip, 1)

            def x_transpose(turn, u):
                e, b = DEEP * turn + u, u % 2
                pe.wait_ge(gath[u], 16 * (NE // DEEP * layer + 1 + turn))
                if not isinstance(e, int) or e >= 2 or layer:
                    wait_apart(pe, x_sb, NE * layer + e - 1)
                x = xg[u][0:CAP, :].rearrange("p (c k) -> p k c", k=KD)
                for k in range(KD):
                    ins = nc.tensor.transpose(ps[:, 2 + b, k * CAP:k * CAP + CAP], x[:, k, :], ident[0:CAP, 0:CAP])
                ins.then_inc(x_flip, 1)

            def gate_up(turn, u):
                e, b = DEEP * turn + u, u % 2
                pe.wait_ge(x_sb, NE * layer + e + 1)
                w = []
                for j in range(2):
                    where, landed_sem, value = expert_slot(layer, u, j, turn)
                    pe.wait_ge(landed_sem, value)
                    w.append(where.rearrange("p (k f) -> p k f", f=F))
                if not isinstance(e, int) or e >= 2 or layer:
                    pe.wait_ge(h_sb, NE * layer + e - 1)
                expert_gu(xts[b], w[0], w[1], b).then_inc(gu_mm, 1)

            def expert_gu(x, wg, wu, bank):
                for k in range(KD):
                    nc.tensor.matmul(ps[0:CAP, bank, 0:F], x[:, k, :], wg[:, k, :], start=k == 0, stop=k == KD - 1)
                    ins = nc.tensor.matmul(ps[CAP:P, bank, 0:F], x[:, k, :], wu[:, k, :], start=k == 0, stop=k == KD - 1)
                return ins

            def expert_ht(h, bank):
                for c in range(2):
                    ins = nc.tensor.transpose(ps[:, bank, c * CAP:c * CAP + CAP], h[CAP:P, c * P:c * P + P],
                                              ident[CAP:P, CAP:P])
                return ins

            def expert_down(ht, wd, bank):
                for c in range(2):
                    nc.tensor.matmul(ps[0:CAP, bank, :], ht[:, c, :], wd[:, c, 0:OUT_HALF], start=c == 0, stop=c == 1)
                    ins = nc.tensor.matmul(ps[CAP:P, bank, :], ht[:, c, :], wd[:, c, OUT_HALF:D], start=c == 0, stop=c == 1)
                return ins

            def h_transpose(turn, u):
                e, b = DEEP * turn + u, u % 2
                pe.wait_ge(h_sb, NE * layer + e + 1)
                if not isinstance(e, int) or e >= 2 or layer:
                    wait_apart(pe, ht_sb, NE * layer + e - 1)
                expert_ht(hmul[b], 4 + b).then_inc(h_flip, 1)

            def down(turn, u):
                e, b = DEEP * turn + u, u % 2
                pe.wait_ge(ht_sb, NE * layer + e + 1)
                where, landed_sem, value = expert_slot(layer, u, 2, turn)
                pe.wait_ge(landed_sem, value)
                if not isinstance(e, int) or e >= 2 or layer:
                    pe.wait_ge(ye_sb, NE * layer + e - 1)
                expert_down(hts[b], where.rearrange("p (c d) -> p c d", d=D), 6 + b).then_inc(d_mm, 1)

            def step(turn, u, last=False):
                gate_up(turn, u)
                if not last:
                    x_transpose(*((turn, u + 1) if u < DEEP - 1 else (turn + 1, 0)))
                if not (isinstance(turn, int) and turn == 0 and u == 0):
                    down(*((turn, u - 1) if u else (turn - 1, DEEP - 1)))
                h_transpose(turn, u)

            pe.wait_ge(r_idx, layer + 1)
            x_transpose(0, 0)
            for u in range(DEEP):
                step(0, u)
            def overfull_mask(o):
                wait_apart(pe, s["pick"], o + 1)
                nc.tensor.matmul(ps[0:NE, 3, 0:1], ovs[0:1, 64:96], ident[0:1, 0:1], start=True, stop=True) \
                    .then_inc(s["mask"], 1)

            def overfull_list(o):
                pe.wait_ge(s["list"], o + 1)
                nc.tensor.matmul(ps[:, 3, 8:9], topk[0:NE, :], ovs[0:NE, 96:97], start=True, stop=True) \
                    .then_inc(s["irow"], 1)

            def overfull_expert(o):
                wait_apart(pe, s["gath"], 16 * (o + 1))
                x = xg[0][0:CAP, :].rearrange("p (c k) -> p k c", k=KD)
                for k in range(KD):
                    ins = nc.tensor.transpose(ps[:, 2, k * CAP:k * CAP + CAP], x[:, k, :], ident[0:CAP, 0:CAP])
                ins.then_inc(s["xf"], 1)
                pe.wait_ge(s["xs"], o + 1)
                pe.wait_ge(s["w"], 48 * (o + 1))
                wv = ovw[:, :, :].rearrange("p j (k f) -> p j k f", f=F)
                expert_gu(xts[0], wv[:, 0], wv[:, 1], 0).then_inc(s["gu"], 1)
                wait_apart(pe, s["h"], o + 1)
                expert_ht(hmul[0], 4).then_inc(s["hf"], 1)
                pe.wait_ge(s["ht"], o + 1)
                expert_down(hts[0], ovw[:, 2, :].rearrange("p (c d) -> p c d", d=D), 6).then_inc(s["d"], 1)

            step(1, 0)
            step(1, 1)
            pe.wait_ge(s["count"], 1)
            extra = pe.value_load(ov_i[0:1, layer:layer + 1], min_val=0, max_val=MAX_EXTRA)
            with pe.If(extra > 0):
                pe.wait_ge(x_sb, NE * layer + 6)
                overfull_mask(0)
                pe.wait_ge(s["own"], MASK_READ)
            step(1, 2)
            step(1, 3)
            with pe.If(extra > 0):
                pe.wait_ge(x_sb, NE * layer + 8)
                overfull_list(0)
                pe.wait_ge(s["idx"], 1)
            with pe.Fori(HELD_TURN + 1, NE // DEEP - 1) as i:
                for u in range(DEEP):
                    step(i, u)
            for u in range(DEEP):
                step(NE // DEEP - 1, u, last=u == DEEP - 1)
            down(NE // DEEP - 1, DEEP - 1)
            pe.wait_ge(ye_sb, NE * (layer + 1))
            with pe.If(extra > 0):
                overfull_expert(0)
            with pe.If(extra > 1):
                with pe.Fori(1, extra) as o:
                    overfull_mask(o)
                    overfull_list(o)
                    overfull_expert(o)

        moe(0)
        norm(2)
        q_proj(1, B_STREAM0)
        pe.wait_ge(cache_b_in, 64)
        for i in range(4):
            tile, quad = divmod(i, 2)
            if i >= 2:
                pe.wait_ge(k_sb, 6 + i - 1)
            for h in range(4):
                c = (4 * quad + h) * P
                ins = nc.tensor.transpose(ps[:, 6 + i % 2, h * P:h * P + P], kcb[:, tile, c:c + P], ident)
            ins.then_inc(k_flip, 1)
        for i in range(KV_BEFORE + 1):
            if i < KV_BEFORE:
                sl, t = kv_item(i)
                if t == 0:
                    arrived(B_STREAM0 + 4 + sl)
                if i >= 2:
                    pe.wait_ge(kv_sb, 2 * NT + i - 1)
                if t is None:
                    sample_mm(4 + i % 2, xT, B_STREAM0 + 4 + sl).then_inc(kv_mm, 1)
                else:
                    rows_mm(4 + i % 2, t, B_STREAM0 + 4 + sl).then_inc(kv_mm, 1)
            b = i - 1
            if 0 <= b < KV_ITEMS:
                sl, t = kv_item(b)
                pe.wait_ge(kv_sb, 2 * NT + b + 1)
                pe.wait_ge(k_sb, 10 + b - 1)
                r, tile, h0, nh = (DEC, 4, 0, B_HEADS) if t is None else (P, t, 2 * sl, 2)
                for h in range(nh):
                    ins = nc.tensor.transpose(ps[:, 6 + b % 2, h * r:h * r + r], kbt[:r, tile, (h0 + h) * P:(h0 + h) * P + P],
                                              ident[:r, :r])
                ins.then_inc(k_flip, 1)
        pe.wait_ge(q_act, 16)
        pe.wait_ge(q_dve, 16)
        pe.wait_ge(k_sb, 10 + KV_ITEMS)
        pe.wait_ge(kv_sb, 2 * NT + KV_BEFORE)
        for step in range(UNITS + 4):
            if step < UNITS:
                u = step
                t, hp, kc, nk, tc, vt = b_unit(u)
                r = ROWS[t]
                if u >= 1:
                    pe.wait_ge(at["b", "biased"], u)
                for g in range(4):
                    lo = HD * (g % 2)
                    ins = nc.tensor.matmul(ps[:r, g, 0:nk], qT[lo:lo + HD, 2 * hp + g // 2, COL[t]:COL[t] + r],
                                           kTb[lo:lo + HD, 2 * hp + g // 2, kc:kc + nk], start=True, stop=True)
                ins.then_inc(at["b", "scores"], 1)
            u = step - 4
            if 0 <= u < UNITS:
                t, hp = b_unit(u)[:2]
                r = ROWS[t]
                pe.wait_ge(at["b", "on"], u + 1)
                for hh in range(2):
                    ins = nc.tensor.transpose(ps[:, 6, (2 + hh) * P:(2 + hh) * P + r], ON[u % 2][:r, hh, :],
                                              ident[:r, :r])
                ins.then_inc(at["b", "onflip"], 1)
            if step < KV_LATE:
                i = KV_BEFORE + step
                sl, t = kv_item(i)
                if step:
                    pe.wait_ge(kv_sb, 2 * NT + i)
                rows_mm(7, t, B_STREAM0 + 4 + sl).then_inc(kv_mm, 1)
            if step == KV_LATE:
                pe.wait_ge(kv_sb, 2 * NT + 2 * KV_ITEMS)
            out_item(1, o_item(1, step))
            if early(step - 1) is not None and early(step - 1) < EARLY - 1:
                moe_norm(1, [early(step - 1)])
            u = step - 3
            if 0 <= u < UNITS:
                t, hp, kc, nk, tc, vt = b_unit(u)
                r = ROWS[t]
                pe.wait_ge(at["b", "pt"], u + 1)
                pe.wait_ge(ptd["b"], u + 1)
                if u >= 1:
                    pe.wait_ge(at["b", "on"], u)
                    pe.wait_ge(at["b", "sq"], u)
                    pe.wait_ge(at["b", "o"], u)
                for hh in range(2):
                    for kb, (v, kr) in enumerate(vt):
                        ins = nc.tensor.matmul(ps[:r, 6, hh * P:hh * P + P], PT_B[:kr, hh, kb, 0:r],
                                               vb[:kr, v, (2 * hp + hh) * P:(2 * hp + hh) * P + P],
                                               start=kb == 0, stop=kb == len(vt) - 1)
                ins.then_inc(at["b", "pv"], 1)
            u = step - 2
            if 0 <= u < UNITS:
                t, hp, kc, nk, tc, vt = b_unit(u)
                r = ROWS[t]
                pe.wait_ge(at["b", "probs"], u + 1)
                if u >= 1:
                    pe.wait_ge(at["b", "pt"], u)
                    pe.wait_ge(ptd["b"], u)
                for hh in range(2):
                    for kb, (v, kr) in enumerate(vt):
                        ins = nc.tensor.transpose(ps[:kr, 4 + hh, kb * P:kb * P + r],
                                                  E_B[u % 3][:r, 2 * hh, kb * P:kb * P + kr], ident[:r, :r])
                ins.then_inc(at["b", "flip"], 1)
        out_sample(1)
        moe(1)


_INS = ["x_prompt", "x_sample", "cache_a_k", "cache_a_v", "cache_b_k", "cache_b_v", "norm_mix", "norm_ffn", "norm_final",
        "w_a_qkv", "b_a_qkv", "a_sinks", "w_a_o", "w_b_qkv", "b_lambda", "b_subln", "w_b_o", "w_route_group",
        "b_route_group", "w_route_expert", "b_route_expert", "w_gate", "w_up", "w_down"]
_OUTS = [(1, SEQ, D), (1, DEC, D), (1, 1, WINDOW, A_KV, HD), (1, 1, WINDOW, A_KV, HD), (1, 1, WINDOW, A_KV, HD),
         (1, 1, WINDOW, A_KV, HD), (1, 1, SEQ, B_HEADS, BHD), (1, 1, SEQ, B_HEADS, BHD), (1, 1, DEC, B_HEADS, BHD),
         (1, 1, DEC, B_HEADS, BHD)]


def kernel(**inputs):
    import concourse.bacc as bacc
    from concourse.bass_utils import run_bass_kernel_spmd

    nc = bacc.Bacc("TRN2", target_bir_lowering=False, num_devices=1)
    arrays, I = {}, {}
    const, dist_a, dist_b = shape_constants()
    given = {name: np.ascontiguousarray(inputs[name]) for name in _INS}
    given.update(const=const, dist_a=dist_a, dist_b=dist_b)
    for name, a in given.items():
        arrays[f"in_{name}"] = a
        I[name] = nc.dram_tensor(f"in_{name}", a.shape, mybir.dt.from_np(a.dtype), kind="ExternalInput").ap()
    O = [nc.dram_tensor(f"out_{i}", list(s), F32, kind="ExternalOutput").ap() for i, s in enumerate(_OUTS)]
    build(nc, I, O)
    r = run_bass_kernel_spmd(nc, [arrays], core_ids=[0])
    return tuple(r.results[0][f"out_{i}"] for i in range(len(_OUTS)))
```
